# Optimizing a Trainium2 kernel written in Bass

```python
import jax, jax.numpy as jnp
from jax import lax
import numpy as np

D_MODEL = 1024
BATCH = 1
SEQ = 1024
DEPTH = 1

CHUNK = 64
QBLK = 128
N_MEM = 256
HEAD_DIM = 64
FOX_HEADS = 8
FOX_W = FOX_HEADS * HEAD_DIM
SWA_HEADS = 8
SWA_KV_HEADS = 2
SWA_Q_W = SWA_HEADS * HEAD_DIM
SWA_KV_W = SWA_KV_HEADS * HEAD_DIM
WINDOW = 128
WINDOW_CHUNKS = WINDOW // CHUNK
MEM_HEADS = 4
MEM_HEAD_DIM = 128
MEM_W = MEM_HEADS * MEM_HEAD_DIM
N_BRANCH = 3
ROPE_THETA = 10000.0
D_FF = ((8 * D_MODEL + 3 * 256 - 1) // (3 * 256)) * 256
EPS = 1e-6
IN_SPLITS = (FOX_W, FOX_W, FOX_W, FOX_HEADS, SWA_Q_W, SWA_KV_W, SWA_KV_W, MEM_W, N_BRANCH * D_MODEL)
D_IN = sum(IN_SPLITS)

kernel_name = 'hybrid_fox_swa_memxattn_gated_block'

def rmsnorm(x, g):
    xf = x.astype(jnp.float32)
    r = lax.rsqrt(jnp.mean(xf * xf, axis=-1, keepdims=True) + EPS)
    return (xf * r).astype(x.dtype) * g

def rope(x, pos):
    half = x.shape[-1] // 2
    inv = ROPE_THETA ** (-jnp.arange(half, dtype=jnp.float32) / half)
    ang = pos.astype(jnp.float32)[:, None] * inv[None, :]
    cos = jnp.cos(ang)[None, :, None, :]
    sin = jnp.sin(ang)[None, :, None, :]
    xf = x.astype(jnp.float32)
    x1, x2 = xf[..., :half], xf[..., half:]
    return jnp.concatenate([x1 * cos - x2 * sin, x2 * cos + x1 * sin], axis=-1).astype(x.dtype)

def fox_attention(q, k, v, logf):
    b, s, h, d = q.shape
    n = s // QBLK
    scale = d ** -0.5
    cum = jnp.cumsum(logf, axis=1)
    cum_k = cum.transpose(0, 2, 1)
    qb = q.reshape(b, n, QBLK, h, d).transpose(1, 0, 2, 3, 4)
    cq = cum.reshape(b, n, QBLK, h).transpose(1, 0, 3, 2)
    kpos = jnp.arange(s)

    def one_block(args):
        qi, cqi, i = args
        sc = jnp.einsum('bqhd,bkhd->bhqk', qi, k).astype(jnp.float32) * scale
        bias = cqi[..., :, None] - cum_k[:, :, None, :]
        qpos = i * QBLK + jnp.arange(QBLK)
        mask = kpos[None, :] <= qpos[:, None]
        sc = jnp.where(mask[None, None], sc + bias, -jnp.inf)
        p = jax.nn.softmax(sc, axis=-1)
        return jnp.einsum('bhqk,bkhd->bqhd', p.astype(v.dtype), v)

    out = lax.map(one_block, (qb, cq, jnp.arange(n)))
    return out.transpose(1, 0, 2, 3, 4).reshape(b, s, h * d)

def swa_sink_attention(q, k, v, sinks):
    b, s, h, d = q.shape
    hk = k.shape[2]
    g = h // hk
    n = s // QBLK
    scale = d ** -0.5
    qb = q.reshape(b, n, QBLK, hk, g, d)
    pad = ((0, 0), (QBLK, 0), (0, 0), (0, 0))
    kp = jnp.pad(k, pad).reshape(b, n + 1, QBLK, hk, d)
    vp = jnp.pad(v, pad).reshape(b, n + 1, QBLK, hk, d)
    kb = jnp.concatenate([kp[:, :-1], kp[:, 1:]], axis=2)
    vb = jnp.concatenate([vp[:, :-1], vp[:, 1:]], axis=2)
    qpos = jnp.arange(n)[:, None] * QBLK + jnp.arange(QBLK)[None, :]
    kpos = jnp.arange(n)[:, None] * QBLK - QBLK + jnp.arange(2 * QBLK)[None, :]
    cq = (qpos // CHUNK)[:, :, None]
    ck = (kpos // CHUNK)[:, None, :]
    valid = (kpos[:, None, :] >= 0) & (ck <= cq) & (ck > cq - WINDOW_CHUNKS)
    sc = jnp.einsum('bnqhgd,bnjhd->bnhgqj', qb, kb).astype(jnp.float32) * scale
    sc = jnp.where(valid[None, :, None, None], sc, -jnp.inf)
    sink = sinks.astype(jnp.float32).reshape(hk, g)[None, None, :, :, None, None]
    m = jnp.maximum(jnp.max(sc, axis=-1, keepdims=True), sink)
    p = jnp.exp(sc - m)
    denom = jnp.sum(p, axis=-1, keepdims=True) + jnp.exp(sink - m)
    o = jnp.einsum('bnhgqj,bnjhd->bnqhgd', (p / denom).astype(v.dtype), vb)
    return o.reshape(b, s, h * d)

def memory_cross_attention(q, mem_n, w_mem_kv):
    b, m, _ = mem_n.shape
    kv = (mem_n @ w_mem_kv).reshape(b, m, 2, MEM_HEADS, MEM_HEAD_DIM)
    km, vm = kv[:, :, 0], kv[:, :, 1]
    sc = jnp.einsum('bshd,bmhd->bhsm', q, km).astype(jnp.float32) * (MEM_HEAD_DIM ** -0.5)
    p = jax.nn.softmax(sc, axis=-1)
    o = jnp.einsum('bhsm,bmhd->bshd', p.astype(vm.dtype), vm)
    return o.reshape(q.shape[0], q.shape[1], MEM_W)

def setup_inputs(seed: int = 0) -> dict:
    key = jax.random.key(seed)
    ks = jax.random.split(key, 20)
    f32 = jnp.float32

    def nrm(k, shape, fan_in):
        return jax.random.normal(k, shape, f32) * (fan_in ** -0.5)

    def gain(k, dim):
        return 1.0 + 0.05 * jax.random.normal(k, (DEPTH, dim), f32)

    return {
        'x': jax.random.normal(ks[0], (BATCH, SEQ, D_MODEL), f32),
        'mem': jax.random.normal(ks[1], (BATCH, N_MEM, D_MODEL), f32),
        'g_mix_pre': gain(ks[2], D_MODEL),
        'g_mix_post': gain(ks[3], D_MODEL),
        'w_in': nrm(ks[4], (DEPTH, D_MODEL, D_IN), D_MODEL),
        'b_fgate': 3.0 + 0.5 * jax.random.normal(ks[5], (DEPTH, FOX_HEADS), f32),
        'b_branch': 0.02 * jax.random.normal(ks[6], (DEPTH, N_BRANCH * D_MODEL), f32),
        'sinks': 0.5 * jax.random.normal(ks[7], (DEPTH, SWA_HEADS), f32),
        'g_mem': gain(ks[8], D_MODEL),
        'w_mem_kv': nrm(ks[9], (DEPTH, D_MODEL, 2 * MEM_W), D_MODEL),
        'w_o_fox': nrm(ks[10], (DEPTH, FOX_W, D_MODEL), FOX_W),
        'w_o_swa': nrm(ks[11], (DEPTH, SWA_Q_W, D_MODEL), SWA_Q_W),
        'w_o_mem': nrm(ks[12], (DEPTH, MEM_W, D_MODEL), MEM_W),
        'w_out': nrm(ks[13], (DEPTH, D_MODEL, D_MODEL), D_MODEL),
        'g_ffn_pre': gain(ks[14], D_MODEL),
        'g_ffn_post': gain(ks[15], D_MODEL),
        'w_ffn_in': nrm(ks[16], (DEPTH, D_MODEL, 2 * D_FF), D_MODEL),
        'w_ffn_out': nrm(ks[17], (DEPTH, D_FF, D_MODEL), D_FF),
    }

def reference(x, mem, g_mix_pre, g_mix_post, w_in, b_fgate, b_branch, sinks, g_mem, w_mem_kv,
              w_o_fox, w_o_swa, w_o_mem, w_out, g_ffn_pre, g_ffn_post, w_ffn_in, w_ffn_out):
    b, s, _ = x.shape
    pos = jnp.arange(s)
    split_idx = list(np.cumsum(IN_SPLITS)[:-1])
    for l in range(DEPTH):
        h = rmsnorm(x, g_mix_pre[l])
        z = h @ w_in[l]
        (fq, fk, fv, flog, sq, sk, sv, mq, glog) = jnp.split(z, split_idx, axis=-1)

        logf = jax.nn.log_sigmoid((flog + b_fgate[l]).astype(jnp.float32))
        y_fox = fox_attention(fq.reshape(b, s, FOX_HEADS, HEAD_DIM),
                              fk.reshape(b, s, FOX_HEADS, HEAD_DIM),
                              fv.reshape(b, s, FOX_HEADS, HEAD_DIM), logf) @ w_o_fox[l]

        q_s = rope(sq.reshape(b, s, SWA_HEADS, HEAD_DIM), pos)
        k_s = rope(sk.reshape(b, s, SWA_KV_HEADS, HEAD_DIM), pos)
        v_s = sv.reshape(b, s, SWA_KV_HEADS, HEAD_DIM)
        y_swa = swa_sink_attention(q_s, k_s, v_s, sinks[l]) @ w_o_swa[l]

        mem_n = rmsnorm(mem, g_mem[l])
        y_mem = memory_cross_attention(mq.reshape(b, s, MEM_HEADS, MEM_HEAD_DIM), mem_n,
                                       w_mem_kv[l]) @ w_o_mem[l]

        gates = jax.nn.sigmoid(glog + b_branch[l]).reshape(b, s, N_BRANCH, D_MODEL)
        merged = gates[:, :, 0] * y_fox + gates[:, :, 1] * y_swa + gates[:, :, 2] * y_mem
        x = x + rmsnorm(merged @ w_out[l], g_mix_post[l])

        h = rmsnorm(x, g_ffn_pre[l])
        a, c = jnp.split(h @ w_ffn_in[l], 2, axis=-1)
        x = x + rmsnorm((jax.nn.silu(a) * c) @ w_ffn_out[l], g_ffn_post[l])
    return x


_drawn_inputs = setup_inputs


def setup_inputs(seed=0):
    import zlib

    import numpy as np

    out = dict(_drawn_inputs(seed))
    spreads = {}
    factors = {'b_branch': 8.0, 'sinks': 64.0, 'g_mem': 2.951}
    for name, (base, spread) in spreads.items():
        noise = np.random.default_rng([zlib.crc32(name.encode()), seed]).standard_normal(out[name].shape)
        drawn = base * np.exp(spread * noise) if base else spread * noise
        out[name] = __import__('jax').numpy.asarray(drawn.astype(out[name].dtype))
    for name, factor in factors.items():
        out[name] = (out[name] * factor).astype(out[name].dtype)
    return out
```

```python
from contextlib import ExitStack

import numpy as np
import concourse.bass as bass
from concourse import mybir

F32, F32R, BF16 = mybir.dt.float32, mybir.dt.float32r, mybir.dt.bfloat16
ALU, ACT, AX = mybir.AluOpType, mybir.ActivationFunctionType, mybir.AxisListType

P = 128
D = 1024
S = 1024
KD = D // P
NT = S // P
HALF = 512
N_MEM = 256
HD = 64
D_FF = 2816
NF = D_FF // P
EPS = 1e-6
BIG = 1.0e30
COL = dict(fq=0, fk=512, fv=1024, flog=1536, sq=1544, sk=2056, sv=2184, mq=2312, glog=2824)
FOX, SWA, MEM = 0, 1, 2


class Kit:

    sems = []

    def __init__(self, nc, stack):
        self.nc, self.stack = nc, stack

    def sb(self, name, shape, dtype=F32, side=None):
        return self.stack.enter_context(self.nc.sbuf_tensor(name, shape, dtype, side=side))

    def ps(self, name, shape, dtype=F32):
        return self.stack.enter_context(self.nc.psum_tensor(name, shape, dtype))

    def sem(self, name):
        made = self.nc.alloc_semaphore(name)
        Kit.sems.append(made)
        return made

    @classmethod
    def free_semaphores(cls, nc):
        nc.clear_and_free_semaphores(cls.sems)
        nc.all_engine_barrier()
        cls.sems = []


def f32(ap):
    return ap.bitcast(F32)


def product(pe, out, a_hi, a_lo, b_hi, b_lo, start, stop):
    pe.matmul(out, a_hi, b_hi, start=start, stop=False)
    pe.matmul(out, a_hi, b_lo, start=False, stop=False)
    return pe.matmul(out, a_lo, b_hi, start=False, stop=stop)


class Weights:

    def __init__(self, kit, name, ring, width, raw, hi, lo):
        self.ring, self.width = ring, width
        self.raw, self.hi, self.lo = raw, hi, lo
        self.loaded = [kit.sem(f"{name}_loaded{i}") for i in range(ring)]
        self.hi_ready = kit.sem(f"{name}_hi_ready")
        self.lo_ready = kit.sem(f"{name}_lo_ready")

    def view(self, tile, slot, a=0, b=None):
        return tile[:, slot * self.width + a:slot * self.width + (self.width if b is None else b)]


def normalise_stage(nc, T):
    with ExitStack() as stack:
        kit = Kit(nc, stack)
        nat = kit.sb("nat", [P, 4, D])
        normed = kit.sb("normed", [P, 2, D])
        junk = kit.sb("junk", [P, D])
        gains = kit.sb("gains", [P, 2, D])
        ssq = kit.sb("ssq", [P, 10])
        msq = kit.sb("msq", [P, 10])
        rstd = kit.sb("rstd", [P, 10])
        turned_ps = kit.ps("turned_ps", [P, 4, HALF])
        kv_ps = kit.ps("kv_ps", [P, 2, HALF])
        loaded = [kit.sem(f"nat_loaded{i}") for i in range(4)]
        consts_loaded = kit.sem("consts_loaded")
        g_loaded = kit.sem("gains_loaded")
        squared, meaned, rooted, scaled = (kit.sem(n) for n in ("squared", "meaned", "rooted", "scaled"))
        turned, hi_done, lo_done = (kit.sem(n) for n in ("turned", "hi_done", "lo_done"))
        kv_done, kv_kept = kit.sem("kv_done"), kit.sem("kv_kept")
        bf_ready = kit.sem("bf_ready")
        half_set = kit.sem("half_set")
        W = Weights(kit, "wkv", 3, D, T.w_raw, T.w_hi, T.w_lo)
        mem_hi, mem_lo = kit.sb("mem_hi", [P, KD, N_MEM], F32R), kit.sb("mem_lo", [P, KD, N_MEM], F32R)

        tiles = [(T.d["mem"][0, P * t:P * (t + 1), :], 0, mem_hi, mem_lo, t) for t in range(2)]
        tiles += [(T.d["x"][0, P * t:P * (t + 1), :], 1, T.h_hi, T.h_lo, t) for t in range(NT)]
        n_tiles = len(tiles)
        w_kv = T.d["w_mem_kv"][0].rearrange("(k p) n -> p k n", p=P)
        n_kv = 8

        block = stack.enter_context(nc.Block())

        @block.sync
        def _(sp):
            def load_w(n):
                if n >= 3:
                    sp.wait_ge(W.lo_ready, n - 2)
                sp.dma_start(W.view(W.raw, n % 3).rearrange("p (k n) -> p k n", k=KD),
                             w_kv[:, :, P * n:P * (n + 1)]).then_inc(W.loaded[n % 3], 16)

            for t, (src, *_) in enumerate(tiles):
                if t >= 4:
                    sp.wait_ge(scaled, t - 3)
                sp.dma_start(nat[:, t % 4, :], src).then_inc(loaded[t % 4], 16)
                if t == 0:
                    sp.dma_start(gains[:, 0, :], T.d["g_mem"][0:1, :].to_broadcast([P, D])).then_inc(g_loaded, 16)
                    sp.dma_start(T.ident[:], T.d["ident"]).then_inc(consts_loaded, 16)
                if t == 1:
                    sp.dma_start(gains[:, 1, :], T.d["g_mix_pre"][0:1, :].to_broadcast([P, D])).then_inc(g_loaded, 16)
                if t < n_kv:
                    load_w(t)
            sp.dma_start(T.masks[:], T.d["masks"]).then_inc(consts_loaded, 16)

        @block.scalar
        def _(act):
            def square(t):
                act.wait_ge(loaded[t % 4], 16 * (t // 4 + 1))
                if t >= 1:
                    act.wait_ge(squared, t)
                act.activation(junk[:], nat[:, t % 4, :], ACT.Square,
                               accum_out=ssq[:, t:t + 1]).then_inc(squared, 1)

            def split_w(n):
                act.wait_ge(W.loaded[n % 3], 16 * (n // 3 + 1))
                if n >= 3:
                    act.wait_ge(kv_done, n - 2)
                act.activation(W.view(W.hi, n % 3), W.view(W.raw, n % 3), ACT.Copy).then_inc(W.hi_ready, 1)

            def keep_kv(n):
                act.wait_ge(kv_done, n + 1)
                act.activation(T.mem_kv[:, n, :], kv_ps[:, n % 2, 0:N_MEM], ACT.Copy).then_inc(kv_kept, 1)

            square(0)
            square(1)
            for t, (_, _, hi, _, at) in enumerate(tiles):
                if t < n_kv:
                    split_w(t)
                if t + 2 < n_tiles:
                    square(t + 2)
                for b in range(2):
                    act.wait_ge(turned, 2 * t + b + 1)
                    act.activation(hi[:, 4 * b:4 * b + 4, P * at:P * (at + 1)],
                                   turned_ps[:, (2 * t + b) % 4, :].rearrange("p (c n) -> p c n", c=4),
                                   ACT.Copy).then_inc(hi_done, 1)
                if t >= 2:
                    keep_kv(t - 2)

        @block.gpsimd
        def _(pool):
            pool.memset(T.minus_half[:], -0.5).then_inc(half_set, 1)
            pool.wait_ge(half_set, 1)
            for t in range(n_tiles):
                pool.wait_ge(squared, t + 1)
                pool.tensor_scalar(msq[:, t:t + 1], ssq[:, t:t + 1], 1.0 / D, EPS,
                                   ALU.mult, ALU.add).then_inc(meaned, 1)
                pool.wait_ge(meaned, t + 1)
                pool.tensor_tensor(rstd[:, t:t + 1], msq[:, t:t + 1], T.minus_half[:], ALU.pow).then_inc(rooted, 1)

        @block.vector
        def _(dve):
            def scale(t):
                dve.wait_ge(rooted, t + 1)
                if t >= 2:
                    dve.wait_ge(turned, 2 * (t - 1))
                dve.wait_ge(g_loaded, 32)
                dve.scalar_tensor_tensor(out=normed[:, t % 2, :], in0=nat[:, t % 4, :],
                                         scalar=rstd[:, t:t + 1], in1=gains[:, tiles[t][1], :],
                                         op0=ALU.mult, op1=ALU.mult).then_inc(scaled, 1)

            scale(0)
            for t, (_, _, hi, lo, at) in enumerate(tiles):
                if t < n_kv:
                    dve.wait_ge(W.hi_ready, t + 1)
                    dve.tensor_tensor(W.view(W.lo, t % 3), W.view(W.raw, t % 3), f32(W.view(W.hi, t % 3)),
                                      ALU.subtract).then_inc(W.lo_ready, 1)
                if t + 1 < n_tiles:
                    scale(t + 1)
                for b in range(2):
                    dve.wait_ge(hi_done, 2 * t + b + 1)
                    cut = (slice(None), slice(4 * b, 4 * b + 4), slice(P * at, P * (at + 1)))
                    dve.tensor_tensor(lo[cut],
                                      turned_ps[:, (2 * t + b) % 4, :].rearrange("p (c n) -> p c n", c=4),
                                      f32(hi[cut]), ALU.subtract).then_inc(lo_done, 1)
            dve.wait_ge(consts_loaded, 32)
            dve.tensor_copy(T.ident_bf[:], T.ident[:]).then_inc(bf_ready, 1)
            dve.tensor_copy(T.masks_bf[:], T.masks[:]).then_inc(bf_ready, 1)

        @block.tensor
        def _(pe):
            def turn(t):
                pe.wait_ge(scaled, t + 1)
                for b in range(2):
                    n = 2 * t + b
                    if n >= 4:
                        pe.wait_ge(lo_done, n - 3)
                    for c in range(4):
                        mm = pe.transpose(turned_ps[:, n % 4, P * c:P * (c + 1)],
                                          normed[:, t % 2, P * (4 * b + c):P * (4 * b + c + 1)], T.ident[:])
                    mm.then_inc(turned, 1)

            def project_kv(n):
                pe.wait_ge(W.lo_ready, n + 1)
                if n >= 2:
                    pe.wait_ge(kv_kept, n - 1)
                for k in range(KD):
                    cut = slice(P * k, P * (k + 1))
                    mm = product(pe, kv_ps[:, n % 2, 0:N_MEM],
                                 W.view(W.hi, n % 3)[:, cut], W.view(W.lo, n % 3)[:, cut],
                                 mem_hi[:, k, :], mem_lo[:, k, :], start=(k == 0), stop=(k == KD - 1))
                mm.then_inc(kv_done, 1)

            pe.wait_ge(consts_loaded, 16)
            for t in range(n_tiles):
                turn(t)
                if t >= 2:
                    if t == 2:
                        pe.wait_ge(lo_done, 4)
                    project_kv(t - 2)


def shared_stage(nc, T):
    with ExitStack() as stack:
        kit = Kit(nc, stack)
        blocks = [COL["flog"], COL["sk"], COL["sv"]]
        nb = len(blocks)
        W = Weights(kit, "wsh", nb, D, T.w_raw, T.w_hi, T.w_lo)
        ps = kit.ps("shared_ps", [P, nb, 2, HALF])
        turn_ps = kit.ps("shared_turn_ps", [P, 2, HALF])
        nh = 8
        z, az, ez, sp_, lf, ones, cum, cum8 = (kit.sb(n, [nh, S]) for n in (
            "z", "abs_z", "exp_z", "softplus", "log_forget", "ones_row", "cum", "cum_scaled"))
        bias = kit.sb("forget_bias", [nh, 1])
        raw = kit.sb("shared_raw", [P, 2, S])
        rot = kit.sb("shared_rot", [P, S])
        done = kit.sem("shared_done")
        small_loaded = kit.sem("small_loaded")
        gate_act, gate_dve = kit.sem("gate_act"), kit.sem("gate_dve")
        cum_stored = kit.sem("cum_stored")
        kept = kit.sem("shared_kept")
        rot_loaded, roped = kit.sem("shared_rot_loaded"), kit.sem("shared_roped")
        mem_hi_done, mem_done = kit.sem("mem_hi_done"), kit.sem("mem_split_done")
        k_hi, k_done = kit.sem("swa_k_hi"), kit.sem("swa_k_done")
        turned, v_hi, v_done = kit.sem("shared_turned"), kit.sem("shared_v_hi"), kit.sem("shared_v_done")
        w_in = T.d["w_in"][0].rearrange("(k p) n -> p k n", p=P)

        block = stack.enter_context(nc.Block())

        @block.sync
        def _(sp):
            for n, col in enumerate(blocks):
                sp.dma_start(W.view(W.raw, n).rearrange("p (k n) -> p k n", k=KD),
                             w_in[:, :, col:col + P]).then_inc(W.loaded[n], 16)
            sp.dma_start(bias[:], T.d["b_fgate"][0:1, :].rearrange("a h -> h a")).then_inc(small_loaded, 16)
            sp.dma_start(T.rope[:], T.d["rope"]).then_inc(small_loaded, 16)
            sp.dma_start(T.sink[:], T.d["sinks"][0:1, :].to_broadcast([P, nh])).then_inc(small_loaded, 16)
            sp.wait_ge(kept, 2)
            for q in range(4):
                sp.dma_start(rot[32 * q:32 * q + 32, :], raw[32 * (q ^ 1):32 * (q ^ 1) + 32, 0, :])\
                    .then_inc(rot_loaded, 16)
            sp.wait_ge(gate_dve, 5)
            sp.dma_start(T.cum_dram, cum8[:]).then_inc(cum_stored, 16)
            sp.wait_ge(cum_stored, 16)

        @block.scalar
        def _(act):
            for n in range(nb):
                act.wait_ge(W.loaded[n], 16)
                act.activation(W.view(W.hi, n), W.view(W.raw, n), ACT.Copy).then_inc(W.hi_ready, 1)
            act.activation(T.mk_hi[:], T.mem_kv[:, 0:4, :], ACT.Copy).then_inc(mem_hi_done, 1)
            for b in range(2):
                act.wait_ge(turned, b + 1)
                act.activation(T.mv_hi[:, 2 * b:2 * b + 2, :, :],
                               turn_ps[:, b, :].rearrange("p (h t d) -> p h t d", h=2, t=2),
                               ACT.Copy).then_inc(mem_hi_done, 1)
            act.wait_ge(done, 2)
            act.wait_ge(small_loaded, 48)
            zp = ps[0:nh, 0, :, :].rearrange("p a n -> p (a n)")
            act.activation(z[:], zp, ACT.Identity, bias=bias[:, 0:1]).then_inc(gate_act, 1)
            act.activation(az[:], zp, ACT.Abs, bias=bias[:, 0:1]).then_inc(gate_act, 1)
            act.wait_ge(gate_act, 2)
            act.activation(ez[:], az[:], ACT.Exp, scale=-1.0).then_inc(gate_act, 1)
            act.wait_ge(gate_act, 3)
            act.activation(sp_[:], ez[:], ACT.Ln, bias=1.0).then_inc(gate_act, 1)
            for n in range(2):
                for h in range(2):
                    act.wait_ge(done, 2 * (n + 1) + h + 1)
                    act.activation(raw[:, n, HALF * h:HALF * (h + 1)], ps[:, n + 1, h, :],
                                   ACT.Copy).then_inc(kept, 1)
            act.wait_ge(roped, 3)
            for kv in range(2):
                for half in range(2):
                    act.activation(T.k1[64 * half:64 * half + 64, kv, :], raw[64 * kv:64 * kv + 64, 0, :],
                                   ACT.Copy).then_inc(k_hi, 1)
            for b in range(2):
                act.wait_ge(turned, 2 + b + 1)
                act.activation(T.v[:, :, 4 * b:4 * b + 4, 0, :],
                               turn_ps[:, b, :].rearrange("p (t h d) -> p h t d", t=4, h=2),
                               ACT.Copy).then_inc(v_hi, 1)

        @block.vector
        def _(dve):
            dve.memset(ones[:], 1.0).then_inc(gate_dve, 1)
            for n in range(nb):
                dve.wait_ge(W.hi_ready, n + 1)
                dve.tensor_tensor(W.view(W.lo, n), W.view(W.raw, n), f32(W.view(W.hi, n)),
                                  ALU.subtract).then_inc(W.lo_ready, 1)
            dve.wait_ge(mem_hi_done, 1)
            dve.tensor_tensor(T.mk_lo[:], T.mem_kv[:, 0:4, :], f32(T.mk_hi[:]), ALU.subtract).then_inc(mem_done, 1)
            for b in range(2):
                dve.wait_ge(mem_hi_done, b + 2)
                dve.tensor_tensor(T.mv_lo[:, 2 * b:2 * b + 2, :, :],
                                  turn_ps[:, b, :].rearrange("p (h t d) -> p h t d", h=2, t=2),
                                  f32(T.mv_hi[:, 2 * b:2 * b + 2, :, :]), ALU.subtract).then_inc(mem_done, 1)
            dve.wait_ge(small_loaded, 48)
            dve.tensor_scalar(T.sink_raw[:], T.sink[:], 1.0 / T.scale[SWA], None, ALU.mult).then_inc(mem_done, 1)
            dve.wait_ge(gate_act, 4)
            dve.scalar_tensor_tensor(out=lf[:], in0=z[:], scalar=0.0, in1=sp_[:],
                                     op0=ALU.min, op1=ALU.subtract).then_inc(gate_dve, 1)
            dve.wait_ge(gate_dve, 2)
            dve.tensor_tensor_scan(cum[:], ones[:], lf[:], 0.0, ALU.mult, ALU.add).then_inc(gate_dve, 1)
            dve.wait_ge(gate_dve, 3)
            dve.tensor_scalar(cum8[:], cum[:], -1.0 / T.scale[FOX], None, ALU.mult).then_inc(gate_dve, 2)
            dve.wait_ge(rot_loaded, 64)
            dve.tensor_tensor(raw[:, 0, :], raw[:, 0, :], T.rope[:, 0, :], ALU.mult).then_inc(roped, 1)
            dve.tensor_tensor(rot[:], rot[:], T.rope[:, 1, :], ALU.mult).then_inc(roped, 1)
            dve.wait_ge(roped, 2)
            dve.tensor_tensor(raw[:, 0, :], raw[:, 0, :], rot[:], ALU.add).then_inc(roped, 1)
            for kv in range(2):
                dve.wait_ge(k_hi, 2 * kv + 2)
                rows = slice(64 * kv, 64 * kv + 64)
                for half in range(2):
                    dve.tensor_tensor(T.k2[64 * half:64 * half + 64, kv, :], raw[rows, 0, :],
                                      f32(T.k1[rows, kv, :]), ALU.subtract).then_inc(k_done, 1)
            for b in range(2):
                dve.wait_ge(v_hi, b + 1)
                dve.tensor_tensor(T.v[:, :, 4 * b:4 * b + 4, 1, :],
                                  turn_ps[:, b, :].rearrange("p (t h d) -> p h t d", t=4, h=2),
                                  f32(T.v[:, :, 4 * b:4 * b + 4, 0, :]), ALU.subtract).then_inc(v_done, 1)

        @block.tensor
        def _(pe):
            for b in range(2):
                for h in range(2):
                    for t in range(2):
                        at = P * (2 * h + t)
                        mm = pe.transpose(turn_ps[:, b, at:at + P],
                                          T.mem_kv[:, 4 + 2 * b + h, P * t:P * (t + 1)], T.ident[:])
                mm.then_inc(turned, 1)
            for n in range(nb):
                pe.wait_ge(W.lo_ready, n + 1)
                for h in range(2):
                    for k in range(KD):
                        cut = slice(P * k, P * (k + 1))
                        at = slice(HALF * h, HALF * (h + 1))
                        mm = product(pe, ps[:, n, h, :], W.view(W.hi, n)[:, cut], W.view(W.lo, n)[:, cut],
                                     T.h_hi[:, k, at], T.h_lo[:, k, at], start=(k == 0), stop=(k == KD - 1))
                    mm.then_inc(done, 1)
            pe.wait_ge(kept, 4)
            pe.wait_ge(mem_done, 3)
            for b in range(2):
                for t in range(4):
                    at = P * (4 * b + t)
                    mm = pe.transpose(turn_ps[:, b, P * t:P * (t + 1)], raw[:, 1, at:at + P], T.ident[:])
                mm.then_inc(turned, 1)


def attention_stage(nc, T, branch):
    name = ("fox", "swa", "mem")[branch]
    scale = T.scale[branch]
    turns = {FOX: 4, SWA: 2, MEM: 2}[branch]
    nb = {FOX: 3, SWA: 2, MEM: 2}[branch]
    heads = {FOX: 2, SWA: 4, MEM: 2}[branch]
    chunks = {FOX: 1, SWA: 2, MEM: 2}[branch]
    units = [(a, g) for a in range(heads) for g in range(NT // 2)]
    NU = len(units)
    NQ = 2 * NU

    def keys(i):
        return {FOX: (0, i + 1), SWA: (max(i - 1, 0), i + 1), MEM: (0, 2)}[branch]

    def key_packs(g):
        out, packs = [], [[]]
        for j in range(keys(2 * g)[0], keys(2 * g + 1)[1]):
            sees = [keys(2 * g + q)[0] <= j < keys(2 * g + q)[1] for q in range(2)]
            out.append((j, 0 if sees[0] else P, 2 * P if sees[1] else P))
        for j, a, b in sorted(out, key=lambda x: x[2] - x[1] < 2 * P):
            used = packs[-1][-1][3] + packs[-1][-1][2] - packs[-1][-1][1] if packs[-1] else 0
            if used + b - a > HALF:
                packs.append([])
                used = 0
            packs[-1].append((j, a, b, used))
        return packs

    packs = [key_packs(g) for _, g in units]
    first_pack = [sum(len(x) for x in packs[:u]) for u in range(NU + 1)]
    NS = first_pack[NU]
    width_of = lambda pack: pack[-1][3] + pack[-1][2] - pack[-1][1]
    score_pieces = [[min(HALF, P * (keys(2 * g + q)[1] - keys(2 * g + q)[0]) - c)
                     for c in range(0, P * (keys(2 * g + q)[1] - keys(2 * g + q)[0]), HALF)]
                    for _, g in units for q in range(2)]
    first_piece = [sum(len(x) for x in score_pieces[:n]) for n in range(NQ + 1)]
    NP = first_piece[NQ]
    RS = 3
    bank = lambda it, n: (n if branch == FOX else it * NP + n) % RS
    unit_of_chunk = NU // chunks

    G = nb * 2 * KD
    start_groups = KD
    left = G - start_groups
    fill = [(left * (p + 1)) // (2 * NU) - (left * p) // (2 * NU) for p in range(2 * NU)]
    fill_at = [start_groups + sum(fill[:p]) for p in range(2 * NU + 1)]
    place = lambda group: next((p for p in range(2 * NU) if fill_at[p] <= group < fill_at[p + 1]), 0)
    split_before = {b: max(0, place(2 * KD * b) // 2 - 1) for b in range(1, nb)}
    halves_by = lambda p: fill_at[p] // KD

    with ExitStack() as stack:
        kit = Kit(nc, stack)
        W = Weights(kit, "w" + name, nb, D, T.w_raw, T.w_hi, T.w_lo)
        raw = kit.sb(name + "_raw", [P, nb, S])
        prob = kit.sb(name + "_prob", [P, 2, 2, S if branch == FOX else 2 * P])
        n_packs = max(len(x) for x in packs)
        pt_hi = kit.sb(name + "_pt_hi", [P, n_packs, HALF], F32R)
        pt_lo = kit.sb(name + "_pt_lo", [P, n_packs, HALF], F32R)
        out_sb = kit.sb(name + "_out", [P, chunks, S])
        tmp = kit.sb(name + "_tmp", [64, 2, 2 * P])
        neg, den, den2, inv, esink = (kit.sb(f"{name}_{n}", [P, 2, 2]) for n in
                                      ("neg", "den", "den2", "inv", "esink"))
        top = kit.sb(name + "_top", [P, 2, 2, 2])
        top2 = kit.sb(name + "_top2", [P, 2, 2])
        if branch == MEM:
            q_hi, q_lo = (kit.sb("mem_" + n, [P, heads, S], F32R) for n in ("q_hi", "q_lo"))
            k_hi, k_lo, v_hi, v_lo = T.mk_hi, T.mk_lo, T.mv_hi, T.mv_lo
        else:
            q_both = kit.sb(name + "_q", [P, heads, S], F32R)
        if branch == SWA:
            rot = kit.sb("swa_rot", [P, nb, S])
            k1, k2, v = T.k1, T.k2, T.v
        if branch == FOX:
            k1 = kit.sb("fox_k1", [P, 2, S], F32R)
            k2 = kit.sb("fox_k2", [P, S], F32R)
            v = kit.sb("fox_v", [P, 2, NT, 2, HD], F32R)
            cum_b = kit.sb("fox_cum", [P, 2, S])
        proj_ps = kit.ps(name + "_proj_ps", [P, 2, HALF])
        score_ps = kit.ps(name + "_score_ps", [P, RS, HALF])
        turn_ps = kit.ps(name + "_turn_ps", [P, 2, HALF])
        out_ps = kit.ps(name + "_out_ps", [P, HALF])

        proj_done = kit.sem(name + "_proj_done")
        kept = kit.sem(name + "_kept")
        act_unpacked = kit.sem(name + "_act_unpacked")
        dve_unpacked = kit.sem(name + "_dve_unpacked")
        v_turned = kit.sem(name + "_v_turned")
        scored = kit.sem(name + "_scored")
        maxed = kit.sem(name + "_maxed")
        topped = kit.sem(name + "_topped")
        negated = kit.sem(name + "_negated")
        exped = kit.sem(name + "_exped")
        sunk = kit.sem(name + "_sunk")
        summed = kit.sem(name + "_summed")
        inverted = kit.sem(name + "_inverted")
        normed = kit.sem(name + "_normed")
        turned = kit.sem(name + "_turned")
        pt_hi_done = kit.sem(name + "_pt_hi_done")
        pt_lo_done = kit.sem(name + "_pt_lo_done")
        pv_done = kit.sem(name + "_pv_done")
        lower_kept = kit.sem(name + "_lower_kept")
        out_done = kit.sem(name + "_out_done")
        stored = [kit.sem(f"{name}_stored{c}") for c in range(chunks)]
        rot_loaded = [kit.sem(f"{name}_rot_loaded{b}") for b in range(nb)]
        roped = kit.sem(name + "_roped")
        cum_loaded = kit.sem(name + "_cum_loaded")
        waited = kit.sem(name + "_waited")
        score_free = maxed if branch == FOX else exped
        ACT_U = {FOX: 6, SWA: 4, MEM: 2}[branch]
        DVE_U = {FOX: 8, SWA: 4, MEM: 2}[branch]
        K_ACT, K_DVE = {FOX: (4, 6), SWA: (4, 4), MEM: (2, 2)}[branch]
        w_in = T.d["w_in"][0].rearrange("(k p) n -> p k n", p=P)
        out_dram = T.out_dram[branch]

        def col(turn, b):
            if branch == FOX:
                return turn * P + (COL["fq"], COL["fk"], COL["fv"])[b]
            return COL["sq" if branch == SWA else "mq"] + (2 * turn + b) * P

        block = stack.enter_context(nc.Block())

        def over_turns(engine, body):
            if turns > 2:
                with engine.Fori(0, turns - 1) as it:
                    body(it, True)
            else:
                for it in range(turns - 1):
                    body(it, True)
            body(turns - 1, False)

        @block.sync
        def _(sp):
            for c in range(chunks):
                sp.sem_inc(stored[c], 1)

            def load_w(turn, b, wait):
                if wait is not None:
                    sp.wait_ge(W.lo_ready, wait)
                sp.dma_start(W.view(W.raw, b).rearrange("p (k n) -> p k n", k=KD),
                             w_in[:, :, bass.ds(col(turn, b), P)]).then_inc(W.loaded[b], 16)

            def body(it, more):
                if branch == FOX:
                    sp.wait_ge(maxed, it * NP + 3)
                    sp.dma_start(cum_b[:], T.cum_dram[bass.ds(it * 2, 2), :].rearrange("(o h) s -> o h s", o=1)
                                 .to_broadcast([P, 2, S])).then_inc(cum_loaded, 16)
                if branch == SWA:
                    for b in range(nb):
                        sp.wait_ge(kept, (it * nb + b) * 2 + 2 + 2)
                        for q in range(4):
                            sp.dma_start(rot[32 * q:32 * q + 32, b, :], raw[32 * (q ^ 1):32 * (q ^ 1) + 32, b, :])\
                                .then_inc(rot_loaded[b], 16)
                if more:
                    for b in range(nb):
                        load_w(it + 1, b, it * nb + b + 1)
                for c in range(chunks):
                    sp.wait_ge(out_done, it * NU + (c + 1) * unit_of_chunk + 1)
                    sp.dma_start(out_dram[bass.ds(P * (it * chunks + c), P), :], out_sb[:, c, :])\
                        .then_inc(stored[c], 16)

            for b in range(nb):
                load_w(0, b, None)
            over_turns(sp, body)
            for c in range(chunks):
                sp.wait_ge(stored[c], 16 * turns + 1)

        @block.scalar
        def _(act):
            act.sem_inc(kept, 2)
            act.sem_inc(exped, RS)

            def split_w(turn, b, wait):
                act.wait_ge(W.loaded[b], 16 * turn + 16)
                if wait is not None:
                    act.wait_ge(proj_done, wait)
                act.activation(W.view(W.hi, b), W.view(W.raw, b), ACT.Copy).then_inc(W.hi_ready, 1)

            def keep(turn, n):
                act.wait_ge(proj_done, turn * (2 * nb) + n + 1)
                act.activation(raw[:, n // 2, HALF * (n % 2):HALF * (n % 2 + 1)], proj_ps[:, n % 2, :],
                               ACT.Copy).then_inc(kept, 1)

            def unpack(it):
                act.wait_ge(kept, (it + 1) * 2 * nb + 2)
                act.wait_ge(scored, it * NP + 1)
                if branch == FOX:
                    act.activation(q_both[0:64, 0, :], raw[0:64, 0, :], ACT.Copy).then_inc(act_unpacked, 1)
                    act.activation(q_both[64:P, 1, :], raw[64:P, 0, :], ACT.Copy).then_inc(act_unpacked, 1)
                    act.activation(k1[64:P, 0, :], raw[0:64, 1, :], ACT.Copy).then_inc(act_unpacked, 1)
                    act.activation(k1[0:64, 1, :], raw[64:P, 1, :], ACT.Copy).then_inc(act_unpacked, 1)
                    act.wait_ge(pv_done, it * NU + 1)
                    for b in range(2):
                        act.wait_ge(v_turned, it * 2 + b + 1)
                        act.activation(v[:, :, 4 * b:4 * b + 4, 0, :],
                                       score_ps[:, b, :]
                                       .rearrange("p (t h d) -> p h t d", t=4, h=2),
                                       ACT.Copy).then_inc(act_unpacked, 1)
                if branch == SWA:
                    for b in range(nb):
                        act.wait_ge(roped, (it * nb + b + 1) * 3)
                        for c in range(2):
                            act.activation(q_both[64 * c:64 * c + 64, 2 * b + c, :], raw[64 * c:64 * c + 64, b, :],
                                           ACT.Copy).then_inc(act_unpacked, 1)
                if branch == MEM:
                    for b in range(nb):
                        act.activation(q_hi[:, b, :], raw[:, b, :], ACT.Copy).then_inc(act_unpacked, 1)

            def exp(it, u):
                act.wait_ge(negated, it * NU + u + 1)
                for q in range(2):
                    i = 2 * units[u][1] + q
                    nk = P * (keys(i)[1] - keys(i)[0])
                    p = prob[:, u % 2, q, 0:nk]
                    n = bank(it, 2 * u + q)
                    act.activation(p, p if branch == FOX else score_ps[:, n, 0:nk], ACT.Exp,
                                   bias=neg[:, u % 2, q:q + 1], scale=scale,
                                   accum_out=den[:, u % 2, q:q + 1]).then_inc(exped, 1)
                if branch == SWA:
                    head = heads * it + units[u][0]
                    act.activation(esink[:, u % 2, :], neg[:, u % 2, :], ACT.Exp,
                                   bias=T.sink[:, head:head + 1]).then_inc(sunk, 1)

            def split_hi(it, u):
                for s, pack in enumerate(packs[u]):
                    n, w = first_pack[u] + s, width_of(pack)
                    act.wait_ge(turned, it * NS + n + 1)
                    act.activation(pt_hi[:, s, 0:w], turn_ps[:, n % 2, 0:w], ACT.Copy).then_inc(pt_hi_done, 1)

            def keep_lower(it, u):
                if branch != MEM:
                    act.wait_ge(pv_done, it * NU + u + 2)
                    act.activation(tmp[:, u % 2, :], out_ps[64:P, 0:2 * P], ACT.Copy).then_inc(lower_kept, 1)

            def body(it, more):
                if more:
                    split_w(it + 1, 0, it * (2 * nb) + 2)
                unpack(it)
                kept_halves = 0
                for u in range(NU + 2):
                    if 2 <= u:
                        keep_lower(it, u - 2)
                    if more:
                        for b in range(1, nb):
                            if split_before[b] == u:
                                split_w(it + 1, b, (it * nb + b) * 2 + 2)
                        finished = halves_by(min(2 * u + 1, 2 * NU))
                        while kept_halves < finished:
                            if kept_halves == 0:
                                act.wait_ge(dve_unpacked, it * DVE_U + DVE_U)
                            keep(it + 1, kept_halves)
                            kept_halves += 1
                    if 1 <= u <= NU:
                        split_hi(it, u - 1)
                    if u < NU:
                        exp(it, u)

            for b in range(nb):
                split_w(0, b, None)
            for n in range(2 * nb):
                keep(0, n)
            over_turns(act, body)

        @block.vector
        def _(dve):
            dve.sem_inc(maxed, RS)
            dve.sem_inc(pt_lo_done, 2)
            dve.sem_inc(out_done, 1)

            def split_w(turn, b):
                dve.wait_ge(W.hi_ready, turn * nb + b + 1)
                dve.tensor_tensor(W.view(W.lo, b), W.view(W.raw, b), f32(W.view(W.hi, b)),
                                  ALU.subtract).then_inc(W.lo_ready, 1)

            def rope(it, b):
                dve.wait_ge(rot_loaded[b], 64 * (it + 1))
                n = (it * nb + b) * 3
                dve.tensor_tensor(raw[:, b, :], raw[:, b, :], T.rope[:, 0, :], ALU.mult).then_inc(roped, 1)
                dve.tensor_tensor(rot[:, b, :], rot[:, b, :], T.rope[:, 1, :], ALU.mult).then_inc(roped, 1)
                dve.wait_ge(roped, n + 2)
                dve.tensor_tensor(raw[:, b, :], raw[:, b, :], rot[:, b, :], ALU.add).then_inc(roped, 1)

            def low(out, whole, high):
                dve.tensor_tensor(out, whole, f32(high), ALU.subtract).then_inc(dve_unpacked, 1)

            def unpack(it):
                dve.wait_ge(kept, (it + 1) * 2 * nb + 2)
                dve.wait_ge(scored, it * NP + 1)
                if branch == FOX:
                    dve.tensor_copy(k1[0:64, 0, :], raw[0:64, 1, :]).then_inc(dve_unpacked, 1)
                    dve.tensor_copy(k1[64:P, 1, :], raw[64:P, 1, :]).then_inc(dve_unpacked, 1)
                    for c in range(2):
                        rows, other = slice(64 * c, 64 * c + 64), slice(64 - 64 * c, P - 64 * c)
                        dve.wait_ge(act_unpacked, it * ACT_U + c + 1)
                        low(q_both[other, c, :], raw[rows, 0, :], q_both[rows, c, :])
                    for c in range(2):
                        rows = slice(64 * c, 64 * c + 64)
                        dve.wait_ge(dve_unpacked, it * DVE_U + c + 1)
                        low(k2[rows, :], raw[rows, 1, :], k1[rows, c, :])
                    for b in range(2):
                        dve.wait_ge(act_unpacked, it * ACT_U + 4 + b + 1)
                        low(v[:, :, 4 * b:4 * b + 4, 1, :],
                            score_ps[:, b, :].rearrange("p (t h d) -> p h t d", t=4, h=2),
                            v[:, :, 4 * b:4 * b + 4, 0, :])
                if branch == SWA:
                    for b in range(nb):
                        rope(it, b)
                        for c in range(2):
                            rows, other = slice(64 * c, 64 * c + 64), slice(64 - 64 * c, P - 64 * c)
                            dve.wait_ge(act_unpacked, it * ACT_U + 2 * b + c + 1)
                            low(q_both[other, 2 * b + c, :], raw[rows, b, :], q_both[rows, 2 * b + c, :])
                if branch == MEM:
                    for b in range(nb):
                        dve.wait_ge(act_unpacked, it * ACT_U + b + 1)
                        low(q_lo[:, b, :], raw[:, b, :], q_hi[:, b, :])

            def maxima(it, u):
                a, g = units[u]
                if branch == FOX and u == 0:
                    dve.wait_ge(cum_loaded, 16 * it + 16)
                for q in range(2):
                    for c, w in enumerate(score_pieces[2 * u + q]):
                        n = first_piece[2 * u + q] + c
                        dve.wait_ge(scored, it * NP + n + 2)
                        if branch == FOX:
                            dve.sem_inc(waited, 1)
                            at = slice(HALF * c, HALF * c + w)
                            dve.tensor_tensor_reduce(prob[:, u % 2, q, at], score_ps[:, bank(it, n), 0:w],
                                                     cum_b[:, a, at], 1.0, -3.0e38, ALU.add, ALU.max,
                                                     top[:, u % 2, q, c:c + 1]).then_inc(maxed, 1)
                        else:
                            dve.reduce_max(top[:, u % 2, q, 0:1], score_ps[:, bank(it, n), 0:w], AX.X)\
                                .then_inc(maxed, 1)
                dve.wait_ge(maxed, it * NP + first_piece[2 * u + 2] + RS)
                tops = top[:, u % 2, :, 0]
                if len(score_pieces[2 * u]) == 2:
                    dve.tensor_tensor(top2[:, u % 2, :], top[:, u % 2, :, 0], top[:, u % 2, :, 1],
                                      ALU.max).then_inc(topped, 1)
                    two = sum(len(score_pieces[2 * v]) == 2 for v in range(NU))
                    dve.wait_ge(topped, it * two + sum(len(score_pieces[2 * v]) == 2 for v in range(u + 1)))
                    tops = top2[:, u % 2, :]
                if branch == SWA:
                    head = heads * it + a
                    dve.tensor_scalar(neg[:, u % 2, :], tops, T.sink_raw[:, head:head + 1], -scale,
                                      ALU.max, ALU.mult).then_inc(negated, 1)
                else:
                    dve.tensor_scalar(neg[:, u % 2, :], tops, -scale, None, ALU.mult).then_inc(negated, 1)

            def normalise(it, u):
                dve.wait_ge(exped, it * NQ + 2 * u + 2 + RS)
                total = den
                if branch == SWA:
                    dve.wait_ge(sunk, it * NU + u + 1)
                    dve.tensor_tensor(den2[:, u % 2, :], den[:, u % 2, :], esink[:, u % 2, :],
                                      ALU.add).then_inc(summed, 1)
                    dve.wait_ge(summed, it * NU + u + 1)
                    total = den2
                dve.reciprocal(inv[:, u % 2, :], total[:, u % 2, :]).then_inc(inverted, 1)
                dve.wait_ge(inverted, it * NU + u + 1)
                for q in range(2):
                    i = 2 * units[u][1] + q
                    nk = P * (keys(i)[1] - keys(i)[0])
                    p = prob[:, u % 2, q, 0:nk]
                    dve.tensor_scalar(p, p, inv[:, u % 2, q:q + 1], None, ALU.mult).then_inc(normed, 1)

            def split_lo(it, u):
                for s, pack in enumerate(packs[u]):
                    n, w = first_pack[u] + s, width_of(pack)
                    dve.wait_ge(pt_hi_done, it * NS + n + 1)
                    dve.tensor_tensor(pt_lo[:, s, 0:w], turn_ps[:, n % 2, 0:w], f32(pt_hi[:, s, 0:w]),
                                      ALU.subtract).then_inc(pt_lo_done, 1)

            def keep_out(it, u):
                a, g = units[u]
                at = slice(2 * P * g, 2 * P * (g + 1))
                chunk = u // unit_of_chunk
                if u % unit_of_chunk == 0:
                    dve.wait_ge(stored[chunk], 16 * it + 1)
                if branch == MEM:
                    dve.wait_ge(pv_done, it * NU + u + 2)
                    dve.tensor_copy(out_sb[:, chunk, at], out_ps[:, 0:2 * P]).then_inc(out_done, 1)
                else:
                    dve.wait_ge(lower_kept, it * NU + u + 1)
                    rows = slice(64 * (a % 2), 64 * (a % 2) + 64)
                    dve.tensor_tensor(out_sb[rows, chunk, at], out_ps[0:64, 0:2 * P], tmp[:, u % 2, :],
                                      ALU.add).then_inc(out_done, 1)

            def body(it, more):
                if more:
                    split_w(it + 1, 0)
                unpack(it)
                for u in range(NU + 2):
                    if more:
                        for b in range(1, nb):
                            if split_before[b] == u:
                                split_w(it + 1, b)
                    if u < NU:
                        maxima(it, u)
                    if 2 <= u:
                        keep_out(it, u - 2)
                    if 1 <= u <= NU:
                        split_lo(it, u - 1)
                    if u < NU:
                        normalise(it, u)

            for b in range(nb):
                split_w(0, b)
            over_turns(dve, body)

        @block.tensor
        def _(pe):
            pe.sem_inc(scored, 1)
            pe.sem_inc(pv_done, 1)

            def project(turn, first, last):
                for n in range(first, last):
                    b, half, k = n // (2 * KD), (n // KD) % 2, n % KD
                    if n % (2 * KD) == 0:
                        pe.wait_ge(W.lo_ready, turn * nb + b + 1)
                    if k == 0:
                        pe.wait_ge(kept, turn * (2 * nb) + 2 * b + half + 1)
                    cut, at = slice(P * k, P * (k + 1)), slice(HALF * half, HALF * (half + 1))
                    mm = product(pe, proj_ps[:, half, :], W.view(W.hi, b)[:, cut], W.view(W.lo, b)[:, cut],
                                 T.h_hi[:, k, at], T.h_lo[:, k, at], start=(k == 0), stop=(k == KD - 1))
                    if k == KD - 1:
                        mm.then_inc(proj_done, 1)

            def turn_values(it):
                pe.wait_ge(kept, (it + 1) * 2 * nb + 2)
                pe.wait_ge(maxed, it * NP + RS)
                for b in range(2):
                    for t in range(4):
                        mm = pe.transpose(score_ps[:, b, P * t:P * (t + 1)],
                                          raw[:, 2, P * (4 * b + t):P * (4 * b + t + 1)], T.ident[:])
                    mm.then_inc(v_turned, 1)

            def scores(it, u):
                a, g = units[u]
                if u == 0:
                    pe.wait_ge(act_unpacked, it * ACT_U + K_ACT)
                    pe.wait_ge(dve_unpacked, it * DVE_U + DVE_U)
                for q in range(2):
                    i = 2 * g + q
                    k0, k1_ = keys(i)
                    nk = P * (k1_ - k0)
                    cut = slice(P * i, P * (i + 1))
                    for c, w in enumerate(score_pieces[2 * u + q]):
                        n = first_piece[2 * u + q] + c
                        pe.wait_ge(score_free, it * NP + n + 1)
                        out = score_ps[:, bank(it, n), 0:w]
                        at = slice(P * k0 + HALF * c, P * k0 + HALF * c + w)
                        last = HALF * c + w == nk
                        if branch == MEM:
                            head = heads * it + a
                            product(pe, out, q_hi[:, a, cut], q_lo[:, a, cut], k_hi[:, head, at],
                                    k_lo[:, head, at], start=True, stop=True).then_inc(scored, 1)
                            continue
                        rows = slice(64 * (a % 2), 64 * (a % 2) + 64)
                        kk1, kk2 = (k1[:, a, at], k2[rows, at]) if branch == FOX else \
                                   (k1[:, it, at], k2[rows, it, at])
                        pe.matmul(out, q_both[:, a, cut], kk1, start=True, stop=False)
                        mm = pe.matmul(out, q_both[rows, a, cut], kk2, start=False, stop=not last)
                        if last:
                            band = P if branch == FOX else w
                            mask = T.masks_bf[:, 0:P] if branch == FOX else T.masks_bf[:, 3 * P - w:3 * P]
                            mm = pe.matmul(score_ps[:, bank(it, n), w - band:w], T.ident_bf[:], mask,
                                           start=False, stop=True)
                        mm.then_inc(scored, 1)

            def transposes(it, u):
                g = units[u][1]
                pe.wait_ge(normed, it * NQ + 2 * u + 2)
                for s, pack in enumerate(packs[u]):
                    n = first_pack[u] + s
                    pe.wait_ge(pt_lo_done, it * NS + n + 1)
                    for j, a, b, to in pack:
                        for q in range(a // P, b // P):
                            at = P * (j - keys(2 * g + q)[0])
                            c = to + P * q - a
                            mm = pe.transpose(turn_ps[:, n % 2, c:c + P], prob[:, u % 2, q, at:at + P],
                                              T.ident[:])
                    mm.then_inc(turned, 1)

            def outputs(it, u):
                head = units[u][0]
                pe.wait_ge(out_done, it * NU + u + 1)
                pe.wait_ge(pt_lo_done, it * NS + first_pack[u + 1] + 2)
                parts = [(s, *part) for s, pack in enumerate(packs[u]) for part in pack]
                for s, j, a, b, to in parts:
                    first, last = (s, j, a, b, to) == parts[0], (s, j, a, b, to) == parts[-1]
                    out, hi, lo = out_ps[:, a:b], pt_hi[:, s, to:to + b - a], pt_lo[:, s, to:to + b - a]
                    if branch == MEM:
                        mm = product(pe, out, v_hi[:, heads * it + head, j, :], v_lo[:, heads * it + head, j, :],
                                     hi, lo, start=first, stop=last)
                    else:
                        vv = v[:, head if branch == FOX else it, j, :, :].rearrange("p a d -> p (a d)")
                        pe.matmul(out, vv, hi, start=first, stop=False)
                        mm = pe.matmul(out, vv, lo, start=False, stop=last)
                mm.then_inc(pv_done, 1)

            def body(it, more):
                if branch == FOX:
                    turn_values(it)
                if more:
                    project(it + 1, 0, start_groups)
                for u in range(NU + 1):
                    if u < NU:
                        scores(it, u)
                        if more:
                            project(it + 1, fill_at[2 * u], fill_at[2 * u + 1])
                    if u >= 1:
                        transposes(it, u - 1)
                    if u < NU and more:
                        project(it + 1, fill_at[2 * u + 1], fill_at[2 * u + 2])
                    if u >= 1:
                        outputs(it, u - 1)

            project(0, 0, G)
            over_turns(pe, body)


def merge_stage(nc, T):
    with ExitStack() as stack:
        kit = Kit(nc, stack)
        NJ = KD
        KO = 4
        width = (KD + KO) * P
        W = Weights(kit, "wmg", 2, width, T.w_raw, T.w_hi, T.w_lo)
        o_hi, o_lo = (kit.sb(n, [P, 2, KO, S], F32R) for n in ("branch_hi", "branch_lo"))
        o_raw = kit.sb("branch_raw", [P, S])
        gate = kit.sb("gate", [P, 2, HALF])
        term = kit.sb("term", [P, 2, HALF])
        bias = kit.sb("gate_bias", [P, 3 * NJ])
        gate_ps, y_ps = kit.ps("gate_ps", [P, 2, HALF]), kit.ps("y_ps", [P, 2, HALF])
        bias_loaded, first_loaded = kit.sem("gate_bias_loaded"), kit.sem("branch0_loaded")
        raw_loaded = kit.sem("branch_raw_loaded")
        o_hi_done, o_lo_done = kit.sem("branch_hi_done"), kit.sem("branch_lo_done")
        gate_done = kit.sem("gate_done")
        y_done = kit.sem("y_done")
        waited = kit.sem("merge_waited")
        gated = kit.sem("gated")
        weighted = kit.sem("weighted")
        summed = kit.sem("merged_summed")
        w_in = T.d["w_in"][0].rearrange("(k p) n -> p k n", p=P)
        w_o = [T.d[n][0].rearrange("(k p) n -> p k n", p=P) for n in ("w_o_fox", "w_o_swa", "w_o_mem")]

        block = stack.enter_context(nc.Block())

        @block.sync
        def _(sp):
            def load(b, j, s, n):
                if n is not None:
                    sp.wait_ge(W.lo_ready, n - 1)
                sp.dma_start(W.view(W.raw, s, 0, KD * P).rearrange("p (k n) -> p k n", k=KD),
                             w_in[:, :, bass.ds(j * P + (COL["glog"] + b * D), P)]).then_inc(W.loaded[s], 16)
                sp.dma_start(W.view(W.raw, s, KD * P).rearrange("p (k n) -> p k n", k=KO),
                             w_o[b][:, :, bass.ds(j * P, P)]).then_inc(W.loaded[s], 16)

            def load_pair(b, it):
                for s in range(2):
                    load(b, it * 2 + s, s, it * 2 + (b * NJ + s))
                if b < 2:
                    sp.wait_ge(o_lo_done, it + (KO + b * KO))
                    sp.dma_start(o_raw[:], T.out_dram[b + 1][bass.ds(it * P, P), :]).then_inc(raw_loaded, 16)

            sp.dma_start(T.merged[:, 0:KO, :], T.out_dram[0].rearrange("(c p) s -> p c s", p=P))\
                .then_inc(first_loaded, 16)
            load(0, 0, 0, None)
            load(0, 1, 1, None)
            sp.dma_start(bias[:], T.d["b_branch"][0].rearrange("(n p) -> p n", p=P),
                         allow_slow_non_contiguous=True).then_inc(bias_loaded, 16)
            sp.wait_ge(o_lo_done, KO)
            sp.dma_start(o_raw[:], T.out_dram[1][0:P, :]).then_inc(raw_loaded, 16)
            with sp.Fori(1, NJ // 2) as it:
                load_pair(0, it)
            for b in (1, 2):
                with sp.Fori(0, NJ // 2) as it:
                    load_pair(b, it)

        @block.scalar
        def _(act):
            def split_w(s, n):
                act.wait_ge(W.loaded[s], n * 16 + (32 - 16 * s))
                act.activation(W.view(W.hi, s), W.view(W.raw, s), ACT.Copy).then_inc(W.hi_ready, 1)

            def step(b, it, s, more):
                n = it * 2 + (b * NJ + s)
                if more:
                    act.wait_ge(y_done, n * 2 + 2)
                    split_w(1 - s, n + 1)
                for h in range(2):
                    act.wait_ge(gate_done, n * 2 + h + 1)
                    act.wait_ge(weighted, n * 2 + h + 1)
                    act.sem_inc(waited, 1)
                    act.activation(gate[:, h, :], gate_ps[:, h, :], ACT.Sigmoid,
                                   bias=bias[:, bass.ds(n, 1)]).then_inc(gated, 1)

            def split_branch(b, it):
                act.wait_ge(raw_loaded, it * 16 + ((b - 1) * KO * 16 + 16))
                act.sem_inc(waited, 1)
                act.activation(o_hi[:, b % 2, bass.ds(it, 1), :].rearrange("p a s -> p (a s)"), o_raw[:],
                               ACT.Copy).then_inc(o_hi_done, 1)

            def pair(b, it, last):
                step(b, it, 0, True)
                if b < 2:
                    split_branch(b + 1, it)
                step(b, it, 1, not last)

            split_w(0, 0)
            act.wait_ge(first_loaded, 16)
            for c in range(KO):
                act.activation(o_hi[:, 0, c, :], T.merged[:, c, :], ACT.Copy).then_inc(o_hi_done, 1)
            act.wait_ge(bias_loaded, 16)
            for b in range(3):
                with act.Fori(0, NJ // 2 - (b == 2)) as it:
                    pair(b, it, False)
            pair(2, NJ // 2 - 1, True)

        @block.vector
        def _(dve):
            dve.sem_inc(weighted, 2)

            def split_w(s, n):
                dve.wait_ge(W.hi_ready, n + 1)
                dve.tensor_tensor(W.view(W.lo, s), W.view(W.raw, s), f32(W.view(W.hi, s)),
                                  ALU.subtract).then_inc(W.lo_ready, 1)

            def step(b, it, s, more):
                n = it * 2 + (b * NJ + s)
                if more:
                    split_w(1 - s, n + 1)
                for h in range(2):
                    dve.wait_ge(gated, n * 2 + h + 1)
                    dve.wait_ge(y_done, n * 2 + h + 1 + 2)
                    at = T.merged[:, bass.ds(it * 2 + s, 1), HALF * h:HALF * (h + 1)].rearrange("p a n -> p (a n)")
                    if b == 0:
                        dve.tensor_tensor(at, y_ps[:, h, :], gate[:, h, :], ALU.mult).then_inc(weighted, 1)
                    else:
                        dve.tensor_tensor(term[:, h, :], y_ps[:, h, :], gate[:, h, :], ALU.mult)\
                            .then_inc(weighted, 1)
                        dve.wait_ge(weighted, n * 2 + h + 1 + 2)
                        dve.tensor_tensor(at, at, term[:, h, :], ALU.add).then_inc(summed, 1)

            def split_branch(b, it):
                dve.wait_ge(o_hi_done, it + (b * KO + 1))
                cut = bass.ds(it, 1)
                dve.tensor_tensor(o_lo[:, b % 2, cut, :].rearrange("p a s -> p (a s)"), o_raw[:],
                                  f32(o_hi[:, b % 2, cut, :]).rearrange("p a s -> p (a s)"),
                                  ALU.subtract).then_inc(o_lo_done, 1)

            def pair(b, it, last):
                step(b, it, 0, True)
                if b < 2:
                    split_branch(b + 1, it)
                step(b, it, 1, not last)

            split_w(0, 0)
            for c in range(KO):
                dve.wait_ge(o_hi_done, c + 1)
                dve.tensor_tensor(o_lo[:, 0, c, :], T.merged[:, c, :], f32(o_hi[:, 0, c, :]),
                                  ALU.subtract).then_inc(o_lo_done, 1)
            dve.wait_ge(o_lo_done, KO)
            for b in range(3):
                with dve.Fori(0, NJ // 2 - (b == 2)) as it:
                    pair(b, it, False)
            pair(2, NJ // 2 - 1, True)

        @block.tensor
        def _(pe):
            pe.sem_inc(y_done, 2)

            def step(b, it, s):
                n = it * 2 + (b * NJ + s)
                pe.wait_ge(W.lo_ready, n + 1)
                hi, lo = W.view(W.hi, s), W.view(W.lo, s)
                for h in range(2):
                    at = slice(HALF * h, HALF * (h + 1))
                    pe.wait_ge(weighted, n * 2 + h + 1)
                    for k in range(KD):
                        cut = slice(P * k, P * (k + 1))
                        mm = product(pe, gate_ps[:, h, :], hi[:, cut], lo[:, cut],
                                     T.h_hi[:, k, at], T.h_lo[:, k, at], start=(k == 0), stop=(k == KD - 1))
                    mm.then_inc(gate_done, 1)
                    for k in range(KO):
                        cut = slice(P * (KD + k), P * (KD + k + 1))
                        mm = product(pe, y_ps[:, h, :], hi[:, cut], lo[:, cut],
                                     o_hi[:, b % 2, k, at], o_lo[:, b % 2, k, at], start=(k == 0), stop=(k == KO - 1))
                    mm.then_inc(y_done, 1)

            for b in range(3):
                pe.wait_ge(o_lo_done, KO * (b + 1))
                with pe.Fori(0, NJ // 2) as it:
                    for s in range(2):
                        step(b, it, s)


def output_stage(nc, T):
    with ExitStack() as stack:
        kit = Kit(nc, stack)
        m_hi, m_lo = T.h_hi, T.h_lo
        x1 = T.merged
        groups = [(0, 3), (3, 6), (6, 8)]
        W = Weights(kit, "wout", 3, D, T.w_raw, T.w_hi, T.w_lo)
        acc = kit.ps("acc_ps", [P, 3, 2, HALF])
        turn_ps = kit.ps("out_turn_ps", [P, 2, HALF])
        gains = kit.sb("out_gains", [P, 2, D])
        part = kit.sb("out_part", [P, D])
        normed = kit.sb("out_normed", [P, 2, D])
        junk = kit.sb("out_junk", [P, HALF])
        ssq = kit.sb("out_ssq", [P, NT, 3])
        stat = kit.sb("out_stat", [P, NT, 5])
        g_loaded, x_loaded = kit.sem("out_gains_loaded"), kit.sem("x_loaded")
        m_hi_done, m_lo_done = kit.sem("m_hi_done"), kit.sem("m_lo_done")
        added = kit.sem("out_added")
        squared = kit.sem("out_squared")
        squared_x1 = kit.sem("out_squared_x1")
        meaned = kit.sem("out_meaned")
        rooted, rooted_x1 = kit.sem("out_rooted"), kit.sem("out_rooted_x1")
        parted = kit.sem("out_parted")
        x1_done = kit.sem("x1_done")
        renormed = kit.sem("renormed")
        turned = kit.sem("out_turned")
        h_hi_done, h_lo_done = kit.sem("h2_hi_done"), kit.sem("h2_lo_done")
        slots = [(gi, j) for gi in range(len(groups)) for j in range(KD)]
        group_of = {t: gi for gi, (a, b) in enumerate(groups) for t in range(a, b)}

        def schedule(split_w, first, second, third):
            n = 3
            for gi, (a, b) in enumerate(groups):
                while n < KD * (gi + 1):
                    split_w(n)
                    n += 1
                more = gi + 1 < len(groups)
                for t in range(a, b):
                    first(t)
                    if more:
                        split_w(n)
                        n += 1
                for t in range(a, b):
                    second(t)
                    for _ in range(min(2, KD * (gi + 2) - n) if more else 0):
                        split_w(n)
                        n += 1
                    third(t)

        block = stack.enter_context(nc.Block())

        @block.sync
        def _(sp):
            for n, (_, j) in enumerate(slots):
                if n >= 3:
                    sp.wait_ge(W.lo_ready, n - 2)
                sp.dma_start(W.view(W.raw, n % 3), T.d["w_out"][0, P * j:P * (j + 1), :])\
                    .then_inc(W.loaded[n % 3], 16)
                if n == 2:
                    for i, name in enumerate(("g_mix_post", "g_ffn_pre")):
                        sp.dma_start(gains[:, i, :], T.d[name][0:1, :].to_broadcast([P, D])).then_inc(g_loaded, 16)
                if n == KD - 1:
                    sp.wait_ge(m_lo_done, KD)
                    sp.dma_start(x1[:], T.d["x"][0].rearrange("(t p) n -> p t n", p=P)).then_inc(x_loaded, 16)

        @block.scalar
        def _(act):
            def split_w(n):
                act.wait_ge(W.loaded[n % 3], 16 * (n // 3 + 1))
                if n >= 3:
                    act.wait_ge(added, n - 2)
                act.activation(W.view(W.hi, n % 3), W.view(W.raw, n % 3), ACT.Copy).then_inc(W.hi_ready, 1)

            def square_acc(t):
                gi = group_of[t]
                act.wait_ge(added, KD * (gi + 1))
                for h in range(2):
                    if t + h:
                        act.wait_ge(squared, 2 * t + h)
                    act.activation(junk[:], acc[:, t - groups[gi][0], h, :], ACT.Square,
                                   accum_out=ssq[:, t, h:h + 1]).then_inc(squared, 1)

            def square_x1(t):
                act.wait_ge(x1_done, t + 1)
                if t >= 2:
                    act.wait_ge(turned, 2 * (t - 1))
                act.activation(normed[:, t % 2, :], x1[:, t, :], ACT.Square,
                               accum_out=ssq[:, t, 2:3]).then_inc(squared_x1, 1)

            def split_h(t):
                for b in range(2):
                    act.wait_ge(turned, 2 * t + b + 1)
                    act.activation(T.h2_hi[:, 4 * b:4 * b + 4, P * t:P * (t + 1)],
                                   turn_ps[:, b, :].rearrange("p (c n) -> p c n", c=4),
                                   ACT.Copy).then_inc(h_hi_done, 1)

            for j in range(KD):
                act.activation(m_hi[:, j, :], T.merged[:, j, :], ACT.Copy).then_inc(m_hi_done, 1)
                if j < 3:
                    split_w(j)
            schedule(split_w, square_acc, square_x1, split_h)

        @block.gpsimd
        def _(pool):
            done = 0
            for a, b in groups:
                for t in range(a, b):
                    pool.wait_ge(squared, 2 * t + 2)
                    pool.tensor_tensor(stat[:, t, 0:1], ssq[:, t, 0:1], ssq[:, t, 1:2], ALU.add)\
                        .then_inc(meaned, 1)
                    pool.wait_ge(meaned, done + 1)
                    pool.tensor_scalar(stat[:, t, 1:2], stat[:, t, 0:1], 1.0 / D, EPS, ALU.mult, ALU.add)\
                        .then_inc(meaned, 1)
                    pool.wait_ge(meaned, done + 2)
                    pool.tensor_tensor(stat[:, t, 2:3], stat[:, t, 1:2], T.minus_half[:], ALU.pow)\
                        .then_inc(rooted, 1)
                    done += 2
                for t in range(a, b):
                    pool.wait_ge(squared_x1, t + 1)
                    pool.tensor_scalar(stat[:, t, 3:4], ssq[:, t, 2:3], 1.0 / D, EPS, ALU.mult, ALU.add)\
                        .then_inc(meaned, 1)
                    pool.wait_ge(meaned, done + 1)
                    pool.tensor_tensor(stat[:, t, 4:5], stat[:, t, 3:4], T.minus_half[:], ALU.pow)\
                        .then_inc(rooted_x1, 1)
                    done += 1

        @block.vector
        def _(dve):
            def split_w(n):
                dve.wait_ge(W.hi_ready, n + 1)
                dve.tensor_tensor(W.view(W.lo, n % 3), W.view(W.raw, n % 3), f32(W.view(W.hi, n % 3)),
                                  ALU.subtract).then_inc(W.lo_ready, 1)

            def residual(t):
                gi = group_of[t]
                dve.wait_ge(rooted, t + 1)
                if t >= 1:
                    dve.wait_ge(x1_done, t)
                if t == 0:
                    dve.wait_ge(g_loaded, 32)
                    dve.wait_ge(x_loaded, 16)
                for h in range(2):
                    at = slice(HALF * h, HALF * (h + 1))
                    dve.scalar_tensor_tensor(out=part[:, at], in0=acc[:, t - groups[gi][0], h, :],
                                             scalar=stat[:, t, 2:3], in1=gains[:, 0, at],
                                             op0=ALU.mult, op1=ALU.mult).then_inc(parted, 1)
                dve.wait_ge(parted, 2 * t + 2)
                dve.tensor_tensor(x1[:, t, :], x1[:, t, :], part[:], ALU.add).then_inc(x1_done, 1)

            def renormalise(t):
                dve.wait_ge(rooted_x1, t + 1)
                dve.scalar_tensor_tensor(out=normed[:, t % 2, :], in0=x1[:, t, :], scalar=stat[:, t, 4:5],
                                         in1=gains[:, 1, :], op0=ALU.mult, op1=ALU.mult).then_inc(renormed, 1)

            def split_h(t):
                for b in range(2):
                    dve.wait_ge(h_hi_done, 2 * t + b + 1)
                    cut = (slice(None), slice(4 * b, 4 * b + 4), slice(P * t, P * (t + 1)))
                    dve.tensor_tensor(T.h2_lo[cut], turn_ps[:, b, :].rearrange("p (c n) -> p c n", c=4),
                                      f32(T.h2_hi[cut]), ALU.subtract).then_inc(h_lo_done, 1)

            for j in range(KD):
                dve.wait_ge(m_hi_done, j + 1)
                dve.tensor_tensor(m_lo[:, j, :], T.merged[:, j, :], f32(m_hi[:, j, :]),
                                  ALU.subtract).then_inc(m_lo_done, 1)
                if j < 3:
                    split_w(j)
            schedule(split_w, residual, renormalise, split_h)

        @block.tensor
        def _(pe):
            def turn(t):
                pe.wait_ge(renormed, t + 1)
                for b in range(2):
                    if t >= 1:
                        pe.wait_ge(h_lo_done, 2 * t + b - 1)
                    for c in range(4):
                        mm = pe.transpose(turn_ps[:, b, P * c:P * (c + 1)],
                                          normed[:, t % 2, P * (4 * b + c):P * (4 * b + c + 1)], T.ident[:])
                    mm.then_inc(turned, 1)

            for n, (gi, j) in enumerate(slots):
                a, b = groups[gi]
                pe.wait_ge(W.lo_ready, n + 1)
                if gi == 0:
                    pe.wait_ge(m_lo_done, j + 1)
                if gi >= 1 and j in (3, 5, 7):
                    t = groups[gi - 1][0] + (j - 3) // 2
                    turn(t)
                for t in range(a, b):
                    if j == 0 and gi >= 1:
                        pe.wait_ge(x1_done, groups[gi - 1][0] + t - a + 1)
                    cut = slice(P * t, P * (t + 1))
                    for h in range(2):
                        at = slice(HALF * h, HALF * (h + 1))
                        w_hi, w_lo = W.view(W.hi, n % 3)[:, at], W.view(W.lo, n % 3)[:, at]
                        mm = product(pe, acc[:, t - a, h, :], m_hi[:, j, cut], m_lo[:, j, cut], w_hi, w_lo,
                                     start=(j == 0), stop=(j == KD - 1))
                mm.then_inc(added, 1)
            for t in range(*groups[-1]):
                turn(t)


def ffn_stage(nc, T):
    with ExitStack() as stack:
        kit = Kit(nc, stack)
        x1 = T.merged
        NG = NF // 2
        W = Weights(kit, "wffn", 3, D, T.w_raw, T.w_hi, T.w_lo)
        y = kit.sb("ffn_y", [P, NT, D])
        u = kit.sb("ffn_u", [P, 2, HALF])
        silu = kit.sb("ffn_silu", [P, 2, HALF])
        u_hi, u_lo = (kit.sb("ffn_" + n, [P, 2, S], F32R) for n in ("u_hi", "u_lo"))
        gain = kit.sb("ffn_gain", [P, D])
        final = kit.sb("ffn_final", [P, 2, D])
        junk = kit.sb("ffn_junk", [P, D])
        ssq, mean, rstd = (kit.sb("ffn_" + n, [P, NT]) for n in ("ssq", "mean", "rstd"))
        a_ps, c_ps = kit.ps("a_ps", [P, 2, HALF]), kit.ps("c_ps", [P, 2, HALF])
        out_ps = kit.ps("ffn_out_ps", [P, 4, HALF])
        g_loaded = kit.sem("ffn_gain_loaded")
        zeroed = kit.sem("ffn_zeroed")
        a_done, c_done = kit.sem("a_done"), kit.sem("c_done")
        silued = kit.sem("silued")
        gated = kit.sem("ffn_gated")
        u_hi_done, u_lo_done = kit.sem("u_hi_done"), kit.sem("u_lo_done")
        part_done = kit.sem("part_done")
        added = kit.sem("ffn_added")
        squared, meaned, rooted = kit.sem("ffn_squared"), kit.sem("ffn_meaned"), kit.sem("ffn_rooted")
        scaled, finished = kit.sem("ffn_scaled"), kit.sem("ffn_finished")
        stored = [kit.sem("out_stored0"), kit.sem("out_stored1")]
        w_in = T.d["w_ffn_in"][0].rearrange("(k p) n -> p k n", p=P)
        w_out = T.d["w_ffn_out"][0]
        out = T.d["out"][0].rearrange("(t p) n -> t p n", p=P)
        A0, C0, A1, C1, R0, R1 = range(6)

        block = stack.enter_context(nc.Block())

        @block.sync
        def _(sp):
            def load(g, i, wait):
                if wait is not None:
                    sp.wait_ge(W.lo_ready, wait)
                to = W.view(W.raw, i % 3)
                if i < R0:
                    src = w_in[:, :, bass.ds(g * 2 * P + (P * (i // 2) + D_FF * (i % 2)), P)]
                    sp.dma_start(to.rearrange("p (k n) -> p k n", k=KD), src).then_inc(W.loaded[i % 3], 16)
                else:
                    src = w_out[bass.ds(g * 2 * P + P * (i - R0), P), :]
                    sp.dma_start(to, src).then_inc(W.loaded[i % 3], 16)

            for i in range(6):
                load(0, i, i - 2 if i >= 3 else None)
            sp.dma_start(gain[:], T.d["g_ffn_post"][0:1, :].to_broadcast([P, D])).then_inc(g_loaded, 16)
            with sp.Fori(1, NG) as g:
                for i in range(6):
                    load(g, i, g * 6 + (i - 2))
            for t in range(NT):
                sp.wait_ge(finished, t + 1)
                sp.dma_start(out[t], final[:, t % 2, :]).then_inc(stored[t % 2], 16)
            for s in stored:
                sp.wait_ge(s, 16 * NT // 2)

        @block.scalar
        def _(act):
            def split_w(g, i, sem=None, value=None):
                act.wait_ge(W.loaded[i % 3], g * 32 + (16 * (i // 3) + 16))
                if sem is not None:
                    act.wait_ge(sem, value)
                act.activation(W.view(W.hi, i % 3), W.view(W.raw, i % 3), ACT.Copy).then_inc(W.hi_ready, 1)

            def halves(g, i):
                for h in range(2):
                    n = g * 4 + (2 * i + h)
                    act.wait_ge(a_done, n + 1)
                    act.wait_ge(gated, n + 1)
                    act.activation(silu[:, h, :], a_ps[:, h, :], ACT.Silu).then_inc(silued, 1)
                    act.wait_ge(gated, n + 1 + 2)
                    act.activation(u_hi[:, i, HALF * h:HALF * (h + 1)], u[:, h, :], ACT.Copy)\
                        .then_inc(u_hi_done, 1)

            def body(g, more):
                halves(g, 0)
                split_w(g, C1, a_done, g * 4 + 2)
                split_w(g, R0, c_done, g * 4 + 2 + 2)
                halves(g, 1)
                split_w(g, R1, a_done, g * 4 + 4)
                if more:
                    split_w(g + 1, A0, c_done, g * 4 + 4 + 2)
                    split_w(g + 1, C0, part_done, g * 4 + 4 + 4)
                    split_w(g + 1, A1, part_done, g * 4 + 4 + 4)

            for i in (A0, C0, A1):
                split_w(0, i)
            with act.Fori(0, NG - 1) as g:
                body(g, True)
            body(NG - 1, False)
            for t in range(NT):
                act.wait_ge(added, 16 * (NG - 1) + 4 + 2 * (t + 1))
                if t >= 1:
                    act.wait_ge(squared, t)
                act.activation(junk[:], y[:, t, :], ACT.Square, accum_out=ssq[:, t:t + 1]).then_inc(squared, 1)

        @block.vector
        def _(dve):
            dve.sem_inc(gated, 2)
            dve.sem_inc(added, 4)

            def split_w(g, i):
                dve.wait_ge(W.hi_ready, g * 6 + (i + 1))
                dve.tensor_tensor(W.view(W.lo, i % 3), W.view(W.raw, i % 3), f32(W.view(W.hi, i % 3)),
                                  ALU.subtract).then_inc(W.lo_ready, 1)

            def halves(g, i):
                for h in range(2):
                    n = g * 4 + (2 * i + h)
                    dve.wait_ge(silued, n + 1)
                    dve.wait_ge(c_done, n + 1 + 2)
                    dve.tensor_tensor(u[:, h, :], c_ps[:, h, :], silu[:, h, :], ALU.mult).then_inc(gated, 1)
                    dve.wait_ge(u_hi_done, n + 1)
                    at = slice(HALF * h, HALF * (h + 1))
                    dve.tensor_tensor(u_lo[:, i, at], u[:, h, :], f32(u_hi[:, i, at]),
                                      ALU.subtract).then_inc(u_lo_done, 1)

            def add_parts(g, first, last):
                for n in range(first, last):
                    dve.wait_ge(part_done, g * 4 + (n // 4 + 1 + 4))
                    at = y[:, n // 2, HALF * (n % 2):HALF * (n % 2 + 1)]
                    dve.tensor_tensor(at, out_ps[:, n % 4, :], at, ALU.add).then_inc(added, 1)

            def body(g, more):
                halves(g, 0)
                split_w(g, C1)
                split_w(g, R0)
                halves(g, 1)
                split_w(g, R1)
                if more:
                    split_w(g + 1, A0)
                dve.wait_ge(added, g * 16 + 4)
                add_parts(g, 0, 16)
                if more:
                    split_w(g + 1, C0)
                    split_w(g + 1, A1)

            for i in (A0, C0, A1):
                split_w(0, i)
            dve.wait_ge(zeroed, 1)
            with dve.Fori(0, NG - 1) as g:
                body(g, True)
            body(NG - 1, False)
            dve.wait_ge(g_loaded, 16)
            for t in range(NT):
                dve.wait_ge(rooted, t + 1)
                dve.scalar_tensor_tensor(out=y[:, t, :], in0=y[:, t, :], scalar=rstd[:, t:t + 1],
                                         in1=gain[:], op0=ALU.mult, op1=ALU.mult).then_inc(scaled, 1)
                dve.wait_ge(scaled, t + 1)
                if t >= 2:
                    dve.wait_ge(stored[t % 2], 16 * (t // 2))
                dve.tensor_tensor(final[:, t % 2, :], y[:, t, :], x1[:, t, :], ALU.add).then_inc(finished, 1)

        @block.gpsimd
        def _(pool):
            pool.memset(y[:], 0.0).then_inc(zeroed, 1)
            for t in range(NT):
                pool.wait_ge(squared, t + 1)
                pool.tensor_scalar(mean[:, t:t + 1], ssq[:, t:t + 1], 1.0 / D, EPS, ALU.mult, ALU.add)\
                    .then_inc(meaned, 1)
                pool.wait_ge(meaned, t + 1)
                pool.tensor_tensor(rstd[:, t:t + 1], mean[:, t:t + 1], T.minus_half[:], ALU.pow).then_inc(rooted, 1)

        @block.tensor
        def _(pe):
            pe.sem_inc(c_done, 2)
            pe.sem_inc(part_done, 4)

            def hidden(g, i):
                a, c = (A0, C0) if i == 0 else (A1, C1)
                for h in range(2):
                    at = slice(HALF * h, HALF * (h + 1))
                    pe.wait_ge(gated, g * 4 + (2 * i + h + 1))
                    for ps, slot, done in ((a_ps, a, a_done), (c_ps, c, c_done)):
                        if h == 0:
                            pe.wait_ge(W.lo_ready, g * 6 + (slot + 1))
                        hi, lo = W.view(W.hi, slot % 3), W.view(W.lo, slot % 3)
                        for k in range(KD):
                            cut = slice(P * k, P * (k + 1))
                            mm = product(pe, ps[:, h, :], hi[:, cut], lo[:, cut], T.h2_hi[:, k, at],
                                         T.h2_lo[:, k, at], start=(k == 0), stop=(k == KD - 1))
                        mm.then_inc(done, 1)

            def output(g):
                for quarter in range(4):
                    for i in range(2):
                        slot = R0 + i
                        hi, lo = W.view(W.hi, slot % 3), W.view(W.lo, slot % 3)
                        if quarter == 0:
                            pe.wait_ge(W.lo_ready, g * 6 + (slot + 1))
                            pe.wait_ge(u_lo_done, g * 4 + (2 * i + 2))
                        for n in range(4 * quarter, 4 * quarter + 4):
                            if i == 0:
                                pe.wait_ge(added, g * 16 + (n + 1))
                            cut = slice(P * (n // 2), P * (n // 2 + 1))
                            at = slice(HALF * (n % 2), HALF * (n % 2 + 1))
                            mm = product(pe, out_ps[:, n % 4, :], u_hi[:, i, cut], u_lo[:, i, cut],
                                         hi[:, at], lo[:, at], start=(i == 0), stop=(i == 1))
                    mm.then_inc(part_done, 1)

            with pe.Fori(0, NG) as g:
                for i in range(2):
                    hidden(g, i)
                output(g)


class Shared:
    pass


def build_program(nc, drams):
    T = Shared()
    Kit.sems = []
    T.d = drams
    T.scale = {FOX: HD ** -0.5, SWA: HD ** -0.5, MEM: 128 ** -0.5}
    T.cum_dram = nc.dram_tensor("cum_scratch", (8, S), F32, kind="Internal").ap()
    T.out_dram = [nc.dram_tensor(f"branch_scratch{b}", (4 * P, S), F32, kind="Internal").ap() for b in range(3)]
    with ExitStack() as whole:
        kit = Kit(nc, whole)
        T.ident = kit.sb("ident", [P, P])
        T.minus_half = kit.sb("minus_half", [P, 1])
        T.ident_bf = kit.sb("ident_bf", [P, P], BF16)
        T.masks_bf = kit.sb("masks_bf", [P, 3 * P], BF16)
        T.w_raw = kit.sb("w_raw", [P, 3 * D])
        T.w_hi, T.w_lo = kit.sb("w_hi", [P, 3 * D], F32R), kit.sb("w_lo", [P, 3 * D], F32R)
        with ExitStack() as first:
            kit1 = Kit(nc, first)
            T.h_hi, T.h_lo = (kit1.sb(n, [P, KD, S], F32R) for n in ("h_hi", "h_lo"))
            with ExitStack() as early:
                kit2 = Kit(nc, early)
                T.rope = kit2.sb("rope_sb", [P, 2, S])
                T.sink, T.sink_raw = kit2.sb("sink", [P, 8]), kit2.sb("sink_unscaled", [P, 8])
                T.k1, T.k2 = kit2.sb("swa_k1", [P, 2, S], F32R), kit2.sb("swa_k2", [P, 2, S], F32R)
                T.v = kit2.sb("swa_v", [P, 2, NT, 2, HD], F32R)
                with ExitStack() as memory:
                    kit3 = Kit(nc, memory)
                    T.mk_hi, T.mk_lo = (kit3.sb(n, [P, 4, N_MEM], F32R) for n in ("mk_hi", "mk_lo"))
                    T.mv_hi, T.mv_lo = (kit3.sb(n, [P, 4, 2, P], F32R) for n in ("mv_hi", "mv_lo"))
                    with ExitStack() as raw:
                        kit4 = Kit(nc, raw)
                        T.masks = kit4.sb("masks_sb", [P, 3 * P])
                        T.mem_kv = kit4.sb("mem_kv", [P, 8, N_MEM])
                        normalise_stage(nc, T)
                        shared_stage(nc, T)
                    attention_stage(nc, T, MEM)
                attention_stage(nc, T, SWA)
            attention_stage(nc, T, FOX)
            T.merged = kit.sb("merged", [P, KD, S], side="right")
            Kit.free_semaphores(nc)
            merge_stage(nc, T)
            T.h2_hi, T.h2_lo = (kit.sb(n, [P, KD, S], F32R, side="right") for n in ("h2_hi", "h2_lo"))
            output_stage(nc, T)
        ffn_stage(nc, T)


_INS = ["x", "mem", "g_mix_pre", "g_mix_post", "w_in", "b_fgate", "b_branch", "sinks", "g_mem", "w_mem_kv",
        "w_o_fox", "w_o_swa", "w_o_mem", "w_out", "g_ffn_pre", "g_ffn_post", "w_ffn_in", "w_ffn_out"]


def _constants():
    query, key = np.arange(P)[:, None], np.arange(P)[None, :]
    causal = np.where(key <= query, 0.0, -BIG)
    band_key = np.arange(2 * P)[None, :] - P
    chunk_q, chunk_k = query // 64, band_key // 64
    band = np.where((chunk_k <= chunk_q) & (chunk_k > chunk_q - 2), 0.0, -BIG)
    half = HD // 2
    inv = (np.float32(10000.0) ** (-np.arange(half, dtype=np.float32) / np.float32(half))).astype(np.float32)
    angle = (np.arange(S, dtype=np.float32)[None, :] * inv[:, None]).astype(np.float32)
    cos, sin = np.cos(angle), np.sin(angle)
    rope = np.stack([np.tile(cos, (4, 1)), np.concatenate([-sin, sin, -sin, sin])], axis=1)
    return {"ident": np.eye(P, dtype=np.float32),
            "masks": np.concatenate([causal, band], axis=1).astype(np.float32),
            "rope": rope.astype(np.float32)}


def kernel(**inputs):
    import concourse.bacc as bacc
    from concourse.bass_utils import run_bass_kernel_spmd

    nc = bacc.Bacc("TRN2", target_bir_lowering=False, num_devices=1, dynamic_dma_scratch_size=1024)
    arrays, drams = {}, {}
    given = {name: np.ascontiguousarray(inputs[name]) for name in _INS}
    for name, a in list(given.items()) + list(_constants().items()):
        arrays[f"in_{name}"] = a
        drams[name] = nc.dram_tensor(f"in_{name}", a.shape, mybir.dt.from_np(a.dtype), kind="ExternalInput").ap()
    drams["out"] = nc.dram_tensor("out", (1, S, D), F32, kind="ExternalOutput").ap()
    build_program(nc, drams)
    result = run_bass_kernel_spmd(nc, [arrays], core_ids=[0])
    return result.results[0]["out"]
```

```python
from contextlib import ExitStack

import numpy as np
import concourse.bass as bass
from concourse import mybir

F32, F32R, BF16 = mybir.dt.float32, mybir.dt.float32r, mybir.dt.bfloat16
ALU, ACT, AX = mybir.AluOpType, mybir.ActivationFunctionType, mybir.AxisListType

P = 128
D = 1024
S = 1024
KD = D // P
NT = S // P
HALF = 512
N_MEM = 256
HD = 64
D_FF = 2816
NF = D_FF // P
EPS = 1e-6
BIG = 1.0e30
COL = dict(fq=0, fk=512, fv=1024, flog=1536, sq=1544, sk=2056, sv=2184, mq=2312, glog=2824)
FOX, SWA, MEM = 0, 1, 2


class Kit:

    sems = []

    def __init__(self, nc, stack):
        self.nc, self.stack = nc, stack

    def sb(self, name, shape, dtype=F32, side=None):
        return self.stack.enter_context(self.nc.sbuf_tensor(name, shape, dtype, side=side))

    def ps(self, name, shape, dtype=F32):
        return self.stack.enter_context(self.nc.psum_tensor(name, shape, dtype))

    def sem(self, name):
        made = self.nc.alloc_semaphore(name)
        Kit.sems.append(made)
        return made

    @classmethod
    def free_semaphores(cls, nc):
        nc.clear_and_free_semaphores(cls.sems)
        nc.all_engine_barrier()
        cls.sems = []


def f32(ap):
    return ap.bitcast(F32)


def product(pe, out, a_hi, a_lo, b_hi, b_lo, start, stop):
    pe.matmul(out, a_hi, b_hi, start=start, stop=False)
    pe.matmul(out, a_hi, b_lo, start=False, stop=False)
    return pe.matmul(out, a_lo, b_hi, start=False, stop=stop)


class Weights:

    def __init__(self, kit, name, ring, width, raw, hi, lo):
        self.ring, self.width = ring, width
        self.raw, self.hi, self.lo = raw, hi, lo
        self.loaded = [kit.sem(f"{name}_loaded{i}") for i in range(ring)]
        self.hi_ready = kit.sem(f"{name}_hi_ready")
        self.lo_ready = kit.sem(f"{name}_lo_ready")

    def view(self, tile, slot, a=0, b=None):
        return tile[:, slot * self.width + a:slot * self.width + (self.width if b is None else b)]


class Projection:

    def __init__(self, kit, T, name, nb, turns, col, before=None):
        self.T, self.nb, self.turns, self.col, self.before = T, nb, turns, col, before
        self.groups = nb * 2 * KD
        self.W = Weights(kit, "w" + name, nb, D, T.w_raw, T.w_hi, T.w_lo)
        self.done = kit.sem(name + "_proj_done")
        self.kept = kit.sem(name + "_kept")
        self.rot_loaded = [kit.sem(f"{name}_rot_loaded{b}") for b in range(2 if name == "swa" else 0)]
        self.roped = kit.sem(name + "_roped")
        self.w_in = T.d["w_in"][0].rearrange("(k p) n -> p k n", p=P)

    def last_use(self, turn, b):
        if isinstance(turn, int) and turn == 0:
            had = self.before
            return (had, (had.turns - 1) * had.nb + b + 1) if had and b < had.nb else (None, 0)
        return self, (turn - 1) * self.nb + (b + 1)

    def load(self, sp, turn, b):
        had, n = self.last_use(turn, b)
        if had:
            sp.wait_ge(had.W.lo_ready, n)
        sp.dma_start(self.W.view(self.W.raw, b).rearrange("p (k n) -> p k n", k=KD),
                     self.w_in[:, :, bass.ds(self.col(turn, b), P)]).then_inc(self.W.loaded[b], 16)

    def split_high(self, act, turn, b):
        W = self.W
        act.wait_ge(W.loaded[b], 16 * turn + 16)
        had, n = self.last_use(turn, b)
        if had:
            act.wait_ge(had.done, n * 2)
        act.activation(W.view(W.hi, b), W.view(W.raw, b), ACT.Copy).then_inc(W.hi_ready, 1)

    def split_low(self, dve, turn, b):
        W = self.W
        dve.wait_ge(W.hi_ready, turn * self.nb + b + 1)
        dve.tensor_tensor(W.view(W.lo, b), W.view(W.raw, b), f32(W.view(W.hi, b)),
                          ALU.subtract).then_inc(W.lo_ready, 1)

    def project(self, pe, turn, first, last):
        W, T = self.W, self.T
        if isinstance(turn, int) and turn == 0 and first == 0 < last and self.before:
            had = self.before
            if had.before:
                pe.wait_ge(had.kept, had.turns * 2 * had.nb + 2)
        for n in range(first, last):
            b, half, k = n // (2 * KD), (n // KD) % 2, n % KD
            if n % (2 * KD) == 0:
                pe.wait_ge(W.lo_ready, turn * self.nb + b + 1)
            if k == 0:
                pe.wait_ge(self.kept, turn * (2 * self.nb) + 2 * b + half + 1)
            cut, at = slice(P * k, P * (k + 1)), slice(HALF * half, HALF * (half + 1))
            mm = product(pe, T.proj_ps[:, half, :], W.view(W.hi, b)[:, cut], W.view(W.lo, b)[:, cut],
                         T.h_hi[:, k, at], T.h_lo[:, k, at], start=(k == 0), stop=(k == KD - 1))
            if k == KD - 1:
                mm.then_inc(self.done, 1)

    def keep(self, act, turn, n):
        act.wait_ge(self.done, turn * (2 * self.nb) + n + 1)
        act.activation(self.T.raw[:, n // 2, HALF * (n % 2):HALF * (n % 2 + 1)], self.T.proj_ps[:, n % 2, :],
                       ACT.Copy).then_inc(self.kept, 1)

    def swap_halves(self, sp, turn, b):
        raw, rot = self.T.raw, self.T.rot
        sp.wait_ge(self.kept, (turn * self.nb + b) * 2 + 2 + 2)
        for q in range(4):
            sp.dma_start(rot[32 * q:32 * q + 32, b, :], raw[32 * (q ^ 1):32 * (q ^ 1) + 32, b, :])\
                .then_inc(self.rot_loaded[b], 16)

    def rope(self, pool, turn, b):
        raw, rot = self.T.raw[:, b, :], self.T.rot[:, b, :]
        pool.wait_ge(self.rot_loaded[b], 64 * (turn + 1))
        pool.tensor_tensor(raw, raw, self.T.rope[:, 0, :], ALU.mult).then_inc(self.roped, 1)
        pool.tensor_tensor(rot, rot, self.T.rope[:, 1, :], ALU.mult).then_inc(self.roped, 1)
        pool.wait_ge(self.roped, (turn * self.nb + b) * 3 + 2)
        pool.tensor_tensor(raw, raw, rot, ALU.add).then_inc(self.roped, 1)


def normalise_stage(nc, T):
    with ExitStack() as stack:
        kit = Kit(nc, stack)
        nat = kit.sb("nat", [P, 4, D])
        normed = T.rot
        junk = T.raw[:, 0, :]
        gains = T.out_sb
        ssq = kit.sb("ssq", [P, 10])
        msq = kit.sb("msq", [P, 10])
        rstd = kit.sb("rstd", [P, 10])
        turned_ps = kit.ps("turned_ps", [P, 4, HALF])
        kv_ps = kit.ps("kv_ps", [P, 2, HALF])
        loaded = [kit.sem(f"nat_loaded{i}") for i in range(4)]
        consts_loaded = kit.sem("consts_loaded")
        g_loaded = kit.sem("gains_loaded")
        squared, meaned, rooted, scaled = (kit.sem(n) for n in ("squared", "meaned", "rooted", "scaled"))
        turned, hi_done, lo_done = (kit.sem(n) for n in ("turned", "hi_done", "lo_done"))
        kv_done, kv_kept = kit.sem("kv_done"), kit.sem("kv_kept")
        bf_ready = kit.sem("bf_ready")
        half_set = kit.sem("half_set")
        W = Weights(kit, "wkv", 3, D, T.w_raw, T.w_hi, T.w_lo)
        mem_hi, mem_lo = kit.sb("mem_hi", [P, KD, N_MEM], F32R), kit.sb("mem_lo", [P, KD, N_MEM], F32R)

        tiles = [(T.d["mem"][0, P * t:P * (t + 1), :], 0, mem_hi, mem_lo, t) for t in range(2)]
        tiles += [(T.d["x"][0, P * t:P * (t + 1), :], 1, T.h_hi, T.h_lo, t) for t in range(NT)]
        n_tiles = len(tiles)
        w_kv = T.d["w_mem_kv"][0].rearrange("(k p) n -> p k n", p=P)
        n_kv = 8

        block = stack.enter_context(nc.Block())

        @block.sync
        def _(sp):
            def load_w(n):
                if n >= 3:
                    sp.wait_ge(W.lo_ready, n - 2)
                sp.dma_start(W.view(W.raw, n % 3).rearrange("p (k n) -> p k n", k=KD),
                             w_kv[:, :, P * n:P * (n + 1)]).then_inc(W.loaded[n % 3], 16)

            for t, (src, *_) in enumerate(tiles):
                if t >= 4:
                    sp.wait_ge(scaled, t - 3)
                sp.dma_start(nat[:, t % 4, :], src).then_inc(loaded[t % 4], 16)
                if t == 0:
                    sp.dma_start(gains[:, 0, :], T.d["g_mem"][0:1, :].to_broadcast([P, D])).then_inc(g_loaded, 16)
                    sp.dma_start(T.ident[:], T.d["ident"]).then_inc(consts_loaded, 16)
                if t == 1:
                    sp.dma_start(gains[:, 1, :], T.d["g_mix_pre"][0:1, :].to_broadcast([P, D])).then_inc(g_loaded, 16)
                if t < n_kv:
                    load_w(t)
            sp.dma_start(T.masks[:], T.d["masks"]).then_inc(consts_loaded, 16)

        @block.scalar
        def _(act):
            def square(t):
                act.wait_ge(loaded[t % 4], 16 * (t // 4 + 1))
                if t >= 1:
                    act.wait_ge(squared, t)
                act.activation(junk[:], nat[:, t % 4, :], ACT.Square,
                               accum_out=ssq[:, t:t + 1]).then_inc(squared, 1)

            def split_w(n):
                act.wait_ge(W.loaded[n % 3], 16 * (n // 3 + 1))
                if n >= 3:
                    act.wait_ge(kv_done, n - 2)
                act.activation(W.view(W.hi, n % 3), W.view(W.raw, n % 3), ACT.Copy).then_inc(W.hi_ready, 1)

            def keep_kv(n):
                act.wait_ge(kv_done, n + 1)
                act.activation(T.mem_kv[:, n, :], kv_ps[:, n % 2, 0:N_MEM], ACT.Copy).then_inc(kv_kept, 1)

            square(0)
            square(1)
            for t, (_, _, hi, _, at) in enumerate(tiles):
                if t < n_kv:
                    split_w(t)
                if t + 2 < n_tiles:
                    square(t + 2)
                for b in range(2):
                    act.wait_ge(turned, 2 * t + b + 1)
                    act.activation(hi[:, 4 * b:4 * b + 4, P * at:P * (at + 1)],
                                   turned_ps[:, (2 * t + b) % 4, :].rearrange("p (c n) -> p c n", c=4),
                                   ACT.Copy).then_inc(hi_done, 1)
                if t >= 2:
                    keep_kv(t - 2)

        @block.gpsimd
        def _(pool):
            pool.memset(T.minus_half[:], -0.5).then_inc(half_set, 1)
            pool.wait_ge(half_set, 1)
            for t in range(n_tiles):
                pool.wait_ge(squared, t + 1)
                pool.tensor_scalar(msq[:, t:t + 1], ssq[:, t:t + 1], 1.0 / D, EPS,
                                   ALU.mult, ALU.add).then_inc(meaned, 1)
                pool.wait_ge(meaned, t + 1)
                pool.tensor_tensor(rstd[:, t:t + 1], msq[:, t:t + 1], T.minus_half[:], ALU.pow).then_inc(rooted, 1)

        @block.vector
        def _(dve):
            def scale(t):
                dve.wait_ge(rooted, t + 1)
                if t >= 2:
                    dve.wait_ge(turned, 2 * (t - 1))
                dve.wait_ge(g_loaded, 32)
                dve.scalar_tensor_tensor(out=normed[:, t % 2, :], in0=nat[:, t % 4, :],
                                         scalar=rstd[:, t:t + 1], in1=gains[:, tiles[t][1], :],
                                         op0=ALU.mult, op1=ALU.mult).then_inc(scaled, 1)

            scale(0)
            for t, (_, _, hi, lo, at) in enumerate(tiles):
                if t < n_kv:
                    dve.wait_ge(W.hi_ready, t + 1)
                    dve.tensor_tensor(W.view(W.lo, t % 3), W.view(W.raw, t % 3), f32(W.view(W.hi, t % 3)),
                                      ALU.subtract).then_inc(W.lo_ready, 1)
                if t + 1 < n_tiles:
                    scale(t + 1)
                for b in range(2):
                    dve.wait_ge(hi_done, 2 * t + b + 1)
                    cut = (slice(None), slice(4 * b, 4 * b + 4), slice(P * at, P * (at + 1)))
                    dve.tensor_tensor(lo[cut],
                                      turned_ps[:, (2 * t + b) % 4, :].rearrange("p (c n) -> p c n", c=4),
                                      f32(hi[cut]), ALU.subtract).then_inc(lo_done, 1)
            dve.wait_ge(consts_loaded, 32)
            dve.tensor_copy(T.ident_bf[:], T.ident[:]).then_inc(bf_ready, 1)
            dve.tensor_copy(T.masks_bf[:], T.masks[:]).then_inc(bf_ready, 1)

        @block.tensor
        def _(pe):
            def turn(t):
                pe.wait_ge(scaled, t + 1)
                for b in range(2):
                    n = 2 * t + b
                    if n >= 4:
                        pe.wait_ge(lo_done, n - 3)
                    for c in range(4):
                        mm = pe.transpose(turned_ps[:, n % 4, P * c:P * (c + 1)],
                                          normed[:, t % 2, P * (4 * b + c):P * (4 * b + c + 1)], T.ident[:])
                    mm.then_inc(turned, 1)

            def project_kv(n):
                pe.wait_ge(W.lo_ready, n + 1)
                if n >= 2:
                    pe.wait_ge(kv_kept, n - 1)
                for k in range(KD):
                    cut = slice(P * k, P * (k + 1))
                    mm = product(pe, kv_ps[:, n % 2, 0:N_MEM],
                                 W.view(W.hi, n % 3)[:, cut], W.view(W.lo, n % 3)[:, cut],
                                 mem_hi[:, k, :], mem_lo[:, k, :], start=(k == 0), stop=(k == KD - 1))
                mm.then_inc(kv_done, 1)

            pe.wait_ge(consts_loaded, 16)
            for t in range(n_tiles):
                turn(t)
                if t >= 2:
                    if t == 2:
                        pe.wait_ge(lo_done, 4)
                    project_kv(t - 2)


def shared_stage(nc, T):
    with ExitStack() as stack:
        kit = Kit(nc, stack)
        blocks = [COL["flog"], COL["sk"], COL["sv"]]
        nb = len(blocks)
        mine = Projection(kit, T, "sh", nb, 1, lambda turn, b: blocks[b])
        W, done = mine.W, mine.done
        mq = T.projection[MEM] = Projection(kit, T, "mem", 2, 2, lambda turn, b: COL["mq"] + (2 * turn + b) * P, mine)
        ps = kit.ps("shared_ps", [P, 2, 2, HALF])
        turn_ps = kit.ps("shared_turn_ps", [P, 2, HALF])
        nh = 8
        z, az, ez, sp_, lf, ones, cum, cum8 = (kit.sb(n, [nh, S]) for n in (
            "z", "abs_z", "exp_z", "softplus", "log_forget", "ones_row", "cum", "cum_scaled"))
        bias = kit.sb("forget_bias", [nh, 1])
        raw = T.rot
        rot = T.out_sb[:, 0, :]
        small_loaded = kit.sem("small_loaded")
        gate_act, gate_dve = kit.sem("gate_act"), kit.sem("gate_dve")
        cum_stored = kit.sem("cum_stored")
        kept = kit.sem("shared_kept")
        rot_loaded, roped = kit.sem("shared_rot_loaded"), kit.sem("shared_roped")
        mem_hi_done, mem_done = kit.sem("mem_hi_done"), kit.sem("mem_split_done")
        k_hi, k_done = kit.sem("swa_k_hi"), kit.sem("swa_k_done")
        turned, v_hi, v_done = kit.sem("shared_turned"), kit.sem("shared_v_hi"), kit.sem("shared_v_done")

        block = stack.enter_context(nc.Block())

        @block.sync
        def _(sp):
            for n in range(nb):
                mine.load(sp, 0, n)
            sp.dma_start(bias[:], T.d["b_fgate"][0:1, :].rearrange("a h -> h a")).then_inc(small_loaded, 16)
            sp.dma_start(T.rope[:], T.d["rope"]).then_inc(small_loaded, 16)
            sp.dma_start(T.sink[:], T.d["sinks"][0:1, :].to_broadcast([P, nh])).then_inc(small_loaded, 16)
            for n in range(2):
                mq.load(sp, 0, n)
            sp.wait_ge(kept, 2)
            for q in range(4):
                sp.dma_start(rot[32 * q:32 * q + 32, :], raw[32 * (q ^ 1):32 * (q ^ 1) + 32, 0, :])\
                    .then_inc(rot_loaded, 16)
            sp.wait_ge(gate_dve, 5)
            sp.dma_start(T.cum_dram, cum8[:]).then_inc(cum_stored, 16)
            for n in range(2):
                mq.load(sp, 1, n)
            sp.wait_ge(cum_stored, 16)

        @block.scalar
        def _(act):
            act.sem_inc(mq.kept, 2)
            for n in range(nb):
                mine.split_high(act, 0, n)
            act.activation(T.mk_hi[:], T.mem_kv[:, 0:4, :], ACT.Copy).then_inc(mem_hi_done, 1)
            for b in range(2):
                act.wait_ge(turned, b + 1)
                act.activation(T.mv_hi[:, 2 * b:2 * b + 2, :, :],
                               turn_ps[:, b, :].rearrange("p (h t d) -> p h t d", h=2, t=2),
                               ACT.Copy).then_inc(mem_hi_done, 1)
            act.wait_ge(done, 2)
            act.wait_ge(small_loaded, 48)
            zp = ps[0:nh, 0, :, :].rearrange("p a n -> p (a n)")
            act.activation(z[:], zp, ACT.Identity, bias=bias[:, 0:1]).then_inc(gate_act, 1)
            act.activation(az[:], zp, ACT.Abs, bias=bias[:, 0:1]).then_inc(gate_act, 1)
            act.wait_ge(gate_act, 2)
            act.activation(ez[:], az[:], ACT.Exp, scale=-1.0).then_inc(gate_act, 1)
            act.wait_ge(gate_act, 3)
            act.activation(sp_[:], ez[:], ACT.Ln, bias=1.0).then_inc(gate_act, 1)
            mq.split_high(act, 0, 0)
            for n in range(2):
                for h in range(2):
                    act.wait_ge(done, 2 * (n + 1) + h + 1)
                    act.activation(raw[:, n, HALF * h:HALF * (h + 1)], ps[:, 1 - n, h, :],
                                   ACT.Copy).then_inc(kept, 1)
                if n == 0:
                    mq.split_high(act, 0, 1)
            act.wait_ge(roped, 3)
            for kv in range(2):
                for half in range(2):
                    act.activation(T.k1[64 * half:64 * half + 64, kv, :], raw[64 * kv:64 * kv + 64, 0, :],
                                   ACT.Copy).then_inc(k_hi, 1)
            for b in range(2):
                act.wait_ge(turned, 2 + b + 1)
                act.activation(T.v[:, :, 4 * b:4 * b + 4, 0, :],
                               turn_ps[:, b, :].rearrange("p (t h d) -> p h t d", t=4, h=2),
                               ACT.Copy).then_inc(v_hi, 1)
            for n in range(4):
                mq.keep(act, 0, n)

        @block.vector
        def _(dve):
            dve.memset(ones[:], 1.0).then_inc(gate_dve, 1)
            for n in range(nb):
                mine.split_low(dve, 0, n)
            dve.wait_ge(mem_hi_done, 1)
            dve.tensor_tensor(T.mk_lo[:], T.mem_kv[:, 0:4, :], f32(T.mk_hi[:]), ALU.subtract).then_inc(mem_done, 1)
            for b in range(2):
                dve.wait_ge(mem_hi_done, b + 2)
                dve.tensor_tensor(T.mv_lo[:, 2 * b:2 * b + 2, :, :],
                                  turn_ps[:, b, :].rearrange("p (h t d) -> p h t d", h=2, t=2),
                                  f32(T.mv_hi[:, 2 * b:2 * b + 2, :, :]), ALU.subtract).then_inc(mem_done, 1)
            dve.wait_ge(small_loaded, 48)
            dve.tensor_scalar(T.sink_raw[:], T.sink[:], 1.0 / T.scale[SWA], None, ALU.mult).then_inc(mem_done, 1)
            dve.wait_ge(gate_act, 4)
            dve.scalar_tensor_tensor(out=lf[:], in0=z[:], scalar=0.0, in1=sp_[:],
                                     op0=ALU.min, op1=ALU.subtract).then_inc(gate_dve, 1)
            dve.wait_ge(gate_dve, 2)
            dve.tensor_tensor_scan(cum[:], ones[:], lf[:], 0.0, ALU.mult, ALU.add).then_inc(gate_dve, 1)
            dve.wait_ge(gate_dve, 3)
            dve.tensor_scalar(cum8[:], cum[:], -1.0 / T.scale[FOX], None, ALU.mult).then_inc(gate_dve, 2)
            mq.split_low(dve, 0, 0)
            mq.split_low(dve, 0, 1)
            dve.wait_ge(rot_loaded, 64)
            dve.tensor_tensor(raw[:, 0, :], raw[:, 0, :], T.rope[:, 0, :], ALU.mult).then_inc(roped, 1)
            dve.tensor_tensor(rot[:], rot[:], T.rope[:, 1, :], ALU.mult).then_inc(roped, 1)
            dve.wait_ge(roped, 2)
            dve.tensor_tensor(raw[:, 0, :], raw[:, 0, :], rot[:], ALU.add).then_inc(roped, 1)
            for kv in range(2):
                dve.wait_ge(k_hi, 2 * kv + 2)
                rows = slice(64 * kv, 64 * kv + 64)
                for half in range(2):
                    dve.tensor_tensor(T.k2[64 * half:64 * half + 64, kv, :], raw[rows, 0, :],
                                      f32(T.k1[rows, kv, :]), ALU.subtract).then_inc(k_done, 1)
            for b in range(2):
                dve.wait_ge(v_hi, b + 1)
                dve.tensor_tensor(T.v[:, :, 4 * b:4 * b + 4, 1, :],
                                  turn_ps[:, b, :].rearrange("p (t h d) -> p h t d", t=4, h=2),
                                  f32(T.v[:, :, 4 * b:4 * b + 4, 0, :]), ALU.subtract).then_inc(v_done, 1)

        @block.tensor
        def _(pe):
            for b in range(2):
                for h in range(2):
                    for t in range(2):
                        at = P * (2 * h + t)
                        mm = pe.transpose(turn_ps[:, b, at:at + P],
                                          T.mem_kv[:, 4 + 2 * b + h, P * t:P * (t + 1)], T.ident[:])
                mm.then_inc(turned, 1)
            for n in range(nb):
                pe.wait_ge(W.lo_ready, n + 1)
                if n == 2:
                    pe.wait_ge(gate_act, 2)
                for h in range(2):
                    for k in range(KD):
                        cut = slice(P * k, P * (k + 1))
                        at = slice(HALF * h, HALF * (h + 1))
                        mm = product(pe, ps[:, n % 2, h, :], W.view(W.hi, n)[:, cut], W.view(W.lo, n)[:, cut],
                                     T.h_hi[:, k, at], T.h_lo[:, k, at], start=(k == 0), stop=(k == KD - 1))
                    mm.then_inc(done, 1)
            mq.project(pe, 0, 0, KD // 2)
            pe.wait_ge(kept, 4)
            pe.wait_ge(mem_done, 3)
            for b in range(2):
                for t in range(4):
                    at = P * (4 * b + t)
                    mm = pe.transpose(turn_ps[:, b, P * t:P * (t + 1)], raw[:, 1, at:at + P], T.ident[:])
                mm.then_inc(turned, 1)
            mq.project(pe, 0, KD // 2, mq.groups)


START = {FOX: 3, SWA: 2, MEM: 2}


def attention_stage(nc, T, branch):
    name = ("fox", "swa", "mem")[branch]
    scale = T.scale[branch]
    turns = {FOX: 4, SWA: 2, MEM: 2}[branch]
    nb = {FOX: 3, SWA: 2, MEM: 2}[branch]
    heads = {FOX: 2, SWA: 4, MEM: 2}[branch]
    chunks = {FOX: 1, SWA: 2, MEM: 2}[branch]
    units = [(a, g) for a in range(heads) for g in range(NT // 2)]
    NU = len(units)
    NQ = 2 * NU

    def keys(i):
        return {FOX: (0, i + 1), SWA: (max(i - 1, 0), i + 1), MEM: (0, 2)}[branch]

    def key_packs(g):
        out, packs = [], [[]]
        for j in range(keys(2 * g)[0], keys(2 * g + 1)[1]):
            sees = [keys(2 * g + q)[0] <= j < keys(2 * g + q)[1] for q in range(2)]
            out.append((j, 0 if sees[0] else P, 2 * P if sees[1] else P))
        for j, a, b in sorted(out, key=lambda x: x[2] - x[1] < 2 * P):
            used = packs[-1][-1][3] + packs[-1][-1][2] - packs[-1][-1][1] if packs[-1] else 0
            if used + b - a > HALF:
                packs.append([])
                used = 0
            packs[-1].append((j, a, b, used))
        return packs

    packs = [key_packs(g) for _, g in units]
    first_pack = [sum(len(x) for x in packs[:u]) for u in range(NU + 1)]
    NS = first_pack[NU]
    width_of = lambda pack: pack[-1][3] + pack[-1][2] - pack[-1][1]
    widths = [[P * (keys(2 * g + q)[1] - keys(2 * g + q)[0]) for q in range(2)] for _, g in units]
    if branch == FOX:
        pieces = [[(q, c, min(HALF, w[q] - c), n, 0) for n, (q, c) in
                   enumerate((q, c) for q in range(2) for c in range(0, w[q], HALF))] for w in widths]
    else:
        pieces = [[(q, 0, w[q], 0, 2 * P * q) for q in range(2)] for w in widths]
    banks_of = [x[-1][3] + 1 for x in pieces]
    maxima_of = [len(x) if branch == FOX or w[0] != w[1] else 1 for x, w in zip(pieces, widths)]
    first_bank = [sum(banks_of[:n]) for n in range(NU + 1)]
    first_max = [sum(maxima_of[:n]) for n in range(NU + 1)]
    NB, NM = first_bank[NU], first_max[NU]
    RS = 3
    STEPS = NU + 4
    PROBS = 3
    bank = lambda it, n: (n if branch == FOX else it * NB + n) % RS
    unit_of_chunk = NU // chunks

    places, start_groups = 2 * (NU + 2), START[branch]

    def plan(n_blocks):
        left = n_blocks * 2 * KD - start_groups
        fill_at = [start_groups + (left * p) // places for p in range(places + 1)]
        split_before = {b: max(0, next(t for t in range(STEPS) if fill_at[2 * t + 2] > 2 * KD * b) - 2)
                        for b in range(n_blocks)}
        return fill_at, split_before

    def halves_by(fill_at, t):
        return fill_at[min(2 * t, places)] // KD

    step_with = lambda n: next(t for t in range(STEPS) if halves_by(plan(nb)[0], t) >= n)
    early_at = {FOX: step_with(4), SWA: max(step_with(2) + 5, NU // 2), MEM: max(step_with(2), NU // 2)}[branch]
    late_at = {FOX: 0, SWA: 6, MEM: 1}[branch]

    with ExitStack() as stack:
        kit = Kit(nc, stack)
        own = T.projection[branch]
        kept, raw, roped = own.kept, T.raw, own.roped
        coming = None
        if branch == MEM:
            coming = T.projection[SWA] = Projection(kit, T, "swa", 2, 2,
                                                    lambda turn, b: COL["sq"] + (2 * turn + b) * P, own)
        if branch == SWA:
            coming = T.projection[FOX] = Projection(
                kit, T, "fox", 3, 4, lambda turn, b: turn * P + (COL["fq"], COL["fk"], COL["fv"])[b], own)
        prob = kit.sb(name + "_prob", [P, PROBS, 2, S if branch == FOX else 2 * P])
        n_packs = max(len(x) for x in packs)
        pt_hi = kit.sb(name + "_pt_hi", [P, 2, n_packs, HALF], F32R)
        pt_lo = kit.sb(name + "_pt_lo", [P, 2, n_packs, HALF], F32R)
        out_sb = T.out_sb
        tmp = kit.sb(name + "_tmp", [64, 2, 2 * P]) if branch != MEM else None
        neg, den, den2, inv, esink = (kit.sb(f"{name}_{n}", [P, 2, 2]) for n in
                                      ("neg", "den", "den2", "inv", "esink"))
        top = kit.sb(name + "_top", [P, 2, 2, 2])
        top2 = kit.sb(name + "_top2", [P, 2, 2])
        if branch == MEM:
            q_hi, q_lo = (kit.sb("mem_" + n, [P, heads, S], F32R) for n in ("q_hi", "q_lo"))
            k_hi, k_lo, v_hi, v_lo = T.mk_hi, T.mk_lo, T.mv_hi, T.mv_lo
        else:
            q_both = kit.sb(name + "_q", [P, heads, S], F32R)
        if branch == SWA:
            k1, k2, v = T.k1, T.k2, T.v
        if branch == FOX:
            k1 = kit.sb("fox_k1", [P, 2, S], F32R)
            k2 = kit.sb("fox_k2", [P, S], F32R)
            v = kit.sb("fox_v", [P, 2, NT, 2, HD], F32R)
            cum_b = kit.sb("fox_cum", [P, 2, S])
        score_ps = kit.ps(name + "_score_ps", [P, RS, HALF])
        turn_ps = kit.ps(name + "_turn_ps", [P, 2, HALF])
        out_ps = kit.ps(name + "_out_ps", [P, HALF])

        act_unpacked = kit.sem(name + "_act_unpacked")
        low_unpacked = kit.sem(name + "_low_unpacked")
        v_hi_done = kit.sem(name + "_v_hi_done")
        v_lo_done = kit.sem(name + "_v_lo_done")
        v_turned = kit.sem(name + "_v_turned")
        scored = kit.sem(name + "_scored")
        maxed = kit.sem(name + "_maxed")
        topped = kit.sem(name + "_topped")
        negated = kit.sem(name + "_negated")
        exped = kit.sem(name + "_exped")
        sunk = kit.sem(name + "_sunk")
        summed = kit.sem(name + "_summed")
        inverted = kit.sem(name + "_inverted")
        normed = kit.sem(name + "_normed")
        turned = kit.sem(name + "_turned")
        pt_hi_done = kit.sem(name + "_pt_hi_done")
        pt_lo_done = kit.sem(name + "_pt_lo_done")
        pv_done = kit.sem(name + "_pv_done")
        lower_kept = kit.sem(name + "_lower_kept")
        out_done = kit.sem(name + "_out_done")
        stored = [kit.sem(f"{name}_stored{c}") for c in range(chunks)]
        cum_loaded = [kit.sem(f"{name}_cum_loaded{a}") for a in range(2)]
        waited = kit.sem(name + "_waited")
        kept_seen = kit.sem(name + "_kept_seen")
        ACT_EARLY, LOW_EARLY = {FOX: (2, 3), SWA: (2, 2), MEM: (1, 1)}[branch]
        ACT_U, LOW_U = 2 * ACT_EARLY, 2 * LOW_EARLY
        out_dram = T.out_dram[branch]

        block = stack.enter_context(nc.Block())

        def over_turns(engine, body):
            if turns > 2:
                with engine.Fori(0, turns - 1) as it:
                    body(it, own, it + 1)
            else:
                for it in range(turns - 1):
                    body(it, own, it + 1)
            body(turns - 1, coming, 0)

        @block.sync
        def _(sp):
            for c in range(chunks):
                sp.sem_inc(stored[c], 1)

            def load_cum(turn, a, wait):
                sp.wait_ge(maxed, wait)
                sp.dma_start(cum_b[:, a, :], T.cum_dram[bass.ds(turn * 2 + a, 1), :].to_broadcast([P, S]))\
                    .then_inc(cum_loaded[a], 16)

            def body(it, nxt, turn, later, later_turn):
                if branch == FOX:
                    load_cum(it, 1, it * NM + RS)
                if branch == SWA:
                    own.swap_halves(sp, it, 1)
                for b in range(later.nb if later else 0):
                    later.load(sp, later_turn, b)
                    if b == 1 and nxt.rot_loaded:
                        nxt.swap_halves(sp, turn, 0)
                if branch == FOX and nxt:
                    load_cum(turn, 0, it * NM + first_max[NU // 2] + RS)
                for c in range(chunks):
                    sp.wait_ge(out_done, it * NU + (c + 1) * unit_of_chunk + 1)
                    sp.dma_start(out_dram[bass.ds(P * (it * chunks + c), P), :], out_sb[:, c, :])\
                        .then_inc(stored[c], 16)

            if branch == FOX:
                load_cum(0, 0, RS)
            if turns > 2:
                with sp.Fori(0, turns - 2) as it:
                    body(it, own, it + 1, own, it + 2)
            body(turns - 2, own, turns - 1, coming, 0)
            body(turns - 1, coming, 0, coming, 1)
            if branch == FOX:
                for store in [(stored[0], 16 * turns + 1), *T.stores]:
                    sp.wait_ge(*store)

        @block.scalar
        def _(act):
            if coming:
                act.sem_inc(coming.kept, 2)
            act.sem_inc(exped, 2 * RS)

            def unpack(it, c):
                if c == 1:
                    act.wait_ge(scored, it * NB + 1)
                rows, swapped = slice(64 * c, 64 * c + 64), slice(64 - 64 * c, P - 64 * c)
                if branch == FOX:
                    act.wait_ge(kept, it * 2 * nb + 4 + 2)
                    act.activation(q_both[rows, c, :], raw[rows, 0, :], ACT.Copy).then_inc(act_unpacked, 1)
                    act.activation(k1[swapped, c, :], raw[rows, 1, :], ACT.Copy).then_inc(act_unpacked, 1)
                if branch == SWA:
                    act.wait_ge(roped, (it * nb + c + 1) * 3)
                    for h in range(2):
                        act.activation(q_both[64 * h:64 * h + 64, 2 * c + h, :], raw[64 * h:64 * h + 64, c, :],
                                       ACT.Copy).then_inc(act_unpacked, 1)
                if branch == MEM:
                    act.wait_ge(kept, (it * nb + c) * 2 + 2 + 2)
                    act.activation(q_hi[:, c, :], raw[:, c, :], ACT.Copy).then_inc(act_unpacked, 1)

            def unpack_values(it):
                act.wait_ge(pv_done, it * NU + 1)
                for b in range(2):
                    act.wait_ge(v_turned, it * 2 + b + 1)
                    act.activation(v[:, :, 4 * b:4 * b + 4, 0, :],
                                   turn_ps[:, b, :].rearrange("p (t h d) -> p h t d", t=4, h=2),
                                   ACT.Copy).then_inc(v_hi_done, 1)

            def exp(it, u):
                act.wait_ge(negated, it * NU + u + 1)
                for q in range(2):
                    i = 2 * units[u][1] + q
                    nk = P * (keys(i)[1] - keys(i)[0])
                    p = prob[:, u % PROBS, q, 0:nk]
                    n, c = bank(it, first_bank[u]), 2 * P * q
                    act.activation(p, p if branch == FOX else score_ps[:, n, c:c + nk], ACT.Exp,
                                   bias=neg[:, u % 2, q:q + 1], scale=scale,
                                   accum_out=den[:, u % 2, q:q + 1]).then_inc(exped, 1)
                if branch == SWA:
                    head = heads * it + units[u][0]
                    act.activation(esink[:, u % 2, :], neg[:, u % 2, :], ACT.Exp,
                                   bias=T.sink[:, head:head + 1]).then_inc(sunk, 1)

            def split_hi(it, u):
                for s, pack in enumerate(packs[u]):
                    n, w = first_pack[u] + s, width_of(pack)
                    act.wait_ge(turned, it * NS + n + 1)
                    act.activation(pt_hi[:, u % 2, s, 0:w], turn_ps[:, n % 2, 0:w], ACT.Copy).then_inc(pt_hi_done, 1)

            def keep_lower(it, u):
                if branch != MEM:
                    act.wait_ge(pv_done, it * NU + u + 2)
                    act.activation(tmp[:, u % 2, :], out_ps[64:P, 0:2 * P], ACT.Copy).then_inc(lower_kept, 1)

            def body(it, nxt, turn):
                fill_at, split_before = plan(nxt.nb) if nxt else (None, None)
                kept_halves = 0
                for t in range(STEPS):
                    if t >= 4:
                        keep_lower(it, t - 4)
                    if nxt:
                        for b in range(nxt.nb):
                            if split_before[b] == t:
                                nxt.split_high(act, turn, b)
                    if 2 <= t < NU + 2:
                        split_hi(it, t - 2)
                    if t < NU:
                        exp(it, t)
                    if branch == FOX and t == 0:
                        unpack_values(it)
                    if t == late_at:
                        unpack(it, 1)
                    if nxt:
                        while kept_halves < halves_by(fill_at, t):
                            if kept_halves == 0:
                                act.wait_ge(low_unpacked, it * LOW_U + (LOW_U if branch == FOX else LOW_EARLY))
                            if kept_halves == 2:
                                act.wait_ge(low_unpacked, it * LOW_U + LOW_U)
                            nxt.keep(act, turn, kept_halves)
                            kept_halves += 1
                        if t == early_at and nxt == own:
                            unpack(turn, 0)

            unpack(0, 0)
            over_turns(act, body)

        def unpack_low(engine, it, c):
            def low(out, whole, high):
                engine.tensor_tensor(out, whole, f32(high), ALU.subtract).then_inc(low_unpacked, 1)

            rows, swapped = slice(64 * c, 64 * c + 64), slice(64 - 64 * c, P - 64 * c)
            if c == 1:
                engine.wait_ge(scored, it * NB + 1)
                engine.wait_ge(low_unpacked, it * LOW_U + LOW_EARLY)
            if branch == FOX:
                n = it * LOW_U + LOW_EARLY * c
                engine.wait_ge(kept, it * 2 * nb + 4 + 2)
                engine.sem_inc(kept_seen, 1)
                engine.tensor_copy(k1[rows, c, :], raw[rows, 1, :]).then_inc(low_unpacked, 1)
                engine.wait_ge(act_unpacked, it * ACT_U + 2 * c + 1)
                low(q_both[swapped, c, :], raw[rows, 0, :], q_both[rows, c, :])
                engine.wait_ge(low_unpacked, n + 1)
                low(k2[rows, :], raw[rows, 1, :], k1[rows, c, :])
            if branch == SWA:
                for h in range(2):
                    mine, other = slice(64 * h, 64 * h + 64), slice(64 - 64 * h, P - 64 * h)
                    engine.wait_ge(act_unpacked, it * ACT_U + 2 * c + h + 1)
                    low(q_both[other, 2 * c + h, :], raw[mine, c, :], q_both[mine, 2 * c + h, :])
            if branch == MEM:
                engine.wait_ge(act_unpacked, it * ACT_U + c + 1)
                low(q_lo[:, c, :], raw[:, c, :], q_hi[:, c, :])

        @block.vector
        def _(dve):
            dve.sem_inc(maxed, RS)
            dve.sem_inc(pt_lo_done, 2)
            dve.sem_inc(out_done, 1)

            def unpack_values(it):
                for b in range(2):
                    dve.wait_ge(v_hi_done, it * 2 + b + 1)
                    dve.tensor_tensor(v[:, :, 4 * b:4 * b + 4, 1, :],
                                      turn_ps[:, b, :].rearrange("p (t h d) -> p h t d", t=4, h=2),
                                      f32(v[:, :, 4 * b:4 * b + 4, 0, :]), ALU.subtract).then_inc(v_lo_done, 1)

            def maxima(it, u):
                a, g = units[u]
                tops = top[:, u % 2, :, 0]
                if branch == FOX:
                    if g == 0:
                        dve.wait_ge(cum_loaded[a], 16 * it + 16)
                    for n, (q, c, w, b, _) in enumerate(pieces[u]):
                        dve.wait_ge(scored, it * NB + first_bank[u] + n + 2)
                        dve.sem_inc(waited, 1)
                        dve.tensor_tensor_reduce(prob[:, u % PROBS, q, c:c + w],
                                                 score_ps[:, bank(it, first_bank[u] + b), 0:w],
                                                 cum_b[:, a, c:c + w], 1.0, -3.0e38, ALU.add, ALU.max,
                                                 top[:, u % 2, q, c // HALF:c // HALF + 1]).then_inc(maxed, 1)
                else:
                    dve.wait_ge(scored, it * NB + u + 2)
                    ps = score_ps[:, bank(it, u), :].rearrange("p (q n) -> p q n", q=2)
                    if maxima_of[u] == 1:
                        dve.reduce_max(tops, ps, AX.X).then_inc(maxed, 1)
                    else:
                        for q in range(2):
                            dve.reduce_max(top[:, u % 2, q, 0:1], ps[:, q, 0:widths[u][q]], AX.X).then_inc(maxed, 1)
                dve.wait_ge(maxed, it * NM + first_max[u + 1] + RS)
                if widths[u][0] > HALF:
                    dve.tensor_tensor(top2[:, u % 2, :], top[:, u % 2, :, 0], top[:, u % 2, :, 1],
                                      ALU.max).then_inc(topped, 1)
                    two = [w[0] > HALF for w in widths]
                    dve.wait_ge(topped, it * sum(two) + sum(two[:u + 1]))
                    tops = top2[:, u % 2, :]
                if branch == SWA:
                    head = heads * it + a
                    dve.tensor_scalar(neg[:, u % 2, :], tops, T.sink_raw[:, head:head + 1], -scale,
                                      ALU.max, ALU.mult).then_inc(negated, 1)
                else:
                    dve.tensor_scalar(neg[:, u % 2, :], tops, -scale, None, ALU.mult).then_inc(negated, 1)

            def normalise(it, u):
                dve.wait_ge(exped, it * NQ + 2 * u + 2 + 2 * RS)
                total = den
                if branch == SWA:
                    dve.wait_ge(sunk, it * NU + u + 1)
                    dve.tensor_tensor(den2[:, u % 2, :], den[:, u % 2, :], esink[:, u % 2, :],
                                      ALU.add).then_inc(summed, 1)
                    dve.wait_ge(summed, it * NU + u + 1)
                    total = den2
                dve.reciprocal(inv[:, u % 2, :], total[:, u % 2, :]).then_inc(inverted, 1)
                dve.wait_ge(inverted, it * NU + u + 1)
                for q in range(2):
                    i = 2 * units[u][1] + q
                    nk = P * (keys(i)[1] - keys(i)[0])
                    p = prob[:, u % PROBS, q, 0:nk]
                    dve.tensor_scalar(p, p, inv[:, u % 2, q:q + 1], None, ALU.mult).then_inc(normed, 1)

            def split_lo(it, u):
                for s, pack in enumerate(packs[u]):
                    n, w = first_pack[u] + s, width_of(pack)
                    dve.wait_ge(pt_hi_done, it * NS + n + 1)
                    dve.tensor_tensor(pt_lo[:, u % 2, s, 0:w], turn_ps[:, n % 2, 0:w], f32(pt_hi[:, u % 2, s, 0:w]),
                                      ALU.subtract).then_inc(pt_lo_done, 1)

            def keep_out(it, u):
                a, g = units[u]
                at = slice(2 * P * g, 2 * P * (g + 1))
                chunk = u // unit_of_chunk
                if u % unit_of_chunk == 0:
                    dve.wait_ge(stored[chunk], 16 * it + 1)
                    if isinstance(it, int) and it == 0 and T.stores:
                        dve.wait_ge(*T.stores[chunk])
                if branch == MEM:
                    dve.wait_ge(pv_done, it * NU + u + 2)
                    dve.tensor_copy(out_sb[:, chunk, at], out_ps[:, 0:2 * P]).then_inc(out_done, 1)
                else:
                    dve.wait_ge(lower_kept, it * NU + u + 1)
                    rows = slice(64 * (a % 2), 64 * (a % 2) + 64)
                    dve.tensor_tensor(out_sb[rows, chunk, at], out_ps[0:64, 0:2 * P], tmp[:, u % 2, :],
                                      ALU.add).then_inc(out_done, 1)

            def body(it, nxt, turn):
                split_before = plan(nxt.nb)[1] if nxt else None
                for t in range(STEPS):
                    if t >= 4:
                        keep_out(it, t - 4)
                    if nxt and t == 0:
                        nxt.split_low(dve, turn, 0)
                    if t < NU:
                        maxima(it, t)
                    for b in range(1, nxt.nb if nxt else 0):
                        if split_before[b] == t:
                            nxt.split_low(dve, turn, b)
                    if 2 <= t < NU + 2:
                        split_lo(it, t - 2)
                    if branch == FOX and t == 0:
                        unpack_values(it)
                    if 1 <= t <= NU:
                        normalise(it, t - 1)
                    if t == late_at and branch != FOX:
                        unpack_low(dve, it, 1)
                    if t == early_at and nxt == own and branch != FOX:
                        unpack_low(dve, turn, 0)

            unpack_low(dve, 0, 0)
            if branch == FOX:
                dve.wait_ge(*T.stores[0])
            over_turns(dve, body)

        @block.gpsimd
        def _(pool):
            if branch == SWA:
                own.rope(pool, 0, 1)
                own.rope(pool, 1, 0)
                own.rope(pool, 1, 1)
            if branch == MEM:
                coming.rope(pool, 0, 0)
            if branch == FOX:
                with pool.Fori(0, turns - 1) as it:
                    unpack_low(pool, it, 1)
                    unpack_low(pool, it + 1, 0)
                unpack_low(pool, turns - 1, 1)

        @block.tensor
        def _(pe):
            pe.sem_inc(scored, 1)
            pe.sem_inc(pv_done, 1)

            def turn_values(it):
                pe.wait_ge(kept, (it + 1) * 2 * nb + 2)
                pe.wait_ge(pt_lo_done, it * NS + 2)
                for b in range(2):
                    for t in range(4):
                        mm = pe.transpose(turn_ps[:, b, P * t:P * (t + 1)],
                                          raw[:, 2, P * (4 * b + t):P * (4 * b + t + 1)], T.ident[:])
                    mm.then_inc(v_turned, 1)

            def scores(it, u):
                a, g = units[u]
                if u == 0:
                    pe.wait_ge(act_unpacked, it * ACT_U + ACT_EARLY)
                    pe.wait_ge(low_unpacked, it * LOW_U + LOW_EARLY)
                if u == NU // 2:
                    pe.wait_ge(act_unpacked, it * ACT_U + ACT_U)
                    pe.wait_ge(low_unpacked, it * LOW_U + LOW_U)
                if branch != FOX:
                    pe.wait_ge(exped, it * NQ + 2 * u + 2)
                for q, c, w, b, to in pieces[u]:
                    k0 = keys(2 * g + q)[0]
                    cut = slice(P * (2 * g + q), P * (2 * g + q + 1))
                    at = slice(P * k0 + c, P * k0 + c + w)
                    n = first_bank[u] + b
                    if branch == FOX:
                        pe.wait_ge(maxed, it * NM + n + 1)
                    ps = score_ps[:, bank(it, n), :]
                    out = ps[:, to:to + w]
                    last = c + w == widths[u][q]
                    if branch == MEM:
                        head = heads * it + a
                        mm = product(pe, out, q_hi[:, a, cut], q_lo[:, a, cut], k_hi[:, head, at],
                                     k_lo[:, head, at], start=True, stop=True)
                    else:
                        rows = slice(64 * (a % 2), 64 * (a % 2) + 64)
                        kk1, kk2 = (k1[:, a, at], k2[rows, at]) if branch == FOX else \
                                   (k1[:, it, at], k2[rows, it, at])
                        pe.matmul(out, q_both[:, a, cut], kk1, start=True, stop=False)
                        mm = pe.matmul(out, q_both[rows, a, cut], kk2, start=False, stop=not last)
                        if last:
                            band = P if branch == FOX else w
                            mask = T.masks_bf[:, 0:P] if branch == FOX else T.masks_bf[:, 3 * P - w:3 * P]
                            mm = pe.matmul(ps[:, to + w - band:to + w], T.ident_bf[:], mask,
                                           start=False, stop=True)
                    if branch == FOX or q == 1:
                        mm.then_inc(scored, 1)

            def transposes(it, u):
                g = units[u][1]
                pe.wait_ge(normed, it * NQ + 2 * u + 2)
                for s, pack in enumerate(packs[u]):
                    n = first_pack[u] + s
                    pe.wait_ge(pt_lo_done, it * NS + n + 1)
                    for j, a, b, to in pack:
                        for q in range(a // P, b // P):
                            at = P * (j - keys(2 * g + q)[0])
                            c = to + P * q - a
                            mm = pe.transpose(turn_ps[:, n % 2, c:c + P], prob[:, u % PROBS, q, at:at + P],
                                              T.ident[:])
                    mm.then_inc(turned, 1)

            def outputs(it, u):
                head = units[u][0]
                if u == 0 and branch == FOX:
                    pe.wait_ge(v_lo_done, it * 2 + 2)
                pe.wait_ge(out_done, it * NU + u + 1)
                pe.wait_ge(pt_lo_done, it * NS + first_pack[u + 1] + 2)
                parts = [(s, *part) for s, pack in enumerate(packs[u]) for part in pack]
                for s, j, a, b, to in parts:
                    first, last = (s, j, a, b, to) == parts[0], (s, j, a, b, to) == parts[-1]
                    out, hi, lo = out_ps[:, a:b], pt_hi[:, u % 2, s, to:to + b - a], pt_lo[:, u % 2, s, to:to + b - a]
                    if branch == MEM:
                        mm = product(pe, out, v_hi[:, heads * it + head, j, :], v_lo[:, heads * it + head, j, :],
                                     hi, lo, start=first, stop=last)
                    else:
                        vv = v[:, head if branch == FOX else it, j, :, :].rearrange("p a d -> p (a d)")
                        pe.matmul(out, vv, hi, start=first, stop=False)
                        mm = pe.matmul(out, vv, lo, start=False, stop=last)
                mm.then_inc(pv_done, 1)

            def body(it, nxt, turn):
                fill_at = plan(nxt.nb)[0] if nxt else None
                scores(it, 0)
                if branch == FOX:
                    turn_values(it)
                if nxt:
                    nxt.project(pe, turn, 0, start_groups)
                for t in range(STEPS - 1):
                    if 2 <= t < NU + 2:
                        transposes(it, t - 2)
                    if nxt and t < NU + 2:
                        nxt.project(pe, turn, fill_at[2 * t], fill_at[2 * t + 1])
                    if t >= 3:
                        outputs(it, t - 3)
                    if nxt and t < NU + 2:
                        nxt.project(pe, turn, fill_at[2 * t + 1], fill_at[2 * t + 2])
                    if t + 1 < NU:
                        scores(it, t + 1)

            over_turns(pe, body)
    T.stores = [(sem, 16 * turns + 1) for sem in stored] + (T.stores if branch == SWA else [])


def merge_stage(nc, T):
    with ExitStack() as stack:
        kit = Kit(nc, stack)
        NJ = KD
        KO = 4
        width = (KD + KO) * P
        W = Weights(kit, "wmg", 2, width, T.w_raw, T.w_hi, T.w_lo)
        o_hi, o_lo = (kit.sb(n, [P, 2, KO, S], F32R) for n in ("branch_hi", "branch_lo"))
        o_raw = kit.sb("branch_raw", [P, S])
        gate = kit.sb("gate", [P, 2, HALF])
        term = kit.sb("term", [P, 2, HALF])
        bias = kit.sb("gate_bias", [P, 3 * NJ])
        gate_ps, y_ps = kit.ps("gate_ps", [P, 2, HALF]), kit.ps("y_ps", [P, 2, HALF])
        bias_loaded, first_loaded = kit.sem("gate_bias_loaded"), kit.sem("branch0_loaded")
        raw_loaded = kit.sem("branch_raw_loaded")
        o_hi_done, o_lo_done = kit.sem("branch_hi_done"), kit.sem("branch_lo_done")
        gate_done = kit.sem("gate_done")
        y_done = kit.sem("y_done")
        waited = kit.sem("merge_waited")
        gated = kit.sem("gated")
        weighted = kit.sem("weighted")
        summed = kit.sem("merged_summed")
        w_in = T.d["w_in"][0].rearrange("(k p) n -> p k n", p=P)
        w_o = [T.d[n][0].rearrange("(k p) n -> p k n", p=P) for n in ("w_o_fox", "w_o_swa", "w_o_mem")]

        block = stack.enter_context(nc.Block())

        @block.sync
        def _(sp):
            def load(b, j, s, n):
                if n is not None:
                    sp.wait_ge(W.lo_ready, n - 1)
                sp.dma_start(W.view(W.raw, s, 0, KD * P).rearrange("p (k n) -> p k n", k=KD),
                             w_in[:, :, bass.ds(j * P + (COL["glog"] + b * D), P)]).then_inc(W.loaded[s], 16)
                sp.dma_start(W.view(W.raw, s, KD * P).rearrange("p (k n) -> p k n", k=KO),
                             w_o[b][:, :, bass.ds(j * P, P)]).then_inc(W.loaded[s], 16)

            def load_pair(b, it):
                for s in range(2):
                    load(b, it * 2 + s, s, it * 2 + (b * NJ + s))
                if b < 2:
                    sp.wait_ge(o_lo_done, it + (KO + b * KO))
                    sp.dma_start(o_raw[:], T.out_dram[b + 1][bass.ds(it * P, P), :]).then_inc(raw_loaded, 16)

            sp.dma_start(T.merged[:, 0:KO, :], T.out_dram[0].rearrange("(c p) s -> p c s", p=P))\
                .then_inc(first_loaded, 16)
            load(0, 0, 0, None)
            load(0, 1, 1, None)
            sp.dma_start(bias[:], T.d["b_branch"][0].rearrange("(n p) -> p n", p=P),
                         allow_slow_non_contiguous=True).then_inc(bias_loaded, 16)
            sp.wait_ge(o_lo_done, KO)
            sp.dma_start(o_raw[:], T.out_dram[1][0:P, :]).then_inc(raw_loaded, 16)
            with sp.Fori(1, NJ // 2) as it:
                load_pair(0, it)
            for b in (1, 2):
                with sp.Fori(0, NJ // 2) as it:
                    load_pair(b, it)

        @block.scalar
        def _(act):
            def split_w(s, n):
                act.wait_ge(W.loaded[s], n * 16 + (32 - 16 * s))
                act.activation(W.view(W.hi, s), W.view(W.raw, s), ACT.Copy).then_inc(W.hi_ready, 1)

            def step(b, it, s, more):
                n = it * 2 + (b * NJ + s)
                if more:
                    act.wait_ge(y_done, n * 2 + 2)
                    split_w(1 - s, n + 1)
                for h in range(2):
                    act.wait_ge(gate_done, n * 2 + h + 1)
                    act.wait_ge(weighted, n * 2 + h + 1)
                    act.sem_inc(waited, 1)
                    act.activation(gate[:, h, :], gate_ps[:, h, :], ACT.Sigmoid,
                                   bias=bias[:, bass.ds(n, 1)]).then_inc(gated, 1)

            def split_branch(b, it):
                act.wait_ge(raw_loaded, it * 16 + ((b - 1) * KO * 16 + 16))
                act.sem_inc(waited, 1)
                act.activation(o_hi[:, b % 2, bass.ds(it, 1), :].rearrange("p a s -> p (a s)"), o_raw[:],
                               ACT.Copy).then_inc(o_hi_done, 1)

            def pair(b, it, last):
                step(b, it, 0, True)
                if b < 2:
                    split_branch(b + 1, it)
                step(b, it, 1, not last)

            split_w(0, 0)
            act.wait_ge(first_loaded, 16)
            for c in range(KO):
                act.activation(o_hi[:, 0, c, :], T.merged[:, c, :], ACT.Copy).then_inc(o_hi_done, 1)
            act.wait_ge(bias_loaded, 16)
            for b in range(3):
                with act.Fori(0, NJ // 2 - (b == 2)) as it:
                    pair(b, it, False)
            pair(2, NJ // 2 - 1, True)

        @block.vector
        def _(dve):
            dve.sem_inc(weighted, 2)

            def split_w(s, n):
                dve.wait_ge(W.hi_ready, n + 1)
                dve.tensor_tensor(W.view(W.lo, s), W.view(W.raw, s), f32(W.view(W.hi, s)),
                                  ALU.subtract).then_inc(W.lo_ready, 1)

            def step(b, it, s, more):
                n = it * 2 + (b * NJ + s)
                if more:
                    split_w(1 - s, n + 1)
                for h in range(2):
                    dve.wait_ge(gated, n * 2 + h + 1)
                    dve.wait_ge(y_done, n * 2 + h + 1 + 2)
                    at = T.merged[:, bass.ds(it * 2 + s, 1), HALF * h:HALF * (h + 1)].rearrange("p a n -> p (a n)")
                    if b == 0:
                        dve.tensor_tensor(at, y_ps[:, h, :], gate[:, h, :], ALU.mult).then_inc(weighted, 1)
                    else:
                        dve.tensor_tensor(term[:, h, :], y_ps[:, h, :], gate[:, h, :], ALU.mult)\
                            .then_inc(weighted, 1)
                        dve.wait_ge(weighted, n * 2 + h + 1 + 2)
                        dve.tensor_tensor(at, at, term[:, h, :], ALU.add).then_inc(summed, 1)

            def split_branch(b, it):
                dve.wait_ge(o_hi_done, it + (b * KO + 1))
                cut = bass.ds(it, 1)
                dve.tensor_tensor(o_lo[:, b % 2, cut, :].rearrange("p a s -> p (a s)"), o_raw[:],
                                  f32(o_hi[:, b % 2, cut, :]).rearrange("p a s -> p (a s)"),
                                  ALU.subtract).then_inc(o_lo_done, 1)

            def pair(b, it, last):
                step(b, it, 0, True)
                if b < 2:
                    split_branch(b + 1, it)
                step(b, it, 1, not last)

            split_w(0, 0)
            for c in range(KO):
                dve.wait_ge(o_hi_done, c + 1)
                dve.tensor_tensor(o_lo[:, 0, c, :], T.merged[:, c, :], f32(o_hi[:, 0, c, :]),
                                  ALU.subtract).then_inc(o_lo_done, 1)
            dve.wait_ge(o_lo_done, KO)
            for b in range(3):
                with dve.Fori(0, NJ // 2 - (b == 2)) as it:
                    pair(b, it, False)
            pair(2, NJ // 2 - 1, True)

        @block.tensor
        def _(pe):
            pe.sem_inc(y_done, 2)

            def step(b, it, s):
                n = it * 2 + (b * NJ + s)
                pe.wait_ge(W.lo_ready, n + 1)
                hi, lo = W.view(W.hi, s), W.view(W.lo, s)
                for h in range(2):
                    at = slice(HALF * h, HALF * (h + 1))
                    pe.wait_ge(weighted, n * 2 + h + 1)
                    for k in range(KD):
                        cut = slice(P * k, P * (k + 1))
                        mm = product(pe, gate_ps[:, h, :], hi[:, cut], lo[:, cut],
                                     T.h_hi[:, k, at], T.h_lo[:, k, at], start=(k == 0), stop=(k == KD - 1))
                    mm.then_inc(gate_done, 1)
                    for k in range(KO):
                        cut = slice(P * (KD + k), P * (KD + k + 1))
                        mm = product(pe, y_ps[:, h, :], hi[:, cut], lo[:, cut],
                                     o_hi[:, b % 2, k, at], o_lo[:, b % 2, k, at], start=(k == 0), stop=(k == KO - 1))
                    mm.then_inc(y_done, 1)

            for b in range(3):
                pe.wait_ge(o_lo_done, KO * (b + 1))
                with pe.Fori(0, NJ // 2) as it:
                    for s in range(2):
                        step(b, it, s)


def output_stage(nc, T):
    with ExitStack() as stack:
        kit = Kit(nc, stack)
        m_hi, m_lo = T.h_hi, T.h_lo
        x1 = T.merged
        groups = [(0, 3), (3, 6), (6, 8)]
        W = Weights(kit, "wout", 3, D, T.w_raw, T.w_hi, T.w_lo)
        acc = kit.ps("acc_ps", [P, 3, 2, HALF])
        turn_ps = kit.ps("out_turn_ps", [P, 2, HALF])
        gains = kit.sb("out_gains", [P, 2, D])
        part = kit.sb("out_part", [P, D])
        normed = kit.sb("out_normed", [P, 2, D])
        junk = kit.sb("out_junk", [P, HALF])
        ssq = kit.sb("out_ssq", [P, NT, 3])
        stat = kit.sb("out_stat", [P, NT, 5])
        g_loaded, x_loaded = kit.sem("out_gains_loaded"), kit.sem("x_loaded")
        m_hi_done, m_lo_done = kit.sem("m_hi_done"), kit.sem("m_lo_done")
        added = kit.sem("out_added")
        squared = kit.sem("out_squared")
        squared_x1 = kit.sem("out_squared_x1")
        meaned = kit.sem("out_meaned")
        rooted, rooted_x1 = kit.sem("out_rooted"), kit.sem("out_rooted_x1")
        parted = kit.sem("out_parted")
        x1_done = kit.sem("x1_done")
        renormed = kit.sem("renormed")
        turned = kit.sem("out_turned")
        h_hi_done, h_lo_done = kit.sem("h2_hi_done"), kit.sem("h2_lo_done")
        slots = [(gi, j) for gi in range(len(groups)) for j in range(KD)]
        group_of = {t: gi for gi, (a, b) in enumerate(groups) for t in range(a, b)}

        def schedule(split_w, first, second, third):
            n = 3
            for gi, (a, b) in enumerate(groups):
                while n < KD * (gi + 1):
                    split_w(n)
                    n += 1
                more = gi + 1 < len(groups)
                for t in range(a, b):
                    first(t)
                    if more:
                        split_w(n)
                        n += 1
                for t in range(a, b):
                    second(t)
                    for _ in range(min(2, KD * (gi + 2) - n) if more else 0):
                        split_w(n)
                        n += 1
                    third(t)

        block = stack.enter_context(nc.Block())

        @block.sync
        def _(sp):
            for n, (_, j) in enumerate(slots):
                if n >= 3:
                    sp.wait_ge(W.lo_ready, n - 2)
                sp.dma_start(W.view(W.raw, n % 3), T.d["w_out"][0, P * j:P * (j + 1), :])\
                    .then_inc(W.loaded[n % 3], 16)
                if n == 2:
                    for i, name in enumerate(("g_mix_post", "g_ffn_pre")):
                        sp.dma_start(gains[:, i, :], T.d[name][0:1, :].to_broadcast([P, D])).then_inc(g_loaded, 16)
                if n == KD - 1:
                    sp.wait_ge(m_lo_done, KD)
                    sp.dma_start(x1[:], T.d["x"][0].rearrange("(t p) n -> p t n", p=P)).then_inc(x_loaded, 16)

        @block.scalar
        def _(act):
            def split_w(n):
                act.wait_ge(W.loaded[n % 3], 16 * (n // 3 + 1))
                if n >= 3:
                    act.wait_ge(added, n - 2)
                act.activation(W.view(W.hi, n % 3), W.view(W.raw, n % 3), ACT.Copy).then_inc(W.hi_ready, 1)

            def square_acc(t):
                gi = group_of[t]
                act.wait_ge(added, KD * (gi + 1))
                for h in range(2):
                    if t + h:
                        act.wait_ge(squared, 2 * t + h)
                    act.activation(junk[:], acc[:, t - groups[gi][0], h, :], ACT.Square,
                                   accum_out=ssq[:, t, h:h + 1]).then_inc(squared, 1)

            def square_x1(t):
                act.wait_ge(x1_done, t + 1)
                if t >= 2:
                    act.wait_ge(turned, 2 * (t - 1))
                act.activation(normed[:, t % 2, :], x1[:, t, :], ACT.Square,
                               accum_out=ssq[:, t, 2:3]).then_inc(squared_x1, 1)

            def split_h(t):
                for b in range(2):
                    act.wait_ge(turned, 2 * t + b + 1)
                    act.activation(T.h2_hi[:, 4 * b:4 * b + 4, P * t:P * (t + 1)],
                                   turn_ps[:, b, :].rearrange("p (c n) -> p c n", c=4),
                                   ACT.Copy).then_inc(h_hi_done, 1)

            for j in range(KD):
                act.activation(m_hi[:, j, :], T.merged[:, j, :], ACT.Copy).then_inc(m_hi_done, 1)
                if j < 3:
                    split_w(j)
            schedule(split_w, square_acc, square_x1, split_h)

        @block.gpsimd
        def _(pool):
            done = 0
            for a, b in groups:
                for t in range(a, b):
                    pool.wait_ge(squared, 2 * t + 2)
                    pool.tensor_tensor(stat[:, t, 0:1], ssq[:, t, 0:1], ssq[:, t, 1:2], ALU.add)\
                        .then_inc(meaned, 1)
                    pool.wait_ge(meaned, done + 1)
                    pool.tensor_scalar(stat[:, t, 1:2], stat[:, t, 0:1], 1.0 / D, EPS, ALU.mult, ALU.add)\
                        .then_inc(meaned, 1)
                    pool.wait_ge(meaned, done + 2)
                    pool.tensor_tensor(stat[:, t, 2:3], stat[:, t, 1:2], T.minus_half[:], ALU.pow)\
                        .then_inc(rooted, 1)
                    done += 2
                for t in range(a, b):
                    pool.wait_ge(squared_x1, t + 1)
                    pool.tensor_scalar(stat[:, t, 3:4], ssq[:, t, 2:3], 1.0 / D, EPS, ALU.mult, ALU.add)\
                        .then_inc(meaned, 1)
                    pool.wait_ge(meaned, done + 1)
                    pool.tensor_tensor(stat[:, t, 4:5], stat[:, t, 3:4], T.minus_half[:], ALU.pow)\
                        .then_inc(rooted_x1, 1)
                    done += 1

        @block.vector
        def _(dve):
            def split_w(n):
                dve.wait_ge(W.hi_ready, n + 1)
                dve.tensor_tensor(W.view(W.lo, n % 3), W.view(W.raw, n % 3), f32(W.view(W.hi, n % 3)),
                                  ALU.subtract).then_inc(W.lo_ready, 1)

            def residual(t):
                gi = group_of[t]
                dve.wait_ge(rooted, t + 1)
                if t >= 1:
                    dve.wait_ge(x1_done, t)
                if t == 0:
                    dve.wait_ge(g_loaded, 32)
                    dve.wait_ge(x_loaded, 16)
                for h in range(2):
                    at = slice(HALF * h, HALF * (h + 1))
                    dve.scalar_tensor_tensor(out=part[:, at], in0=acc[:, t - groups[gi][0], h, :],
                                             scalar=stat[:, t, 2:3], in1=gains[:, 0, at],
                                             op0=ALU.mult, op1=ALU.mult).then_inc(parted, 1)
                dve.wait_ge(parted, 2 * t + 2)
                dve.tensor_tensor(x1[:, t, :], x1[:, t, :], part[:], ALU.add).then_inc(x1_done, 1)

            def renormalise(t):
                dve.wait_ge(rooted_x1, t + 1)
                dve.scalar_tensor_tensor(out=normed[:, t % 2, :], in0=x1[:, t, :], scalar=stat[:, t, 4:5],
                                         in1=gains[:, 1, :], op0=ALU.mult, op1=ALU.mult).then_inc(renormed, 1)

            def split_h(t):
                for b in range(2):
                    dve.wait_ge(h_hi_done, 2 * t + b + 1)
                    cut = (slice(None), slice(4 * b, 4 * b + 4), slice(P * t, P * (t + 1)))
                    dve.tensor_tensor(T.h2_lo[cut], turn_ps[:, b, :].rearrange("p (c n) -> p c n", c=4),
                                      f32(T.h2_hi[cut]), ALU.subtract).then_inc(h_lo_done, 1)

            for j in range(KD):
                dve.wait_ge(m_hi_done, j + 1)
                dve.tensor_tensor(m_lo[:, j, :], T.merged[:, j, :], f32(m_hi[:, j, :]),
                                  ALU.subtract).then_inc(m_lo_done, 1)
                if j < 3:
                    split_w(j)
            schedule(split_w, residual, renormalise, split_h)

        @block.tensor
        def _(pe):
            def turn(t):
                pe.wait_ge(renormed, t + 1)
                for b in range(2):
                    if t >= 1:
                        pe.wait_ge(h_lo_done, 2 * t + b - 1)
                    for c in range(4):
                        mm = pe.transpose(turn_ps[:, b, P * c:P * (c + 1)],
                                          normed[:, t % 2, P * (4 * b + c):P * (4 * b + c + 1)], T.ident[:])
                    mm.then_inc(turned, 1)

            for n, (gi, j) in enumerate(slots):
                a, b = groups[gi]
                pe.wait_ge(W.lo_ready, n + 1)
                if gi == 0:
                    pe.wait_ge(m_lo_done, j + 1)
                if gi >= 1 and j in (3, 5, 7):
                    t = groups[gi - 1][0] + (j - 3) // 2
                    turn(t)
                for t in range(a, b):
                    if j == 0 and gi >= 1:
                        pe.wait_ge(x1_done, groups[gi - 1][0] + t - a + 1)
                    cut = slice(P * t, P * (t + 1))
                    for h in range(2):
                        at = slice(HALF * h, HALF * (h + 1))
                        w_hi, w_lo = W.view(W.hi, n % 3)[:, at], W.view(W.lo, n % 3)[:, at]
                        mm = product(pe, acc[:, t - a, h, :], m_hi[:, j, cut], m_lo[:, j, cut], w_hi, w_lo,
                                     start=(j == 0), stop=(j == KD - 1))
                mm.then_inc(added, 1)
            for t in range(*groups[-1]):
                turn(t)


def ffn_stage(nc, T):
    with ExitStack() as stack:
        kit = Kit(nc, stack)
        x1 = T.merged
        NG = NF // 2
        W = Weights(kit, "wffn", 3, D, T.w_raw, T.w_hi, T.w_lo)
        y = kit.sb("ffn_y", [P, NT, D])
        u = kit.sb("ffn_u", [P, 2, HALF])
        silu = kit.sb("ffn_silu", [P, 2, HALF])
        u_hi, u_lo = (kit.sb("ffn_" + n, [P, 2, S], F32R) for n in ("u_hi", "u_lo"))
        gain = kit.sb("ffn_gain", [P, D])
        junk = kit.sb("ffn_junk", [P, D])
        ssq, mean, rstd = (kit.sb("ffn_" + n, [P, NT]) for n in ("ssq", "mean", "rstd"))
        a_ps, c_ps = kit.ps("a_ps", [P, 2, HALF]), kit.ps("c_ps", [P, 2, HALF])
        out_ps = kit.ps("ffn_out_ps", [P, 4, HALF])
        g_loaded = kit.sem("ffn_gain_loaded")
        zeroed = kit.sem("ffn_zeroed")
        a_done, c_done = kit.sem("a_done"), kit.sem("c_done")
        silued = kit.sem("silued")
        gated = kit.sem("ffn_gated")
        u_hi_done, u_lo_done = kit.sem("u_hi_done"), kit.sem("u_lo_done")
        part_done = kit.sem("part_done")
        added = kit.sem("ffn_added")
        squared, meaned, rooted = kit.sem("ffn_squared"), kit.sem("ffn_meaned"), kit.sem("ffn_rooted")
        scaled, finished = kit.sem("ffn_scaled"), kit.sem("ffn_finished")
        last_finished, stored = kit.sem("ffn_last_finished"), kit.sem("out_stored")
        w_in = T.d["w_ffn_in"][0].rearrange("(k p) n -> p k n", p=P)
        w_out = T.d["w_ffn_out"][0]
        out = T.d["out"][0].rearrange("(t p) n -> t p n", p=P)
        A0, C0, A1, C1, R0, R1 = range(6)

        block = stack.enter_context(nc.Block())

        @block.sync
        def _(sp):
            def load(g, i, wait):
                if wait is not None:
                    sp.wait_ge(W.lo_ready, wait)
                to = W.view(W.raw, i % 3)
                if i < R0:
                    src = w_in[:, :, bass.ds(g * 2 * P + (P * (i // 2) + D_FF * (i % 2)), P)]
                    sp.dma_start(to.rearrange("p (k n) -> p k n", k=KD), src).then_inc(W.loaded[i % 3], 16)
                else:
                    src = w_out[bass.ds(g * 2 * P + P * (i - R0), P), :]
                    sp.dma_start(to, src).then_inc(W.loaded[i % 3], 16)

            for i in range(6):
                load(0, i, i - 2 if i >= 3 else None)
            sp.dma_start(gain[:], T.d["g_ffn_post"][0:1, :].to_broadcast([P, D])).then_inc(g_loaded, 16)
            with sp.Fori(1, NG) as g:
                for i in range(6):
                    load(g, i, g * 6 + (i - 2))
            for t in range(NT):
                if t < NT - 1:
                    sp.wait_ge(finished, t + 1)
                else:
                    sp.wait_ge(last_finished, 1)
                sp.dma_start(out[t], y[:, t, :]).then_inc(stored, 16)
            sp.wait_ge(stored, 16 * NT)

        @block.scalar
        def _(act):
            def split_w(g, i, sem=None, value=None):
                act.wait_ge(W.loaded[i % 3], g * 32 + (16 * (i // 3) + 16))
                if sem is not None:
                    act.wait_ge(sem, value)
                act.activation(W.view(W.hi, i % 3), W.view(W.raw, i % 3), ACT.Copy).then_inc(W.hi_ready, 1)

            def halves(g, i):
                for h in range(2):
                    n = g * 4 + (2 * i + h)
                    act.wait_ge(a_done, n + 1)
                    act.wait_ge(gated, n + 1)
                    act.activation(silu[:, h, :], a_ps[:, h, :], ACT.Silu).then_inc(silued, 1)
                    if (i, h) == (1, 1):
                        split_w(g, R1, a_done, g * 4 + 4)
                    act.wait_ge(gated, n + 1 + 2)
                    act.activation(u_hi[:, i, HALF * h:HALF * (h + 1)], u[:, h, :], ACT.Copy)\
                        .then_inc(u_hi_done, 1)

            def body(g, more):
                halves(g, 0)
                split_w(g, C1, a_done, g * 4 + 2)
                split_w(g, R0, c_done, g * 4 + 2 + 2)
                halves(g, 1)
                if more:
                    split_w(g + 1, A0, c_done, g * 4 + 4 + 2)
                    split_w(g + 1, C0, part_done, g * 16 + 16 + 4)
                    split_w(g + 1, A1, part_done, g * 16 + 16 + 4)

            for i in (A0, C0, A1):
                split_w(0, i)
            with act.Fori(0, NG - 1) as g:
                body(g, True)
            body(NG - 1, False)
            for t in range(NT):
                act.wait_ge(added, 16 * (NG - 1) + 4 + 2 * (t + 1))
                if t >= 1:
                    act.wait_ge(squared, t)
                act.activation(junk[:], y[:, t, :], ACT.Square, accum_out=ssq[:, t:t + 1]).then_inc(squared, 1)

        @block.vector
        def _(dve):
            dve.sem_inc(gated, 2)
            dve.sem_inc(added, 4)

            def split_w(g, i):
                dve.wait_ge(W.hi_ready, g * 6 + (i + 1))
                dve.tensor_tensor(W.view(W.lo, i % 3), W.view(W.raw, i % 3), f32(W.view(W.hi, i % 3)),
                                  ALU.subtract).then_inc(W.lo_ready, 1)

            def halves(g, i):
                for h in range(2):
                    n = g * 4 + (2 * i + h)
                    if (i, h) == (1, 1):
                        split_w(g, R1)
                    dve.wait_ge(silued, n + 1)
                    dve.wait_ge(c_done, n + 1 + 2)
                    dve.tensor_tensor(u[:, h, :], c_ps[:, h, :], silu[:, h, :], ALU.mult).then_inc(gated, 1)
                    dve.wait_ge(u_hi_done, n + 1)
                    at = slice(HALF * h, HALF * (h + 1))
                    dve.tensor_tensor(u_lo[:, i, at], u[:, h, :], f32(u_hi[:, i, at]),
                                      ALU.subtract).then_inc(u_lo_done, 1)

            def add_parts(g, first, last):
                for n in range(first, last):
                    dve.wait_ge(part_done, g * 16 + (n + 1 + 4))
                    at = y[:, n // 2, HALF * (n % 2):HALF * (n % 2 + 1)]
                    dve.tensor_tensor(at, out_ps[:, n % 4, :], at, ALU.add).then_inc(added, 1)

            def body(g, more):
                halves(g, 0)
                split_w(g, C1)
                split_w(g, R0)
                halves(g, 1)
                if more:
                    split_w(g + 1, A0)
                dve.wait_ge(added, g * 16 + 4)
                if more:
                    add_parts(g, 0, 16)
                    split_w(g + 1, C0)
                    split_w(g + 1, A1)
                    return
                dve.wait_ge(g_loaded, 16)
                for quarter in range(4):
                    add_parts(g, 4 * quarter, 4 * quarter + 4)
                    if quarter >= 1:
                        scale_rows(2 * quarter - 2)
                        scale_rows(2 * quarter - 1)
                scale_rows(6)
                scale_rows(7)
                dve.wait_ge(scaled, NT)
                dve.tensor_tensor(y[:, 7, :], y[:, 7, :], x1[:, 7, :], ALU.add).then_inc(last_finished, 1)

            def scale_rows(t):
                dve.wait_ge(rooted, t + 1)
                dve.scalar_tensor_tensor(out=y[:, t, :], in0=y[:, t, :], scalar=rstd[:, t:t + 1],
                                         in1=gain[:], op0=ALU.mult, op1=ALU.mult).then_inc(scaled, 1)

            for i in (A0, C0, A1):
                split_w(0, i)
            dve.wait_ge(zeroed, 1)
            with dve.Fori(0, NG - 1) as g:
                body(g, True)
            body(NG - 1, False)

        @block.gpsimd
        def _(pool):
            pool.memset(y[:], 0.0).then_inc(zeroed, 1)
            for quarter in range(4):
                for t in (2 * quarter, 2 * quarter + 1):
                    pool.wait_ge(squared, t + 1)
                    pool.tensor_scalar(mean[:, t:t + 1], ssq[:, t:t + 1], 1.0 / D, EPS, ALU.mult, ALU.add)\
                        .then_inc(meaned, 1)
                    pool.wait_ge(meaned, t + 1)
                    pool.tensor_tensor(rstd[:, t:t + 1], mean[:, t:t + 1], T.minus_half[:], ALU.pow)\
                        .then_inc(rooted, 1)
                for t in (2 * quarter, 2 * quarter + 1)[:1 if quarter == 3 else 2]:
                    pool.wait_ge(scaled, t + 1)
                    pool.tensor_tensor(y[:, t, :], y[:, t, :], x1[:, t, :], ALU.add).then_inc(finished, 1)

        @block.tensor
        def _(pe):
            pe.sem_inc(c_done, 2)
            pe.sem_inc(part_done, 4)

            def hidden(g, i):
                a, c = (A0, C0) if i == 0 else (A1, C1)
                for h in range(2):
                    at = slice(HALF * h, HALF * (h + 1))
                    pe.wait_ge(gated, g * 4 + (2 * i + h + 1))
                    for ps, slot, done in ((a_ps, a, a_done), (c_ps, c, c_done)):
                        if h == 0:
                            pe.wait_ge(W.lo_ready, g * 6 + (slot + 1))
                        hi, lo = W.view(W.hi, slot % 3), W.view(W.lo, slot % 3)
                        for k in range(KD):
                            cut = slice(P * k, P * (k + 1))
                            mm = product(pe, ps[:, h, :], hi[:, cut], lo[:, cut], T.h2_hi[:, k, at],
                                         T.h2_lo[:, k, at], start=(k == 0), stop=(k == KD - 1))
                        mm.then_inc(done, 1)

            def output(g):
                for quarter in range(4):
                    for i in range(2):
                        slot = R0 + i
                        hi, lo = W.view(W.hi, slot % 3), W.view(W.lo, slot % 3)
                        if quarter == 0:
                            pe.wait_ge(W.lo_ready, g * 6 + (slot + 1))
                            pe.wait_ge(u_lo_done, g * 4 + (2 * i + 2))
                        for n in range(4 * quarter, 4 * quarter + 4):
                            if i == 0:
                                pe.wait_ge(added, g * 16 + (n + 1))
                            cut = slice(P * (n // 2), P * (n // 2 + 1))
                            at = slice(HALF * (n % 2), HALF * (n % 2 + 1))
                            mm = product(pe, out_ps[:, n % 4, :], u_hi[:, i, cut], u_lo[:, i, cut],
                                         hi[:, at], lo[:, at], start=(i == 0), stop=(i == 1))
                            if i == 1:
                                mm.then_inc(part_done, 1)

            with pe.Fori(0, NG) as g:
                for i in range(2):
                    hidden(g, i)
                output(g)


class Shared:
    pass


def build_program(nc, drams):
    T = Shared()
    Kit.sems = []
    T.d = drams
    T.scale = {FOX: HD ** -0.5, SWA: HD ** -0.5, MEM: 128 ** -0.5}
    T.cum_dram = nc.dram_tensor("cum_scratch", (8, S), F32, kind="Internal").ap()
    T.out_dram = [nc.dram_tensor(f"branch_scratch{b}", (4 * P, S), F32, kind="Internal").ap() for b in range(3)]
    with ExitStack() as whole:
        kit = Kit(nc, whole)
        T.ident = kit.sb("ident", [P, P])
        T.minus_half = kit.sb("minus_half", [P, 1])
        T.ident_bf = kit.sb("ident_bf", [P, P], BF16)
        T.masks_bf = kit.sb("masks_bf", [P, 3 * P], BF16)
        T.w_raw = kit.sb("w_raw", [P, 3 * D])
        T.w_hi, T.w_lo = kit.sb("w_hi", [P, 3 * D], F32R), kit.sb("w_lo", [P, 3 * D], F32R)
        T.projection, T.stores = {}, []
        with ExitStack() as first:
            kit1 = Kit(nc, first)
            T.h_hi, T.h_lo = (kit1.sb(n, [P, KD, S], F32R) for n in ("h_hi", "h_lo"))
            projected = first.enter_context(ExitStack())
            kit5 = Kit(nc, projected)
            T.raw = kit5.sb("raw", [P, 3, S])
            T.out_sb = kit5.sb("branch_out", [P, 2, S])
            T.proj_ps = kit5.ps("proj_ps", [P, 2, HALF])
            with ExitStack() as early:
                kit2 = Kit(nc, early)
                T.rot = kit2.sb("rot", [P, 2, S])
                T.rope = kit2.sb("rope_sb", [P, 2, S])
                T.sink, T.sink_raw = kit2.sb("sink", [P, 8]), kit2.sb("sink_unscaled", [P, 8])
                T.k1, T.k2 = kit2.sb("swa_k1", [P, 2, S], F32R), kit2.sb("swa_k2", [P, 2, S], F32R)
                T.v = kit2.sb("swa_v", [P, 2, NT, 2, HD], F32R)
                with ExitStack() as memory:
                    kit3 = Kit(nc, memory)
                    T.mk_hi, T.mk_lo = (kit3.sb(n, [P, 4, N_MEM], F32R) for n in ("mk_hi", "mk_lo"))
                    T.mv_hi, T.mv_lo = (kit3.sb(n, [P, 4, 2, P], F32R) for n in ("mv_hi", "mv_lo"))
                    with ExitStack() as raw:
                        kit4 = Kit(nc, raw)
                        T.masks = kit4.sb("masks_sb", [P, 3 * P])
                        T.mem_kv = kit4.sb("mem_kv", [P, 8, N_MEM])
                        normalise_stage(nc, T)
                        shared_stage(nc, T)
                    attention_stage(nc, T, MEM)
                attention_stage(nc, T, SWA)
            attention_stage(nc, T, FOX)
            projected.close()
            T.merged = kit.sb("merged", [P, KD, S], side="right")
            Kit.free_semaphores(nc)
            merge_stage(nc, T)
            T.h2_hi, T.h2_lo = (kit.sb(n, [P, KD, S], F32R, side="right") for n in ("h2_hi", "h2_lo"))
            output_stage(nc, T)
        ffn_stage(nc, T)


_INS = ["x", "mem", "g_mix_pre", "g_mix_post", "w_in", "b_fgate", "b_branch", "sinks", "g_mem", "w_mem_kv",
        "w_o_fox", "w_o_swa", "w_o_mem", "w_out", "g_ffn_pre", "g_ffn_post", "w_ffn_in", "w_ffn_out"]


def _constants():
    query, key = np.arange(P)[:, None], np.arange(P)[None, :]
    causal = np.where(key <= query, 0.0, -BIG)
    band_key = np.arange(2 * P)[None, :] - P
    chunk_q, chunk_k = query // 64, band_key // 64
    band = np.where((chunk_k <= chunk_q) & (chunk_k > chunk_q - 2), 0.0, -BIG)
    half = HD // 2
    inv = (np.float32(10000.0) ** (-np.arange(half, dtype=np.float32) / np.float32(half))).astype(np.float32)
    angle = (np.arange(S, dtype=np.float32)[None, :] * inv[:, None]).astype(np.float32)
    cos, sin = np.cos(angle), np.sin(angle)
    rope = np.stack([np.tile(cos, (4, 1)), np.concatenate([-sin, sin, -sin, sin])], axis=1)
    return {"ident": np.eye(P, dtype=np.float32),
            "masks": np.concatenate([causal, band], axis=1).astype(np.float32),
            "rope": rope.astype(np.float32)}


def kernel(**inputs):
    import concourse.bacc as bacc
    from concourse.bass_utils import run_bass_kernel_spmd

    nc = bacc.Bacc("TRN2", target_bir_lowering=False, num_devices=1, dynamic_dma_scratch_size=1024)
    arrays, drams = {}, {}
    given = {name: np.ascontiguousarray(inputs[name]) for name in _INS}
    for name, a in list(given.items()) + list(_constants().items()):
        arrays[f"in_{name}"] = a
        drams[name] = nc.dram_tensor(f"in_{name}", a.shape, mybir.dt.from_np(a.dtype), kind="ExternalInput").ap()
    drams["out"] = nc.dram_tensor("out", (1, S, D), F32, kind="ExternalOutput").ap()
    build_program(nc, drams)
    result = run_bass_kernel_spmd(nc, [arrays], core_ids=[0])
    return result.results[0]["out"]
```

```python
from contextlib import ExitStack

import numpy as np
import concourse.bass as bass
from concourse import mybir

F32, F32R, BF16 = mybir.dt.float32, mybir.dt.float32r, mybir.dt.bfloat16
ALU, ACT, AX = mybir.AluOpType, mybir.ActivationFunctionType, mybir.AxisListType

P = 128
D = 1024
S = 1024
KD = D // P
NT = S // P
HALF = 512
N_MEM = 256
HD = 64
D_FF = 2816
NF = D_FF // P
EPS = 1e-6
BIG = 1.0e30
COL = dict(fq=0, fk=512, fv=1024, flog=1536, sq=1544, sk=2056, sv=2184, mq=2312, glog=2824)
FOX, SWA, MEM = 0, 1, 2


class Kit:

    sems = []

    def __init__(self, nc, stack):
        self.nc, self.stack = nc, stack

    def sb(self, name, shape, dtype=F32, side=None):
        return self.stack.enter_context(self.nc.sbuf_tensor(name, shape, dtype, side=side))

    def ps(self, name, shape, dtype=F32):
        return self.stack.enter_context(self.nc.psum_tensor(name, shape, dtype))

    def sem(self, name):
        made = self.nc.alloc_semaphore(name)
        Kit.sems.append(made)
        return made


def f32(ap):
    return ap.bitcast(F32)


def product(pe, out, a_hi, a_lo, b_hi, b_lo, start, stop):
    pe.matmul(out, a_hi, b_hi, start=start, stop=False)
    pe.matmul(out, a_hi, b_lo, start=False, stop=False)
    return pe.matmul(out, a_lo, b_hi, start=False, stop=stop)


class Weights:

    def __init__(self, kit, name, ring, width, raw, hi, lo):
        self.ring, self.width = ring, width
        self.raw, self.hi, self.lo = raw, hi, lo
        self.loaded = [kit.sem(f"{name}_loaded{i}") for i in range(ring)]
        self.hi_ready = kit.sem(f"{name}_hi_ready")
        self.lo_ready = kit.sem(f"{name}_lo_ready")

    def view(self, tile, slot, a=0, b=None):
        return tile[:, slot * self.width + a:slot * self.width + (self.width if b is None else b)]


class Projection:

    def __init__(self, kit, T, name, nb, turns, col, before=None):
        self.T, self.nb, self.turns, self.col, self.before = T, nb, turns, col, before
        self.groups = nb * 2 * KD
        self.W = Weights(kit, "w" + name, nb, D, T.w_raw, T.w_hi, T.w_lo)
        self.done = kit.sem(name + "_proj_done")
        self.kept = kit.sem(name + "_kept")
        self.rot_loaded = [kit.sem(f"{name}_rot_loaded{b}") for b in range(2 if name == "swa" else 0)]
        self.roped = kit.sem(name + "_roped")
        self.w_in = T.d["w_in"][0].rearrange("(k p) n -> p k n", p=P)

    def sems(self):
        return [self.done, self.kept, self.roped, *self.rot_loaded, *self.W.loaded, self.W.hi_ready, self.W.lo_ready]

    def last_use(self, turn, b):
        if isinstance(turn, int) and turn == 0:
            had = self.before
            return (had, (had.turns - 1) * had.nb + b + 1) if had and b < had.nb else (None, 0)
        return self, (turn - 1) * self.nb + (b + 1)

    def load(self, sp, turn, b):
        had, n = self.last_use(turn, b)
        if had:
            sp.wait_ge(had.W.lo_ready, n)
        sp.dma_start(self.W.view(self.W.raw, b).rearrange("p (k n) -> p k n", k=KD),
                     self.w_in[:, :, bass.ds(self.col(turn, b), P)]).then_inc(self.W.loaded[b], 16)

    def split_high(self, act, turn, b):
        W = self.W
        act.wait_ge(W.loaded[b], 16 * turn + 16)
        had, n = self.last_use(turn, b)
        if had:
            act.wait_ge(had.done, n * 2)
        act.activation(W.view(W.hi, b), W.view(W.raw, b), ACT.Copy).then_inc(W.hi_ready, 1)

    def split_low(self, dve, turn, b):
        W = self.W
        dve.wait_ge(W.hi_ready, turn * self.nb + b + 1)
        dve.tensor_tensor(W.view(W.lo, b), W.view(W.raw, b), f32(W.view(W.hi, b)),
                          ALU.subtract).then_inc(W.lo_ready, 1)

    def project(self, pe, turn, first, last):
        W, T = self.W, self.T
        if isinstance(turn, int) and turn == 0 and first == 0 < last and self.before:
            had = self.before
            if had.before:
                pe.wait_ge(had.kept, had.turns * 2 * had.nb + 2)
        for n in range(first, last):
            b, half, k = n // (2 * KD), (n // KD) % 2, n % KD
            if n % (2 * KD) == 0:
                pe.wait_ge(W.lo_ready, turn * self.nb + b + 1)
            if k == 0:
                pe.wait_ge(self.kept, turn * (2 * self.nb) + 2 * b + half + 1)
            cut, at = slice(P * k, P * (k + 1)), slice(HALF * half, HALF * (half + 1))
            mm = product(pe, T.proj_ps[:, half, :], W.view(W.hi, b)[:, cut], W.view(W.lo, b)[:, cut],
                         T.h_hi[:, k, at], T.h_lo[:, k, at], start=(k == 0), stop=(k == KD - 1))
            if k == KD - 1:
                mm.then_inc(self.done, 1)

    def keep(self, act, turn, n):
        act.wait_ge(self.done, turn * (2 * self.nb) + n + 1)
        act.activation(self.T.raw[:, n // 2, HALF * (n % 2):HALF * (n % 2 + 1)], self.T.proj_ps[:, n % 2, :],
                       ACT.Copy).then_inc(self.kept, 1)

    def swap_halves(self, sp, turn, b):
        raw, rot = self.T.raw, self.T.rot
        sp.wait_ge(self.kept, (turn * self.nb + b) * 2 + 2 + 2)
        for q in range(4):
            sp.dma_start(rot[32 * q:32 * q + 32, b, :], raw[32 * (q ^ 1):32 * (q ^ 1) + 32, b, :])\
                .then_inc(self.rot_loaded[b], 16)

    def rope(self, pool, turn, b):
        raw, rot = self.T.raw[:, b, :], self.T.rot[:, b, :]
        pool.wait_ge(self.rot_loaded[b], 64 * (turn + 1))
        pool.tensor_tensor(raw, raw, self.T.rope[:, 0, :], ALU.mult).then_inc(self.roped, 1)
        pool.tensor_tensor(rot, rot, self.T.rope[:, 1, :], ALU.mult).then_inc(self.roped, 1)
        pool.wait_ge(self.roped, (turn * self.nb + b) * 3 + 2)
        pool.tensor_tensor(raw, raw, rot, ALU.add).then_inc(self.roped, 1)


def normalise_stage(nc, T):
    with ExitStack() as stack:
        kit = Kit(nc, stack)
        nat = kit.sb("nat", [P, 4, D])
        normed = T.rot
        junk = T.raw[:, 0, :]
        gains = T.out_sb
        ssq = kit.sb("ssq", [P, 10])
        msq = kit.sb("msq", [P, 10])
        rstd = kit.sb("rstd", [P, 10])
        turned_ps = kit.ps("turned_ps", [P, 4, HALF])
        kv_ps = kit.ps("kv_ps", [P, 2, HALF])
        loaded = [kit.sem(f"nat_loaded{i}") for i in range(4)]
        consts_loaded = kit.sem("consts_loaded")
        g_loaded = [kit.sem("g_mem_loaded"), kit.sem("g_mix_pre_loaded")]
        squared, meaned, rooted, scaled = (kit.sem(n) for n in ("squared", "meaned", "rooted", "scaled"))
        turned, hi_done, lo_done = (kit.sem(n) for n in ("turned", "hi_done", "lo_done"))
        kv_done, kv_kept = kit.sem("kv_done"), kit.sem("kv_kept")
        bf_ready = kit.sem("bf_ready")
        half_set = kit.sem("half_set")
        W = Weights(kit, "wkv", 3, D, T.w_raw, T.w_hi, T.w_lo)
        coming = T.projection["shared"] = Projection(
            kit, T, "sh", 3, 1, lambda turn, b: (COL["flog"], COL["sk"], COL["sv"])[b])
        mem_hi, mem_lo = kit.sb("mem_hi", [P, KD, N_MEM], F32R), kit.sb("mem_lo", [P, KD, N_MEM], F32R)

        tiles = [(T.d["mem"][0, P * t:P * (t + 1), :], 0, mem_hi, mem_lo, t) for t in range(2)]
        tiles += [(T.d["x"][0, P * t:P * (t + 1), :], 1, T.h_hi, T.h_lo, t) for t in range(NT)]
        n_tiles = len(tiles)
        w_kv = T.d["w_mem_kv"][0].rearrange("(k p) n -> p k n", p=P)
        n_kv = 8

        block = stack.enter_context(nc.Block())

        @block.sync
        def _(sp):
            def load_w(n):
                if n >= 3:
                    sp.wait_ge(W.lo_ready, n - 2)
                sp.dma_start(W.view(W.raw, (n + 1) % 3).rearrange("p (k n) -> p k n", k=KD),
                             w_kv[:, :, P * n:P * (n + 1)]).then_inc(W.loaded[n % 3], 16)

            for t, (src, *_) in enumerate(tiles):
                if t >= 4:
                    sp.wait_ge(scaled, t - 3)
                sp.dma_start(nat[:, t % 4, :], src).then_inc(loaded[t % 4], 16)
                if t == 0:
                    sp.dma_start(gains[:, 0, :], T.d["g_mem"][0:1, :].to_broadcast([P, D])).then_inc(g_loaded[0], 16)
                    sp.dma_start(T.ident[:], T.d["ident"]).then_inc(consts_loaded, 16)
                if t == 2:
                    sp.dma_start(gains[:, 1, :], T.d["g_mix_pre"][0:1, :].to_broadcast([P, D])).then_inc(g_loaded[1], 16)
                if 1 <= t <= n_kv:
                    load_w(t - 1)
            sp.dma_start(T.masks[:], T.d["masks"]).then_inc(consts_loaded, 16)
            for b in range(3):
                sp.wait_ge(W.lo_ready, n_kv - 2 + b)
                coming.load(sp, 0, b)

        @block.scalar
        def _(act):
            def square(t):
                act.wait_ge(loaded[t % 4], 16 * (t // 4 + 1))
                if t >= 1:
                    act.wait_ge(squared, t)
                act.activation(junk[:], nat[:, t % 4, :], ACT.Square,
                               accum_out=ssq[:, t:t + 1]).then_inc(squared, 1)

            def split_w(n):
                act.wait_ge(W.loaded[n % 3], 16 * (n // 3 + 1))
                if n >= 3:
                    act.wait_ge(kv_done, n - 2)
                act.activation(W.view(W.hi, (n + 1) % 3), W.view(W.raw, (n + 1) % 3), ACT.Copy).then_inc(W.hi_ready, 1)

            def keep_kv(n):
                act.wait_ge(kv_done, n + 1)
                act.activation(T.mem_kv[:, n, :], kv_ps[:, n % 2, 0:N_MEM], ACT.Copy).then_inc(kv_kept, 1)

            square(0)
            square(1)
            for t, (_, _, hi, _, at) in enumerate(tiles):
                if t < n_kv:
                    split_w(t)
                if t + 2 < n_tiles:
                    square(t + 2)
                for b in range(2):
                    act.wait_ge(turned, 2 * t + b + 1)
                    act.activation(hi[:, 4 * b:4 * b + 4, P * at:P * (at + 1)],
                                   turned_ps[:, (2 * t + b) % 4, :].rearrange("p (c n) -> p c n", c=4),
                                   ACT.Copy).then_inc(hi_done, 1)
                if t >= n_kv:
                    act.wait_ge(kv_done, t - 2)
                    coming.split_high(act, 0, t - n_kv)
                if t >= 2:
                    keep_kv(t - 2)

        @block.gpsimd
        def _(pool):
            pool.memset(T.minus_half[:], -0.5).then_inc(half_set, 1)
            pool.wait_ge(half_set, 1)
            for t in range(n_tiles):
                pool.wait_ge(squared, t + 1)
                pool.tensor_scalar(msq[:, t:t + 1], ssq[:, t:t + 1], 1.0 / D, EPS,
                                   ALU.mult, ALU.add).then_inc(meaned, 1)
                pool.wait_ge(meaned, t + 1)
                pool.tensor_tensor(rstd[:, t:t + 1], msq[:, t:t + 1], T.minus_half[:], ALU.pow).then_inc(rooted, 1)

        @block.vector
        def _(dve):
            def scale(t):
                dve.wait_ge(rooted, t + 1)
                if t >= 2:
                    dve.wait_ge(turned, 2 * (t - 1))
                dve.wait_ge(g_loaded[tiles[t][1]], 16)
                dve.scalar_tensor_tensor(out=normed[:, t % 2, :], in0=nat[:, t % 4, :],
                                         scalar=rstd[:, t:t + 1], in1=gains[:, tiles[t][1], :],
                                         op0=ALU.mult, op1=ALU.mult).then_inc(scaled, 1)

            scale(0)
            for t, (_, _, hi, lo, at) in enumerate(tiles):
                if t < n_kv:
                    dve.wait_ge(W.hi_ready, t + 1)
                    dve.tensor_tensor(W.view(W.lo, (t + 1) % 3), W.view(W.raw, (t + 1) % 3), f32(W.view(W.hi, (t + 1) % 3)),
                                      ALU.subtract).then_inc(W.lo_ready, 1)
                if t + 1 < n_tiles:
                    scale(t + 1)
                for b in range(2):
                    dve.wait_ge(hi_done, 2 * t + b + 1)
                    cut = (slice(None), slice(4 * b, 4 * b + 4), slice(P * at, P * (at + 1)))
                    dve.tensor_tensor(lo[cut],
                                      turned_ps[:, (2 * t + b) % 4, :].rearrange("p (c n) -> p c n", c=4),
                                      f32(hi[cut]), ALU.subtract).then_inc(lo_done, 1)
                if t >= n_kv:
                    coming.split_low(dve, 0, t - n_kv)
            dve.wait_ge(consts_loaded, 32)
            dve.tensor_copy(T.ident_bf[:], T.ident[:]).then_inc(bf_ready, 1)
            dve.tensor_copy(T.masks_bf[:], T.masks[:]).then_inc(bf_ready, 1)

        @block.tensor
        def _(pe):
            def turn(t):
                pe.wait_ge(scaled, t + 1)
                for b in range(2):
                    n = 2 * t + b
                    if n >= 4:
                        pe.wait_ge(lo_done, n - 3)
                    for c in range(4):
                        mm = pe.transpose(turned_ps[:, n % 4, P * c:P * (c + 1)],
                                          normed[:, t % 2, P * (4 * b + c):P * (4 * b + c + 1)], T.ident[:])
                    mm.then_inc(turned, 1)

            def project_kv(n):
                pe.wait_ge(W.lo_ready, n + 1)
                if n >= 2:
                    pe.wait_ge(kv_kept, n - 1)
                for k in range(KD):
                    cut = slice(P * k, P * (k + 1))
                    mm = product(pe, kv_ps[:, n % 2, 0:N_MEM],
                                 W.view(W.hi, (n + 1) % 3)[:, cut], W.view(W.lo, (n + 1) % 3)[:, cut],
                                 mem_hi[:, k, :], mem_lo[:, k, :], start=(k == 0), stop=(k == KD - 1))
                mm.then_inc(kv_done, 1)

            pe.wait_ge(consts_loaded, 16)
            for t in range(n_tiles):
                turn(t)
                if t >= 2:
                    if t == 2:
                        pe.wait_ge(lo_done, 4)
                    project_kv(t - 2)


def shared_stage(nc, T):
    with ExitStack() as stack:
        kit = Kit(nc, stack)
        mine = T.projection["shared"]
        nb = mine.nb
        W, done = mine.W, mine.done
        mq = T.projection[MEM] = Projection(kit, T, "mem", 2, 2, lambda turn, b: COL["mq"] + (2 * turn + b) * P, mine)
        ps = kit.ps("shared_ps", [P, 2, 2, HALF])
        turn_ps = kit.ps("shared_turn_ps", [P, 2, HALF])
        nh = 8
        z, az, ez, sp_, lf, ones, cum, cum8 = (kit.sb(n, [nh, S]) for n in (
            "z", "abs_z", "exp_z", "softplus", "log_forget", "ones_row", "cum", "cum_scaled"))
        bias = kit.sb("forget_bias", [nh, 1])
        raw = T.rot
        rot = T.out_sb[:, 0, :]
        small_loaded = kit.sem("small_loaded")
        gate_act, gate_dve = kit.sem("gate_act"), kit.sem("gate_dve")
        cum_stored = kit.sem("cum_stored")
        kept = kit.sem("shared_kept")
        rot_loaded, roped = kit.sem("shared_rot_loaded"), kit.sem("shared_roped")
        mem_hi_done, mem_done = kit.sem("mem_hi_done"), kit.sem("mem_split_done")
        k_hi, k_done = kit.sem("swa_k_hi"), kit.sem("swa_k_done")
        turned, v_hi, v_done = kit.sem("shared_turned"), kit.sem("shared_v_hi"), kit.sem("shared_v_done")

        block = stack.enter_context(nc.Block())

        @block.sync
        def _(sp):
            sp.dma_start(bias[:], T.d["b_fgate"][0:1, :].rearrange("a h -> h a")).then_inc(small_loaded, 16)
            sp.dma_start(T.rope[:], T.d["rope"]).then_inc(small_loaded, 16)
            sp.dma_start(T.sink[:], T.d["sinks"][0:1, :].to_broadcast([P, nh])).then_inc(small_loaded, 16)
            for n in range(2):
                mq.load(sp, 0, n)
            sp.wait_ge(kept, 2)
            for q in range(4):
                sp.dma_start(rot[32 * q:32 * q + 32, :], raw[32 * (q ^ 1):32 * (q ^ 1) + 32, 0, :])\
                    .then_inc(rot_loaded, 16)
            sp.wait_ge(gate_dve, 5)
            sp.dma_start(T.cum_dram, cum8[:]).then_inc(cum_stored, 16)
            for n in range(2):
                mq.load(sp, 1, n)
            sp.wait_ge(cum_stored, 16)

        @block.scalar
        def _(act):
            act.sem_inc(mq.kept, 2)
            mine.split_high(act, 0, 2)
            act.activation(T.mk_hi[:], T.mem_kv[:, 0:4, :], ACT.Copy).then_inc(mem_hi_done, 1)
            for b in range(2):
                act.wait_ge(turned, b + 1)
                act.activation(T.mv_hi[:, 2 * b:2 * b + 2, :, :],
                               turn_ps[:, b, :].rearrange("p (h t d) -> p h t d", h=2, t=2),
                               ACT.Copy).then_inc(mem_hi_done, 1)
            act.wait_ge(done, 2)
            act.wait_ge(small_loaded, 48)
            zp = ps[0:nh, 0, :, :].rearrange("p a n -> p (a n)")
            act.activation(z[:], zp, ACT.Identity, bias=bias[:, 0:1]).then_inc(gate_act, 1)
            act.activation(az[:], zp, ACT.Abs, bias=bias[:, 0:1]).then_inc(gate_act, 1)
            act.wait_ge(gate_act, 2)
            act.activation(ez[:], az[:], ACT.Exp, scale=-1.0).then_inc(gate_act, 1)
            act.wait_ge(gate_act, 3)
            act.activation(sp_[:], ez[:], ACT.Ln, bias=1.0).then_inc(gate_act, 1)
            mq.split_high(act, 0, 0)
            for n in range(2):
                for h in range(2):
                    act.wait_ge(done, 2 * (n + 1) + h + 1)
                    act.activation(raw[:, n, HALF * h:HALF * (h + 1)], ps[:, 1 - n, h, :],
                                   ACT.Copy).then_inc(kept, 1)
                if n == 0:
                    mq.split_high(act, 0, 1)
            act.wait_ge(roped, 3)
            for kv in range(2):
                for half in range(2):
                    act.activation(T.k1[64 * half:64 * half + 64, kv, :], raw[64 * kv:64 * kv + 64, 0, :],
                                   ACT.Copy).then_inc(k_hi, 1)
            for b in range(2):
                act.wait_ge(turned, 2 + b + 1)
                act.activation(T.v[:, :, 4 * b:4 * b + 4, 0, :],
                               turn_ps[:, b, :].rearrange("p (t h d) -> p h t d", t=4, h=2),
                               ACT.Copy).then_inc(v_hi, 1)
            for n in range(4):
                mq.keep(act, 0, n)
                if n == 1:
                    mq.split_high(act, 1, 0)

        @block.vector
        def _(dve):
            mine.split_low(dve, 0, 2)
            dve.memset(ones[:], 1.0).then_inc(gate_dve, 1)
            dve.wait_ge(mem_hi_done, 1)
            dve.tensor_tensor(T.mk_lo[:], T.mem_kv[:, 0:4, :], f32(T.mk_hi[:]), ALU.subtract).then_inc(mem_done, 1)
            for b in range(2):
                dve.wait_ge(mem_hi_done, b + 2)
                dve.tensor_tensor(T.mv_lo[:, 2 * b:2 * b + 2, :, :],
                                  turn_ps[:, b, :].rearrange("p (h t d) -> p h t d", h=2, t=2),
                                  f32(T.mv_hi[:, 2 * b:2 * b + 2, :, :]), ALU.subtract).then_inc(mem_done, 1)
            dve.wait_ge(small_loaded, 48)
            dve.tensor_scalar(T.sink_raw[:], T.sink[:], 1.0 / T.scale[SWA], None, ALU.mult).then_inc(mem_done, 1)
            dve.wait_ge(gate_act, 4)
            dve.scalar_tensor_tensor(out=lf[:], in0=z[:], scalar=0.0, in1=sp_[:],
                                     op0=ALU.min, op1=ALU.subtract).then_inc(gate_dve, 1)
            dve.wait_ge(gate_dve, 2)
            dve.tensor_tensor_scan(cum[:], ones[:], lf[:], 0.0, ALU.mult, ALU.add).then_inc(gate_dve, 1)
            dve.wait_ge(gate_dve, 3)
            dve.tensor_scalar(cum8[:], cum[:], -1.0 / T.scale[FOX], None, ALU.mult).then_inc(gate_dve, 2)
            mq.split_low(dve, 0, 0)
            mq.split_low(dve, 0, 1)
            dve.wait_ge(rot_loaded, 64)
            dve.tensor_tensor(raw[:, 0, :], raw[:, 0, :], T.rope[:, 0, :], ALU.mult).then_inc(roped, 1)
            dve.tensor_tensor(rot[:], rot[:], T.rope[:, 1, :], ALU.mult).then_inc(roped, 1)
            dve.wait_ge(roped, 2)
            dve.tensor_tensor(raw[:, 0, :], raw[:, 0, :], rot[:], ALU.add).then_inc(roped, 1)
            for kv in range(2):
                dve.wait_ge(k_hi, 2 * kv + 2)
                rows = slice(64 * kv, 64 * kv + 64)
                for half in range(2):
                    dve.tensor_tensor(T.k2[64 * half:64 * half + 64, kv, :], raw[rows, 0, :],
                                      f32(T.k1[rows, kv, :]), ALU.subtract).then_inc(k_done, 1)
            for b in range(2):
                dve.wait_ge(v_hi, b + 1)
                dve.tensor_tensor(T.v[:, :, 4 * b:4 * b + 4, 1, :],
                                  turn_ps[:, b, :].rearrange("p (t h d) -> p h t d", t=4, h=2),
                                  f32(T.v[:, :, 4 * b:4 * b + 4, 0, :]), ALU.subtract).then_inc(v_done, 1)
            mq.split_low(dve, 1, 0)

        @block.tensor
        def _(pe):
            for b in range(2):
                for h in range(2):
                    for t in range(2):
                        at = P * (2 * h + t)
                        mm = pe.transpose(turn_ps[:, b, at:at + P],
                                          T.mem_kv[:, 4 + 2 * b + h, P * t:P * (t + 1)], T.ident[:])
                mm.then_inc(turned, 1)
            for n in range(nb):
                pe.wait_ge(W.lo_ready, n + 1)
                if n == 2:
                    pe.wait_ge(gate_act, 2)
                for h in range(2):
                    for k in range(KD):
                        cut = slice(P * k, P * (k + 1))
                        at = slice(HALF * h, HALF * (h + 1))
                        mm = product(pe, ps[:, n % 2, h, :], W.view(W.hi, n)[:, cut], W.view(W.lo, n)[:, cut],
                                     T.h_hi[:, k, at], T.h_lo[:, k, at], start=(k == 0), stop=(k == KD - 1))
                    mm.then_inc(done, 1)
            mq.project(pe, 0, 0, KD // 2)
            pe.wait_ge(kept, 4)
            pe.wait_ge(mem_done, 3)
            for b in range(2):
                for t in range(4):
                    at = P * (4 * b + t)
                    mm = pe.transpose(turn_ps[:, b, P * t:P * (t + 1)], raw[:, 1, at:at + P], T.ident[:])
                mm.then_inc(turned, 1)
            mq.project(pe, 0, KD // 2, mq.groups)


EARLY_GATES = 2
START = {FOX: 3, SWA: 3, MEM: 1}
START_FIRST = {SWA: 5, MEM: 3}


def attention_stage(nc, T, branch):
    name = ("fox", "swa", "mem")[branch]
    scale = T.scale[branch]
    turns = {FOX: 4, SWA: 2, MEM: 2}[branch]
    nb = {FOX: 3, SWA: 2, MEM: 2}[branch]
    heads = {FOX: 2, SWA: 4, MEM: 2}[branch]
    chunks = {FOX: 1, SWA: 2, MEM: 2}[branch]
    units = [(a, g) for a in range(heads) for g in range(NT // 2)]
    NU = len(units)
    NQ = 2 * NU

    def keys(i):
        return {FOX: (0, i + 1), SWA: (max(i - 1, 0), i + 1), MEM: (0, 2)}[branch]

    def key_packs(g):
        out, packs = [], [[]]
        for j in range(keys(2 * g)[0], keys(2 * g + 1)[1]):
            sees = [keys(2 * g + q)[0] <= j < keys(2 * g + q)[1] for q in range(2)]
            out.append((j, 0 if sees[0] else P, 2 * P if sees[1] else P))
        for j, a, b in sorted(out, key=lambda x: x[2] - x[1] < 2 * P):
            used = packs[-1][-1][3] + packs[-1][-1][2] - packs[-1][-1][1] if packs[-1] else 0
            if used + b - a > HALF:
                packs.append([])
                used = 0
            packs[-1].append((j, a, b, used))
        return packs

    packs = [key_packs(g) for _, g in units]
    first_pack = [sum(len(x) for x in packs[:u]) for u in range(NU + 1)]
    NS = first_pack[NU]
    width_of = lambda pack: pack[-1][3] + pack[-1][2] - pack[-1][1]
    widths = [[P * (keys(2 * g + q)[1] - keys(2 * g + q)[0]) for q in range(2)] for _, g in units]
    if branch == FOX:
        pieces = [[(q, c, min(HALF, w[q] - c), n, 0) for n, (q, c) in
                   enumerate((q, c) for q in range(2) for c in range(0, w[q], HALF))] for w in widths]
    else:
        pieces = [[(q, 0, w[q], 0, 2 * P * q) for q in range(2)] for w in widths]
    banks_of = [x[-1][3] + 1 for x in pieces]
    maxima_of = [len(x) if branch == FOX or w[0] != w[1] else 1 for x, w in zip(pieces, widths)]
    first_bank = [sum(banks_of[:n]) for n in range(NU + 1)]
    first_max = [sum(maxima_of[:n]) for n in range(NU + 1)]
    NB, NM = first_bank[NU], first_max[NU]
    RS = 3
    STEPS = NU + 4
    SPLIT_T = NU
    PROBS = 3
    bank = lambda it, n: (n if branch == FOX else it * NB + n) % RS
    unit_of_chunk = NU // chunks

    places = 2 * (NU + 2)

    def plan(n_blocks, it=None):
        start_groups = START_FIRST[branch] if isinstance(it, int) and it == 0 else START[branch]
        left = n_blocks * 2 * KD - start_groups
        fill_at = [start_groups + (left * p) // places for p in range(places + 1)]
        split_before = {b: max(0, next(t for t in range(STEPS) if fill_at[2 * t + 2] > 2 * KD * b) - 2)
                        for b in range(n_blocks)}
        return fill_at, split_before

    def halves_by(fill_at, t):
        return fill_at[min(2 * t, places)] // KD

    step_with = lambda n: next(t for t in range(STEPS) if halves_by(plan(nb)[0], t) >= n)
    early_at = {FOX: step_with(4), SWA: max(step_with(2) + 5, NU // 2), MEM: max(step_with(2), NU // 2)}[branch]
    parts = 1 if branch == MEM else 2
    late_at = {FOX: 0, SWA: 4, MEM: 1}[branch]

    with ExitStack() as stack:
        kit = Kit(nc, stack)
        own = T.projection[branch]
        kept, raw, roped = own.kept, T.raw, own.roped
        coming = None
        if branch == MEM:
            coming = T.projection[SWA] = Projection(kit, T, "swa", 2, 2,
                                                    lambda turn, b: COL["sq"] + (2 * turn + b) * P, own)
        if branch == SWA:
            coming = T.projection[FOX] = Projection(
                kit, T, "fox", 3, 4, lambda turn, b: turn * P + (COL["fq"], COL["fk"], COL["fv"])[b], own)
        if branch == FOX:
            T.merge_weights = MergeWeights(kit, T)
            coming = T.projection["gate"] = Projection(
                kit, T, "gate", EARLY_GATES, 1, lambda turn, b: COL["glog"] + b * P, own)
        prob = kit.sb(name + "_prob", [P, PROBS, 2, S if branch == FOX else 2 * P])
        n_packs = max(len(x) for x in packs)
        pt_hi = kit.sb(name + "_pt_hi", [P, 2, n_packs, HALF], F32R)
        pt_lo = kit.sb(name + "_pt_lo", [P, 2, n_packs, HALF], F32R)
        out_sb = T.out_sb
        tmp = kit.sb(name + "_tmp", [64, 2, 2 * P]) if branch != MEM else None
        neg, den, den2, inv, esink = (kit.sb(f"{name}_{n}", [P, 2, 2]) for n in
                                      ("neg", "den", "den2", "inv", "esink"))
        top = kit.sb(name + "_top", [P, 2, 2, 2])
        top2 = kit.sb(name + "_top2", [P, 2, 2])
        if branch == MEM:
            q_hi, q_lo = (kit.sb("mem_" + n, [P, heads, S], F32R) for n in ("q_hi", "q_lo"))
            k_hi, k_lo, v_hi, v_lo = T.mk_hi, T.mk_lo, T.mv_hi, T.mv_lo
        else:
            q_both = kit.sb(name + "_q", [P, heads, S], F32R)
        if branch == SWA:
            k1, k2, v = T.k1, T.k2, T.v
        if branch == FOX:
            k1 = kit.sb("fox_k1", [P, 2, S], F32R)
            k2 = kit.sb("fox_k2", [P, S], F32R)
            v = kit.sb("fox_v", [P, 2, NT, 2, HD], F32R)
            cum_b = kit.sb("fox_cum", [P, 2, S])
        score_ps = kit.ps(name + "_score_ps", [P, RS, HALF])
        turn_ps = kit.ps(name + "_turn_ps", [P, 2, HALF])
        out_ps = kit.ps(name + "_out_ps", [P, HALF])

        act_unpacked = kit.sem(name + "_act_unpacked")
        low_unpacked = kit.sem(name + "_low_unpacked")
        v_hi_done = kit.sem(name + "_v_hi_done")
        v_lo_done = kit.sem(name + "_v_lo_done")
        v_turned = kit.sem(name + "_v_turned")
        scored = kit.sem(name + "_scored")
        maxed = kit.sem(name + "_maxed")
        topped = kit.sem(name + "_topped")
        negated = kit.sem(name + "_negated")
        exped = kit.sem(name + "_exped")
        sunk = kit.sem(name + "_sunk")
        summed = kit.sem(name + "_summed")
        inverted = kit.sem(name + "_inverted")
        normed = kit.sem(name + "_normed")
        turned = kit.sem(name + "_turned")
        pt_hi_done = kit.sem(name + "_pt_hi_done")
        pt_lo_done = kit.sem(name + "_pt_lo_done")
        pv_done = kit.sem(name + "_pv_done")
        lower_kept = kit.sem(name + "_lower_kept")
        out_done = kit.sem(name + "_out_done")
        stored = [kit.sem(f"{name}_stored{c}") for c in range(chunks)]
        cum_loaded = [kit.sem(f"{name}_cum_loaded{a}") for a in range(2)]
        waited = kit.sem(name + "_waited")
        kept_seen = kit.sem(name + "_kept_seen")
        ACT_EARLY, LOW_EARLY = {FOX: (2, 3), SWA: (2, 2), MEM: (1, 1)}[branch]
        ACT_U, LOW_U = 2 * ACT_EARLY, 2 * LOW_EARLY
        out_dram = T.out_dram[branch]

        if branch == FOX:
            nc.clear_and_free_semaphores(T.spent)
        block = stack.enter_context(nc.Block())

        def over_turns(engine, body):
            if turns > 2:
                with engine.Fori(0, turns - 2) as it:
                    body(it, own, it + 1, own, it + 2)
            body(turns - 2, own, turns - 1, coming, 0)
            body(turns - 1, coming, 0, coming if coming.turns > 1 else None, 1)

        @block.sync
        def _(sp):
            for c in range(chunks):
                sp.sem_inc(stored[c], 1)

            def load_cum(turn, a, wait):
                sp.wait_ge(maxed, wait)
                sp.dma_start(cum_b[:, a, :], T.cum_dram[bass.ds(turn * 2 + a, 1), :].to_broadcast([P, S]))\
                    .then_inc(cum_loaded[a], 16)

            def body(it, nxt, turn, later, later_turn):
                if branch == FOX:
                    load_cum(it, 1, it * NM + RS)
                if branch == SWA:
                    own.swap_halves(sp, it, 1)
                for b in range(later.nb if later else 0):
                    later.load(sp, later_turn, b)
                    if b == 1 and nxt.rot_loaded:
                        nxt.swap_halves(sp, turn, 0)
                if branch == FOX and nxt is own:
                    load_cum(turn, 0, it * NM + first_max[NU // 2] + RS)
                if branch == FOX and nxt is coming:
                    sp.wait_ge(coming.W.lo_ready, EARLY_GATES)
                    for slot in range(2):
                        T.merge_weights.load_first(sp, slot)
                for c in range(chunks):
                    sp.wait_ge(out_done, it * NU + (c + 1) * unit_of_chunk + 1)
                    sp.dma_start(out_dram[bass.ds(P * (it * chunks + c), P), :], out_sb[:, c, :])\
                        .then_inc(stored[c], 16)

            if branch == FOX:
                load_cum(0, 0, RS)
            over_turns(sp, body)
        @block.scalar
        def _(act):
            if coming:
                act.sem_inc(coming.kept, 2)
            act.sem_inc(exped, 2 * RS)

            def unpack(it, c, part):
                if c == 1:
                    act.wait_ge(scored, it * NB + 1)
                rows, swapped = slice(64 * c, 64 * c + 64), slice(64 - 64 * c, P - 64 * c)
                if branch == FOX:
                    act.wait_ge(kept, it * 2 * nb + 2 * part + 2 + 2)
                    if part == 0:
                        act.activation(q_both[rows, c, :], raw[rows, 0, :], ACT.Copy).then_inc(act_unpacked, 1)
                    else:
                        act.activation(k1[swapped, c, :], raw[rows, 1, :], ACT.Copy).then_inc(act_unpacked, 1)
                if branch == SWA:
                    act.wait_ge(roped, (it * nb + c + 1) * 3)
                    mine = slice(64 * part, 64 * part + 64)
                    act.activation(q_both[mine, 2 * c + part, :], raw[mine, c, :],
                                   ACT.Copy).then_inc(act_unpacked, 1)
                if branch == MEM:
                    act.wait_ge(kept, (it * nb + c) * 2 + 2 + 2)
                    act.activation(q_hi[:, c, :], raw[:, c, :], ACT.Copy).then_inc(act_unpacked, 1)

            def unpack_values(it):
                act.wait_ge(pv_done, it * NU + 1)
                for b in range(2):
                    act.wait_ge(v_turned, it * 2 + b + 1)
                    act.activation(v[:, :, 4 * b:4 * b + 4, 0, :],
                                   turn_ps[:, b, :].rearrange("p (t h d) -> p h t d", t=4, h=2),
                                   ACT.Copy).then_inc(v_hi_done, 1)

            def exp(it, u):
                act.wait_ge(negated, it * NU + u + 1)
                for q in range(2):
                    i = 2 * units[u][1] + q
                    nk = P * (keys(i)[1] - keys(i)[0])
                    p = prob[:, u % PROBS, q, 0:nk]
                    n, c = bank(it, first_bank[u]), 2 * P * q
                    act.activation(p, p if branch == FOX else score_ps[:, n, c:c + nk], ACT.Exp,
                                   bias=neg[:, u % 2, q:q + 1], scale=scale,
                                   accum_out=den[:, u % 2, q:q + 1]).then_inc(exped, 1)
                if branch == SWA:
                    head = heads * it + units[u][0]
                    act.activation(esink[:, u % 2, :], neg[:, u % 2, :], ACT.Exp,
                                   bias=T.sink[:, head:head + 1]).then_inc(sunk, 1)

            def split_hi(it, u):
                for s, pack in enumerate(packs[u]):
                    n, w = first_pack[u] + s, width_of(pack)
                    act.wait_ge(turned, it * NS + n + 1)
                    act.activation(pt_hi[:, u % 2, s, 0:w], turn_ps[:, n % 2, 0:w], ACT.Copy).then_inc(pt_hi_done, 1)

            def keep_lower(it, u):
                if branch != MEM:
                    act.wait_ge(pv_done, it * NU + u + 2)
                    act.activation(tmp[:, u % 2, :], out_ps[64:P, 0:2 * P], ACT.Copy).then_inc(lower_kept, 1)

            def body(it, nxt, turn, later, later_turn):
                fill_at, split_before = plan(nxt.nb, it)
                kept_halves = 0
                for t in range(STEPS):
                    if t >= 4:
                        keep_lower(it, t - 4)
                    for b in range(1, nxt.nb):
                        if split_before[b] == t:
                            nxt.split_high(act, turn, b)
                    if 2 <= t < NU + 2:
                        split_hi(it, t - 2)
                    if t < NU:
                        exp(it, t)
                    if branch == FOX and t == 0:
                        unpack_values(it)
                    for part in range(parts):
                        if t == late_at + part:
                            unpack(it, 1, part)
                    while kept_halves < halves_by(fill_at, t):
                        if kept_halves == 0:
                            act.wait_ge(low_unpacked, it * LOW_U + (LOW_U if branch == FOX else LOW_EARLY))
                        if kept_halves == 2:
                            act.wait_ge(low_unpacked, it * LOW_U + LOW_U)
                        nxt.keep(act, turn, kept_halves)
                        kept_halves += 1
                    for part in range(parts):
                        if t == early_at + part and nxt is own:
                            unpack(turn, 0, part)
                    if t == SPLIT_T and later:
                        later.split_high(act, later_turn, 0)

            for part in range(parts):
                unpack(0, 0, part)
            over_turns(act, body)

        def unpack_low(engine, it, c, part):
            def low(out, whole, high):
                engine.tensor_tensor(out, whole, f32(high), ALU.subtract).then_inc(low_unpacked, 1)

            rows, swapped = slice(64 * c, 64 * c + 64), slice(64 - 64 * c, P - 64 * c)
            if c == 1 and part == 0:
                engine.wait_ge(scored, it * NB + 1)
                engine.wait_ge(low_unpacked, it * LOW_U + LOW_EARLY)
            if branch == FOX and part == 0:
                engine.wait_ge(act_unpacked, it * ACT_U + 2 * c + 1)
                low(q_both[swapped, c, :], raw[rows, 0, :], q_both[rows, c, :])
            if branch == FOX and part == 1:
                engine.wait_ge(kept, it * 2 * nb + 4 + 2)
                engine.sem_inc(kept_seen, 1)
                engine.tensor_copy(k1[rows, c, :], raw[rows, 1, :]).then_inc(low_unpacked, 1)
                engine.wait_ge(low_unpacked, it * LOW_U + (LOW_EARLY * c + 2))
                low(k2[rows, :], raw[rows, 1, :], k1[rows, c, :])
            if branch == SWA:
                mine, other = slice(64 * part, 64 * part + 64), slice(64 - 64 * part, P - 64 * part)
                engine.wait_ge(act_unpacked, it * ACT_U + 2 * c + part + 1)
                low(q_both[other, 2 * c + part, :], raw[mine, c, :], q_both[mine, 2 * c + part, :])
            if branch == MEM:
                engine.wait_ge(act_unpacked, it * ACT_U + c + 1)
                low(q_lo[:, c, :], raw[:, c, :], q_hi[:, c, :])

        @block.vector
        def _(dve):
            dve.sem_inc(maxed, RS)
            dve.sem_inc(pt_lo_done, 2)
            dve.sem_inc(out_done, 1)

            def unpack_values(it):
                for b in range(2):
                    dve.wait_ge(v_hi_done, it * 2 + b + 1)
                    dve.tensor_tensor(v[:, :, 4 * b:4 * b + 4, 1, :],
                                      turn_ps[:, b, :].rearrange("p (t h d) -> p h t d", t=4, h=2),
                                      f32(v[:, :, 4 * b:4 * b + 4, 0, :]), ALU.subtract).then_inc(v_lo_done, 1)

            def maxima(it, u):
                a, g = units[u]
                tops = top[:, u % 2, :, 0]
                if branch == FOX:
                    if g == 0:
                        dve.wait_ge(cum_loaded[a], 16 * it + 16)
                    for n, (q, c, w, b, _) in enumerate(pieces[u]):
                        dve.wait_ge(scored, it * NB + first_bank[u] + n + 2)
                        dve.sem_inc(waited, 1)
                        dve.tensor_tensor_reduce(prob[:, u % PROBS, q, c:c + w],
                                                 score_ps[:, bank(it, first_bank[u] + b), 0:w],
                                                 cum_b[:, a, c:c + w], 1.0, -3.0e38, ALU.add, ALU.max,
                                                 top[:, u % 2, q, c // HALF:c // HALF + 1]).then_inc(maxed, 1)
                else:
                    dve.wait_ge(scored, it * NB + u + 2)
                    ps = score_ps[:, bank(it, u), :].rearrange("p (q n) -> p q n", q=2)
                    if maxima_of[u] == 1:
                        dve.reduce_max(tops, ps, AX.X).then_inc(maxed, 1)
                    else:
                        for q in range(2):
                            dve.reduce_max(top[:, u % 2, q, 0:1], ps[:, q, 0:widths[u][q]], AX.X).then_inc(maxed, 1)
                dve.wait_ge(maxed, it * NM + first_max[u + 1] + RS)
                if widths[u][0] > HALF:
                    dve.tensor_tensor(top2[:, u % 2, :], top[:, u % 2, :, 0], top[:, u % 2, :, 1],
                                      ALU.max).then_inc(topped, 1)
                    two = [w[0] > HALF for w in widths]
                    dve.wait_ge(topped, it * sum(two) + sum(two[:u + 1]))
                    tops = top2[:, u % 2, :]
                if branch == SWA:
                    head = heads * it + a
                    dve.tensor_scalar(neg[:, u % 2, :], tops, T.sink_raw[:, head:head + 1], -scale,
                                      ALU.max, ALU.mult).then_inc(negated, 1)
                else:
                    dve.tensor_scalar(neg[:, u % 2, :], tops, -scale, None, ALU.mult).then_inc(negated, 1)

            def normalise(it, u):
                dve.wait_ge(exped, it * NQ + 2 * u + 2 + 2 * RS)
                total = den
                if branch == SWA:
                    dve.wait_ge(sunk, it * NU + u + 1)
                    dve.tensor_tensor(den2[:, u % 2, :], den[:, u % 2, :], esink[:, u % 2, :],
                                      ALU.add).then_inc(summed, 1)
                    dve.wait_ge(summed, it * NU + u + 1)
                    total = den2
                dve.reciprocal(inv[:, u % 2, :], total[:, u % 2, :]).then_inc(inverted, 1)
                dve.wait_ge(inverted, it * NU + u + 1)
                for q in range(2):
                    i = 2 * units[u][1] + q
                    nk = P * (keys(i)[1] - keys(i)[0])
                    p = prob[:, u % PROBS, q, 0:nk]
                    dve.tensor_scalar(p, p, inv[:, u % 2, q:q + 1], None, ALU.mult).then_inc(normed, 1)

            def split_lo(it, u):
                for s, pack in enumerate(packs[u]):
                    n, w = first_pack[u] + s, width_of(pack)
                    dve.wait_ge(pt_hi_done, it * NS + n + 1)
                    dve.tensor_tensor(pt_lo[:, u % 2, s, 0:w], turn_ps[:, n % 2, 0:w], f32(pt_hi[:, u % 2, s, 0:w]),
                                      ALU.subtract).then_inc(pt_lo_done, 1)

            def keep_out(it, u):
                a, g = units[u]
                at = slice(2 * P * g, 2 * P * (g + 1))
                chunk = u // unit_of_chunk
                if u % unit_of_chunk == 0:
                    dve.wait_ge(stored[chunk], 16 * it + 1)
                    if isinstance(it, int) and it == 0 and T.stores:
                        dve.wait_ge(*T.stores[chunk])
                if branch == MEM:
                    dve.wait_ge(pv_done, it * NU + u + 2)
                    dve.tensor_copy(out_sb[:, chunk, at], out_ps[:, 0:2 * P]).then_inc(out_done, 1)
                else:
                    dve.wait_ge(lower_kept, it * NU + u + 1)
                    rows = slice(64 * (a % 2), 64 * (a % 2) + 64)
                    dve.tensor_tensor(out_sb[rows, chunk, at], out_ps[0:64, 0:2 * P], tmp[:, u % 2, :],
                                      ALU.add).then_inc(out_done, 1)

            def body(it, nxt, turn, later, later_turn):
                split_before = plan(nxt.nb, it)[1]
                for t in range(STEPS):
                    if t >= 4:
                        keep_out(it, t - 4)
                    if t < NU:
                        maxima(it, t)
                    for b in range(1, nxt.nb):
                        if split_before[b] == t:
                            nxt.split_low(dve, turn, b)
                    if 2 <= t < NU + 2:
                        split_lo(it, t - 2)
                    if branch == FOX and t == 0:
                        unpack_values(it)
                    if 1 <= t <= NU:
                        normalise(it, t - 1)
                    for part in range(parts):
                        if t == late_at + part and branch == MEM:
                            unpack_low(dve, it, 1, part)
                        if t == early_at + part and nxt is own and branch == MEM:
                            unpack_low(dve, turn, 0, part)
                    if t == SPLIT_T and later:
                        later.split_low(dve, later_turn, 0)

            for part in range(parts):
                unpack_low(dve, 0, 0, part)
            if branch == FOX:
                dve.wait_ge(*T.stores[0])
            over_turns(dve, body)

        @block.gpsimd
        def _(pool):
            if branch == SWA:
                for turn, c in ((0, 1), (1, 0), (1, 1)):
                    if turn:
                        pool.wait_ge(low_unpacked, turn * LOW_U + LOW_EARLY * c)
                    own.rope(pool, turn, c)
                    for part in range(parts):
                        unpack_low(pool, turn, c, part)
            if branch == MEM:
                coming.rope(pool, 0, 0)
            if branch == FOX:
                with pool.Fori(0, turns - 1) as it:
                    for turn, c in ((it, 1), (it + 1, 0)):
                        for part in range(parts):
                            unpack_low(pool, turn, c, part)
                for part in range(parts):
                    unpack_low(pool, turns - 1, 1, part)

        @block.tensor
        def _(pe):
            pe.sem_inc(scored, 1)
            pe.sem_inc(pv_done, 1)

            def turn_values(it):
                pe.wait_ge(kept, (it + 1) * 2 * nb + 2)
                pe.wait_ge(pt_lo_done, it * NS + 2)
                for b in range(2):
                    for t in range(4):
                        mm = pe.transpose(turn_ps[:, b, P * t:P * (t + 1)],
                                          raw[:, 2, P * (4 * b + t):P * (4 * b + t + 1)], T.ident[:])
                    mm.then_inc(v_turned, 1)

            def scores(it, u):
                a, g = units[u]
                if u == 0:
                    pe.wait_ge(act_unpacked, it * ACT_U + ACT_EARLY)
                    pe.wait_ge(low_unpacked, it * LOW_U + LOW_EARLY)
                if u == NU // 2:
                    pe.wait_ge(act_unpacked, it * ACT_U + ACT_U)
                    pe.wait_ge(low_unpacked, it * LOW_U + LOW_U)
                if branch != FOX:
                    pe.wait_ge(exped, it * NQ + 2 * u + 2)
                for q, c, w, b, to in pieces[u]:
                    k0 = keys(2 * g + q)[0]
                    cut = slice(P * (2 * g + q), P * (2 * g + q + 1))
                    at = slice(P * k0 + c, P * k0 + c + w)
                    n = first_bank[u] + b
                    if branch == FOX:
                        pe.wait_ge(maxed, it * NM + n + 1)
                    ps = score_ps[:, bank(it, n), :]
                    out = ps[:, to:to + w]
                    last = c + w == widths[u][q]
                    if branch == MEM:
                        head = heads * it + a
                        mm = product(pe, out, q_hi[:, a, cut], q_lo[:, a, cut], k_hi[:, head, at],
                                     k_lo[:, head, at], start=True, stop=True)
                    else:
                        rows = slice(64 * (a % 2), 64 * (a % 2) + 64)
                        kk1, kk2 = (k1[:, a, at], k2[rows, at]) if branch == FOX else \
                                   (k1[:, it, at], k2[rows, it, at])
                        pe.matmul(out, q_both[:, a, cut], kk1, start=True, stop=False)
                        mm = pe.matmul(out, q_both[rows, a, cut], kk2, start=False, stop=not last)
                        if last:
                            band = P if branch == FOX else w
                            mask = T.masks_bf[:, 0:P] if branch == FOX else T.masks_bf[:, 3 * P - w:3 * P]
                            mm = pe.matmul(ps[:, to + w - band:to + w], T.ident_bf[:], mask,
                                           start=False, stop=True)
                    if branch == FOX or q == 1:
                        mm.then_inc(scored, 1)

            def transposes(it, u, first, last):
                g = units[u][1]
                if first == 0:
                    pe.wait_ge(normed, it * NQ + 2 * u + 2)
                for s, pack in list(enumerate(packs[u]))[first:last]:
                    n = first_pack[u] + s
                    pe.wait_ge(pt_lo_done, it * NS + n + 1)
                    for j, a, b, to in pack:
                        for q in range(a // P, b // P):
                            at = P * (j - keys(2 * g + q)[0])
                            c = to + P * q - a
                            mm = pe.transpose(turn_ps[:, n % 2, c:c + P], prob[:, u % PROBS, q, at:at + P],
                                              T.ident[:])
                    mm.then_inc(turned, 1)

            def outputs(it, u):
                head = units[u][0]
                if u == 0 and branch == FOX:
                    pe.wait_ge(v_lo_done, it * 2 + 2)
                pe.wait_ge(out_done, it * NU + u + 1)
                pe.wait_ge(pt_lo_done, it * NS + first_pack[u + 1] + 2)
                parts = [(s, *part) for s, pack in enumerate(packs[u]) for part in pack]
                for s, j, a, b, to in parts:
                    first, last = (s, j, a, b, to) == parts[0], (s, j, a, b, to) == parts[-1]
                    out, hi, lo = out_ps[:, a:b], pt_hi[:, u % 2, s, to:to + b - a], pt_lo[:, u % 2, s, to:to + b - a]
                    if branch == MEM:
                        mm = product(pe, out, v_hi[:, heads * it + head, j, :], v_lo[:, heads * it + head, j, :],
                                     hi, lo, start=first, stop=last)
                    else:
                        vv = v[:, head if branch == FOX else it, j, :, :].rearrange("p a d -> p (a d)")
                        pe.matmul(out, vv, hi, start=first, stop=False)
                        mm = pe.matmul(out, vv, lo, start=False, stop=last)
                mm.then_inc(pv_done, 1)

            def body(it, nxt, turn, *_):
                fill_at = plan(nxt.nb, it)[0]
                nxt.project(pe, turn, 0, fill_at[0])
                scores(it, 0)
                if branch == FOX:
                    turn_values(it)
                for t in range(STEPS - 1):
                    if 2 <= t < NU + 2:
                        transposes(it, t - 2, 0, 2)
                    if t < NU + 2:
                        nxt.project(pe, turn, fill_at[2 * t], fill_at[2 * t + 1])
                    if 2 <= t < NU + 2:
                        transposes(it, t - 2, 2, None)
                    if t >= 3:
                        outputs(it, t - 3)
                    if t < NU + 2:
                        nxt.project(pe, turn, fill_at[2 * t + 1], fill_at[2 * t + 2])
                    if t + 1 < NU:
                        scores(it, t + 1)

            over_turns(pe, body)
    T.stores = [(sem, 16 * turns + 1) for sem in stored] + T.stores


def merge_stage(nc, T):
    with ExitStack() as stack:
        kit = Kit(nc, stack)
        NJ = KD
        W = T.merge_weights
        o_hi, o_lo = (kit.sb(n, [P, 2, KO, S], F32R) for n in ("branch_hi", "branch_lo"))
        o_raw = T.raw[:, EARLY_GATES, :]
        gate, term = (T.out_sb[:, i, :].rearrange("p (h n) -> p h n", h=2) for i in range(2))
        bias = kit.sb("gate_bias", [P, 3 * NJ])
        gate_ps, y_ps = kit.ps("gate_ps", [P, 2, HALF]), kit.ps("y_ps", [P, 2, HALF])
        bias_loaded = kit.sem("gate_bias_loaded")
        first_loaded = [kit.sem(f"branch0_loaded{c}") for c in range(KO)]
        raw_loaded = kit.sem("branch_raw_loaded")
        o_hi_done, o_lo_done = kit.sem("branch_hi_done"), kit.sem("branch_lo_done")
        first_hi_done, first_lo_done = kit.sem("branch0_hi_done"), kit.sem("branch0_lo_done")
        gate_done = kit.sem("gate_done")
        y_done = kit.sem("y_done")
        waited = kit.sem("merge_waited")
        gated = kit.sem("gated")
        weighted = kit.sem("weighted")
        summed = kit.sem("merged_summed")
        w_in = T.d["w_in"][0].rearrange("(k p) n -> p k n", p=P)
        w_o = W.w_o

        T.w_out_loaded = [kit.sem(f"w_out_loaded{i}") for i in range(3)]

        block = stack.enter_context(nc.Block())

        @block.sync
        def _(sp):
            def load(b, j, s, n):
                if n is not None:
                    sp.wait_ge(W.lo_ready, n - 1)
                sp.dma_start(W.view(W.raw, s, 0, KD * P).rearrange("p (k n) -> p k n", k=KD),
                             w_in[:, :, bass.ds(j * P + (COL["glog"] + b * D), P)]).then_inc(W.loaded[s], 16)
                sp.dma_start(W.view(W.raw, s, KD * P).rearrange("p (k n) -> p k n", k=KO),
                             w_o[b][:, :, bass.ds(j * P, P)]).then_inc(W.loaded[s], 16)

            def load_pair(b, it):
                for s in range(2):
                    load(b, it * 2 + s, s, it * 2 + (b * NJ + s))
                if b < 2:
                    sp.wait_ge(o_lo_done, it + b * KO)
                    sp.dma_start(o_raw[:], T.out_dram[b + 1][bass.ds(it * P, P), :]).then_inc(raw_loaded, 16)

            fox_stored = T.stores[0][0]
            for c in range(KO):
                sp.wait_ge(fox_stored, 16 * (c + 1) + 1)
                sp.dma_start(T.merged[:, c, :], T.out_dram[0][P * c:P * (c + 1), :]).then_inc(first_loaded[c], 16)
            sp.dma_start(bias[:], T.d["b_branch"][0].rearrange("(n p) -> p n", p=P),
                         allow_slow_non_contiguous=True).then_inc(bias_loaded, 16)
            for store in T.stores:
                sp.wait_ge(*store)
            sp.dma_start(o_raw[:], T.out_dram[1][0:P, :]).then_inc(raw_loaded, 16)
            with sp.Fori(1, NJ // 2) as it:
                load_pair(0, it)
            for b in (1, 2):
                with sp.Fori(0, NJ // 2) as it:
                    load_pair(b, it)
            sp.wait_ge(W.lo_ready, 3 * NJ)
            for j in range(3):
                sp.dma_start(T.w_raw[:, D * j:D * (j + 1)], T.d["w_out"][0, P * j:P * (j + 1), :])\
                    .then_inc(T.w_out_loaded[j], 16)

        @block.scalar
        def _(act):
            def split_w(s, n, first=0):
                act.wait_ge(W.loaded[s], n * 16 + (32 - 16 * s))
                act.activation(W.view(W.hi, s, first), W.view(W.raw, s, first), ACT.Copy).then_inc(W.hi_ready, 1)

            def early_step(s):
                if s == 1:
                    act.wait_ge(y_done, 4)
                    split_w(0, 2)
                for h in range(2):
                    act.wait_ge(weighted, s * 2 + h + 1)
                    act.activation(gate[:, h, :], T.raw[:, s, HALF * h:HALF * (h + 1)], ACT.Sigmoid,
                                   bias=bias[:, s:s + 1]).then_inc(gated, 1)

            def step(b, it, s, more):
                n = it * 2 + (b * NJ + s)
                if more:
                    act.wait_ge(y_done, n * 2 + 2)
                    split_w(1 - s, n + 1)
                for h in range(2):
                    act.wait_ge(gate_done, n * 2 + (h + 1 - 2 * EARLY_GATES))
                    act.wait_ge(weighted, n * 2 + h + 1)
                    act.sem_inc(waited, 1)
                    act.activation(gate[:, h, :], gate_ps[:, h, :], ACT.Sigmoid,
                                   bias=bias[:, bass.ds(n, 1)]).then_inc(gated, 1)

            def split_branch(b, it):
                act.wait_ge(raw_loaded, it * 16 + ((b - 1) * KO * 16 + 16))
                act.sem_inc(waited, 1)
                act.activation(o_hi[:, b % 2, bass.ds(it, 1), :].rearrange("p a s -> p (a s)"), o_raw[:],
                               ACT.Copy).then_inc(o_hi_done, 1)

            def pair(b, it, last):
                step(b, it, 0, True)
                if b < 2:
                    split_branch(b + 1, it)
                step(b, it, 1, not last)

            split_w(0, 0, KD * P)
            for half in range(2):
                at = slice(HALF * half, HALF * (half + 1))
                for c in range(KO):
                    if half == 0:
                        act.wait_ge(first_loaded[c], 16)
                    act.activation(o_hi[:, 0, c, at], T.merged[:, c, at], ACT.Copy).then_inc(first_hi_done, 1)
                if half == 0:
                    split_w(1, 1, KD * P)
            act.wait_ge(bias_loaded, 16)
            act.wait_ge(*T.stores[0])
            early_step(0)
            split_branch(1, 0)
            early_step(1)
            for b in range(3):
                with act.Fori(int(b == 0), NJ // 2 - (b == 2)) as it:
                    pair(b, it, False)
            pair(2, NJ // 2 - 1, True)

        @block.vector
        def _(dve):
            dve.sem_inc(weighted, 2)

            def split_w(s, n, first=0):
                dve.wait_ge(W.hi_ready, n + 1)
                dve.tensor_tensor(W.view(W.lo, s, first), W.view(W.raw, s, first), f32(W.view(W.hi, s, first)),
                                  ALU.subtract).then_inc(W.lo_ready, 1)

            def step(b, it, s, more):
                n = it * 2 + (b * NJ + s)
                if more:
                    split_w(1 - s, n + 1)
                products(b, it, s)

            def products(b, it, s):
                n = it * 2 + (b * NJ + s)
                for h in range(2):
                    dve.wait_ge(gated, n * 2 + h + 1)
                    dve.wait_ge(y_done, n * 2 + h + 1 + 2)
                    at = T.merged[:, bass.ds(it * 2 + s, 1), HALF * h:HALF * (h + 1)].rearrange("p a n -> p (a n)")
                    if b == 0:
                        dve.tensor_tensor(at, y_ps[:, h, :], gate[:, h, :], ALU.mult).then_inc(weighted, 1)
                    else:
                        dve.tensor_tensor(term[:, h, :], y_ps[:, h, :], gate[:, h, :], ALU.mult)\
                            .then_inc(weighted, 1)
                        dve.wait_ge(weighted, n * 2 + h + 1 + 2)
                        dve.tensor_tensor(at, at, term[:, h, :], ALU.add).then_inc(summed, 1)

            def split_branch(b, it):
                dve.wait_ge(o_hi_done, it + ((b - 1) * KO + 1))
                cut = bass.ds(it, 1)
                dve.tensor_tensor(o_lo[:, b % 2, cut, :].rearrange("p a s -> p (a s)"), o_raw[:],
                                  f32(o_hi[:, b % 2, cut, :]).rearrange("p a s -> p (a s)"),
                                  ALU.subtract).then_inc(o_lo_done, 1)

            def pair(b, it, last):
                step(b, it, 0, True)
                if b < 2:
                    split_branch(b + 1, it)
                step(b, it, 1, not last)

            split_w(0, 0, KD * P)
            for half in range(2):
                at = slice(HALF * half, HALF * (half + 1))
                for c in range(KO):
                    dve.wait_ge(first_hi_done, KO * half + c + 1)
                    dve.tensor_tensor(o_lo[:, 0, c, at], T.merged[:, c, at], f32(o_hi[:, 0, c, at]),
                                      ALU.subtract).then_inc(first_lo_done, 1)
                if half == 0:
                    split_w(1, 1, KD * P)
            dve.wait_ge(first_lo_done, 2 * KO)
            products(0, 0, 0)
            split_branch(1, 0)
            split_w(0, 2)
            products(0, 0, 1)
            for b in range(3):
                with dve.Fori(int(b == 0), NJ // 2 - (b == 2)) as it:
                    pair(b, it, False)
            pair(2, NJ // 2 - 1, True)

        @block.tensor
        def _(pe):
            pe.sem_inc(y_done, 2)

            def early_step(s):
                pe.wait_ge(W.lo_ready, s + 1)
                hi, lo = W.view(W.hi, s), W.view(W.lo, s)
                for h in range(2):
                    at = slice(HALF * h, HALF * (h + 1))
                    pe.wait_ge(weighted, s * 2 + h + 1)
                    for k in range(KO):
                        if s == 0:
                            pe.wait_ge(first_lo_done, KO * h + k + 1)
                        cut = slice(P * (KD + k), P * (KD + k + 1))
                        mm = product(pe, y_ps[:, h, :], hi[:, cut], lo[:, cut],
                                     o_hi[:, 0, k, at], o_lo[:, 0, k, at], start=(k == 0), stop=(k == KO - 1))
                    mm.then_inc(y_done, 1)

            def step(b, it, s):
                n = it * 2 + (b * NJ + s)
                pe.wait_ge(W.lo_ready, n + 1)
                hi, lo = W.view(W.hi, s), W.view(W.lo, s)
                for h in range(2):
                    at = slice(HALF * h, HALF * (h + 1))
                    pe.wait_ge(weighted, n * 2 + h + 1)
                    for k in range(KD):
                        cut = slice(P * k, P * (k + 1))
                        mm = product(pe, gate_ps[:, h, :], hi[:, cut], lo[:, cut],
                                     T.h_hi[:, k, at], T.h_lo[:, k, at], start=(k == 0), stop=(k == KD - 1))
                    mm.then_inc(gate_done, 1)
                    for k in range(KO):
                        cut = slice(P * (KD + k), P * (KD + k + 1))
                        mm = product(pe, y_ps[:, h, :], hi[:, cut], lo[:, cut],
                                     o_hi[:, b % 2, k, at], o_lo[:, b % 2, k, at], start=(k == 0), stop=(k == KO - 1))
                    mm.then_inc(y_done, 1)

            early_step(0)
            early_step(1)
            for b in range(3):
                if b >= 1:
                    pe.wait_ge(o_lo_done, KO * b)
                with pe.Fori(int(b == 0), NJ // 2) as it:
                    for s in range(2):
                        step(b, it, s)


def output_stage(nc, T):
    with ExitStack() as stack:
        kit = Kit(nc, stack)
        m_hi, m_lo = T.h_hi, T.h_lo
        x1 = T.merged
        w_hi, w_lo = (kit.sb("w_out_" + n, [P, KD, D], F32R) for n in ("hi", "lo"))
        raw_slot = lambda j: T.w_raw[:, D * (j % 3):D * (j % 3 + 1)]
        acc_ps = kit.ps("acc_ps", [P, 2, 2, HALF])
        acc = [acc_ps[:, 0], acc_ps[:, 1], T.ac_ps]
        turn_ps = kit.ps("out_turn_ps", [P, 2, HALF])
        gains = kit.sb("out_gains", [P, 2, D])
        part = kit.sb("out_part", [P, D])
        normed = kit.sb("out_normed", [P, 2, D])
        junk = kit.sb("out_junk", [P, HALF])
        ssq = kit.sb("out_ssq", [P, NT, 3])
        stat = kit.sb("out_stat", [P, NT, 5])
        w_loaded = T.w_out_loaded
        w_hi_done, w_lo_done = kit.sem("w_out_hi_done"), kit.sem("w_out_lo_done")
        g_loaded = kit.sem("out_gains_loaded")
        x_loaded = [kit.sem(f"x_loaded{t}") for t in range(NT)]
        m_hi_done, m_lo_done = kit.sem("m_hi_done"), kit.sem("m_lo_done")
        rows_done = kit.sem("rows_done")
        squared = kit.sem("out_squared")
        squared_x1 = kit.sem("out_squared_x1")
        meaned = kit.sem("out_meaned")
        rooted, rooted_x1 = kit.sem("out_rooted"), kit.sem("out_rooted_x1")
        parted = kit.sem("out_parted")
        x1_done = kit.sem("x1_done")
        renormed = kit.sem("renormed")
        turned = kit.sem("out_turned")
        h_hi_done, h_lo_done = kit.sem("h2_hi_done"), kit.sem("h2_lo_done")
        ffn = T.ffn_weights = FfnWeights(kit, T)

        def order(first, second, third, between):
            for t in (0, 1):
                first(t)
            for t in (0, 1):
                second(t)
            for t in range(2, NT):
                first(t)
                third(t - 2 if t == 2 else t - 1)
                second(t)
                if t == 2:
                    third(1)
                if 3 <= t < 6:
                    between(t - 3)
            third(NT - 1)

        block = stack.enter_context(nc.Block())

        @block.sync
        def _(sp):
            for j in range(KD):
                if j >= 3:
                    sp.wait_ge(w_lo_done, j - 2)
                    sp.dma_start(raw_slot(j), T.d["w_out"][0, P * j:P * (j + 1), :]).then_inc(w_loaded[j % 3], 16)
                    t = j - 3
                    sp.wait_ge(m_lo_done, t + 1)
                    sp.dma_start(x1[:, t, :], T.d["x"][0, P * t:P * (t + 1), :]).then_inc(x_loaded[t], 16)
                if j == 4:
                    for i, name in enumerate(("g_mix_post", "g_ffn_pre")):
                        sp.dma_start(gains[:, i, :], T.d[name][0:1, :].to_broadcast([P, D])).then_inc(g_loaded, 16)
            for t in range(KD - 3, NT):
                sp.wait_ge(m_lo_done, t + 1)
                sp.dma_start(x1[:, t, :], T.d["x"][0, P * t:P * (t + 1), :]).then_inc(x_loaded[t], 16)
            for i in range(3):
                sp.wait_ge(w_lo_done, KD)
                ffn.load(sp, 0, i, None)

        @block.scalar
        def _(act):
            def rows_squared(t):
                act.wait_ge(rows_done, t + 1)
                for h in range(2):
                    if t + h:
                        act.wait_ge(squared, 2 * t + h)
                    act.activation(junk[:], acc[t % 3][:, h, :], ACT.Square,
                                   accum_out=ssq[:, t, h:h + 1]).then_inc(squared, 1)

            def x1_squared(t):
                act.wait_ge(x1_done, t + 1)
                if t >= 2:
                    act.wait_ge(turned, 2 * (t - 1))
                act.activation(normed[:, t % 2, :], x1[:, t, :], ACT.Square,
                               accum_out=ssq[:, t, 2:3]).then_inc(squared_x1, 1)

            def split_h(t):
                for b in range(2):
                    act.wait_ge(turned, 2 * t + b + 1)
                    act.activation(T.h_hi[:, 4 * b:4 * b + 4, P * t:P * (t + 1)],
                                   turn_ps[:, b, :].rearrange("p (c n) -> p c n", c=4),
                                   ACT.Copy).then_inc(h_hi_done, 1)

            for j in range(KD):
                act.activation(m_hi[:, j, :], T.merged[:, j, :], ACT.Copy).then_inc(m_hi_done, 1)
                act.wait_ge(w_loaded[j % 3], 16 * (j // 3 + 1))
                act.activation(w_hi[:, j, :], raw_slot(j), ACT.Copy).then_inc(w_hi_done, 1)
            order(rows_squared, x1_squared, split_h, lambda i: ffn.split_high(act, 0, i))

        @block.gpsimd
        def _(pool):
            steps = [0]

            def rows_root(t):
                pool.wait_ge(squared, 2 * t + 2)
                pool.tensor_tensor(stat[:, t, 0:1], ssq[:, t, 0:1], ssq[:, t, 1:2], ALU.add).then_inc(meaned, 1)
                pool.wait_ge(meaned, steps[0] + 1)
                pool.tensor_scalar(stat[:, t, 1:2], stat[:, t, 0:1], 1.0 / D, EPS, ALU.mult, ALU.add)\
                    .then_inc(meaned, 1)
                pool.wait_ge(meaned, steps[0] + 2)
                pool.tensor_tensor(stat[:, t, 2:3], stat[:, t, 1:2], T.minus_half[:], ALU.pow).then_inc(rooted, 1)
                steps[0] += 2

            def x1_root(t):
                pool.wait_ge(squared_x1, t + 1)
                pool.tensor_scalar(stat[:, t, 3:4], ssq[:, t, 2:3], 1.0 / D, EPS, ALU.mult, ALU.add)\
                    .then_inc(meaned, 1)
                pool.wait_ge(meaned, steps[0] + 1)
                pool.tensor_tensor(stat[:, t, 4:5], stat[:, t, 3:4], T.minus_half[:], ALU.pow)\
                    .then_inc(rooted_x1, 1)
                steps[0] += 1

            order(rows_root, x1_root, lambda t: None, lambda i: None)

        @block.vector
        def _(dve):
            def residual(t):
                dve.wait_ge(rooted, t + 1)
                if t >= 1:
                    dve.wait_ge(x1_done, t)
                if t == 0:
                    dve.wait_ge(g_loaded, 32)
                for h in range(2):
                    at = slice(HALF * h, HALF * (h + 1))
                    dve.scalar_tensor_tensor(out=part[:, at], in0=acc[t % 3][:, h, :],
                                             scalar=stat[:, t, 2:3], in1=gains[:, 0, at],
                                             op0=ALU.mult, op1=ALU.mult).then_inc(parted, 1)
                dve.wait_ge(parted, 2 * t + 2)
                dve.wait_ge(x_loaded[t], 16)
                dve.tensor_tensor(x1[:, t, :], x1[:, t, :], part[:], ALU.add).then_inc(x1_done, 1)

            def renormalise(t):
                dve.wait_ge(rooted_x1, t + 1)
                dve.scalar_tensor_tensor(out=normed[:, t % 2, :], in0=x1[:, t, :], scalar=stat[:, t, 4:5],
                                         in1=gains[:, 1, :], op0=ALU.mult, op1=ALU.mult).then_inc(renormed, 1)

            def split_h(t):
                for b in range(2):
                    dve.wait_ge(h_hi_done, 2 * t + b + 1)
                    cut = (slice(None), slice(4 * b, 4 * b + 4), slice(P * t, P * (t + 1)))
                    dve.tensor_tensor(T.h_lo[cut], turn_ps[:, b, :].rearrange("p (c n) -> p c n", c=4),
                                      f32(T.h_hi[cut]), ALU.subtract).then_inc(h_lo_done, 1)

            for j in range(KD):
                dve.wait_ge(m_hi_done, j + 1)
                dve.tensor_tensor(m_lo[:, j, :], T.merged[:, j, :], f32(m_hi[:, j, :]),
                                  ALU.subtract).then_inc(m_lo_done, 1)
                dve.wait_ge(w_hi_done, j + 1)
                dve.tensor_tensor(w_lo[:, j, :], raw_slot(j), f32(w_hi[:, j, :]),
                                  ALU.subtract).then_inc(w_lo_done, 1)
            order(residual, renormalise, split_h, lambda i: ffn.split_low(dve, 0, i))

        @block.tensor
        def _(pe):
            def turn(t):
                pe.wait_ge(renormed, t + 1)
                for b in range(2):
                    if t >= 1:
                        pe.wait_ge(h_lo_done, 2 * t + b - 1)
                    for c in range(4):
                        mm = pe.transpose(turn_ps[:, b, P * c:P * (c + 1)],
                                          normed[:, t % 2, P * (4 * b + c):P * (4 * b + c + 1)], T.ident[:])
                    mm.then_inc(turned, 1)

            def add_block(t, j):
                cut = slice(P * t, P * (t + 1))
                for h in range(2):
                    at = slice(HALF * h, HALF * (h + 1))
                    mm = product(pe, acc[t % 3][:, h, :], m_hi[:, j, cut], m_lo[:, j, cut],
                                 w_hi[:, j, at], w_lo[:, j, at], start=(j == 0), stop=(j == KD - 1))
                if j == KD - 1:
                    mm.then_inc(rows_done, 1)

            for j in range(KD):
                pe.wait_ge(m_lo_done, j + 1)
                pe.wait_ge(w_lo_done, j + 1)
                for t in (0, 1):
                    add_block(t, j)
            for t in range(2, NT):
                if t >= 3:
                    pe.wait_ge(parted, 2 * (t - 3) + 2)
                for j in range(KD):
                    add_block(t, j)
                    if t == 3 and j == 3:
                        turn(1)
                turn(t - 2 if t == 2 else t - 1)
            pe.sem_inc(ffn.c_done, 2)
            pe.wait_ge(parted, 2 * 5 + 2)
            pe.wait_ge(h_lo_done, 2 * 3 + 2)
            pe.wait_ge(ffn.lo_ready, 2)
            ffn.hidden_half(pe, T, 0, 0, 0, KD)
            ffn.hidden_half(pe, T, 1, 0, 0, KD // 2)
            turn(NT - 1)
            ffn.hidden_half(pe, T, 1, 0, KD // 2, KD)


KO = 4


class MergeWeights(Weights):

    def __init__(self, kit, T):
        super().__init__(kit, "wmg", 2, (KD + KO) * P, T.w_raw, T.w_hi, T.w_lo)
        self.w_o = [T.d[n][0].rearrange("(k p) n -> p k n", p=P) for n in ("w_o_fox", "w_o_swa", "w_o_mem")]

    def load_first(self, sp, s):
        for k in range(0, KO, 2):
            sp.dma_start(self.view(self.raw, s, (KD + k) * P, (KD + k + 2) * P).rearrange("p (k n) -> p k n", k=2),
                         self.w_o[0][:, k:k + 2, P * s:P * (s + 1)]).then_inc(self.loaded[s], 16)


class FfnWeights(Weights):

    def __init__(self, kit, T):
        super().__init__(kit, "wffn", 3, D, T.w_raw, T.w_hi, T.w_lo)
        self.w_in = T.d["w_ffn_in"][0].rearrange("(k p) n -> p k n", p=P)
        self.w_out = T.d["w_ffn_out"][0]
        self.a_done, self.c_done = kit.sem("a_done"), kit.sem("c_done")
        self.later_ps = None

    def hidden_half(self, pe, T, which, half, first=0, last=KD, slot=None):
        slot = which if slot is None else slot
        out = (self.later_ps if half else T.ac_ps)[:, which, :]
        hi, lo, at = self.view(self.hi, slot % 3), self.view(self.lo, slot % 3), slice(HALF * half, HALF * (half + 1))
        for k in range(first, last):
            cut = slice(P * k, P * (k + 1))
            mm = product(pe, out, hi[:, cut], lo[:, cut], T.h_hi[:, k, at], T.h_lo[:, k, at],
                         start=(k == 0), stop=(k == KD - 1))
        if last == KD:
            mm.then_inc((self.a_done, self.c_done)[which], 1)

    def load(self, sp, g, i, wait):
        if wait is not None:
            sp.wait_ge(self.lo_ready, wait)
        to = self.view(self.raw, i % 3)
        if i < 4:
            src = self.w_in[:, :, bass.ds(g * 2 * P + (P * (i // 2) + D_FF * (i % 2)), P)]
            sp.dma_start(to.rearrange("p (k n) -> p k n", k=KD), src).then_inc(self.loaded[i % 3], 16)
        else:
            src = self.w_out[bass.ds(g * 2 * P + P * (i - 4), P), :]
            sp.dma_start(to, src).then_inc(self.loaded[i % 3], 16)

    def split_high(self, act, g, i, sem=None, value=None):
        act.wait_ge(self.loaded[i % 3], g * 32 + (16 * (i // 3) + 16))
        if sem is not None:
            act.wait_ge(sem, value)
        act.activation(self.view(self.hi, i % 3), self.view(self.raw, i % 3), ACT.Copy).then_inc(self.hi_ready, 1)

    def split_low(self, dve, g, i):
        dve.wait_ge(self.hi_ready, g * 6 + (i + 1))
        dve.tensor_tensor(self.view(self.lo, i % 3), self.view(self.raw, i % 3), f32(self.view(self.hi, i % 3)),
                          ALU.subtract).then_inc(self.lo_ready, 1)


def ffn_stage(nc, T):
    with ExitStack() as stack:
        kit = Kit(nc, stack)
        x1 = T.merged
        NG = NF // 2
        W = T.ffn_weights
        y = kit.sb("ffn_y", [P, NT, D])
        u = kit.sb("ffn_u", [P, 2, HALF])
        silu = kit.sb("ffn_silu", [P, 2, HALF])
        u_hi, u_lo = (kit.sb("ffn_" + n, [P, 2, S], F32R) for n in ("u_hi", "u_lo"))
        gain = kit.sb("ffn_gain", [P, D])
        junk = kit.sb("ffn_junk", [P, D])
        ssq, mean, rstd = (kit.sb("ffn_" + n, [P, NT]) for n in ("ssq", "mean", "rstd"))
        W.later_ps = kit.ps("ac_later_ps", [P, 2, HALF])
        a_ps, c_ps = ([ps[:, i, :] for ps in (T.ac_ps, W.later_ps)] for i in range(2))
        out_ps = kit.ps("ffn_out_ps", [P, 4, HALF])
        g_loaded = kit.sem("ffn_gain_loaded")
        zeroed = kit.sem("ffn_zeroed")
        a_done, c_done = W.a_done, W.c_done
        silued = kit.sem("silued")
        gated = kit.sem("ffn_gated")
        u_hi_done, u_lo_done = kit.sem("u_hi_done"), kit.sem("u_lo_done")
        part_done = kit.sem("part_done")
        added = kit.sem("ffn_added")
        squared, meaned, rooted = kit.sem("ffn_squared"), kit.sem("ffn_meaned"), kit.sem("ffn_rooted")
        scaled, finished = kit.sem("ffn_scaled"), kit.sem("ffn_finished")
        last_finished, stored = kit.sem("ffn_last_finished"), kit.sem("out_stored")
        out = T.d["out"][0].rearrange("(t p) n -> t p n", p=P)
        A0, C0, A1, C1, R0, R1 = range(6)

        block = stack.enter_context(nc.Block())

        @block.sync
        def _(sp):
            for i in range(3, 6):
                W.load(sp, 0, i, i - 2)
            sp.dma_start(gain[:], T.d["g_ffn_post"][0:1, :].to_broadcast([P, D])).then_inc(g_loaded, 16)
            with sp.Fori(1, NG) as g:
                for i in range(6):
                    W.load(sp, g, i, g * 6 + (i - 2))
            for t in range(NT):
                if t < NT - 2:
                    sp.wait_ge(finished, t + 1)
                else:
                    sp.wait_ge(last_finished, t - (NT - 2) + 1)
                sp.dma_start(out[t], y[:, t, :]).then_inc(stored, 16)
            sp.wait_ge(stored, 16 * NT)

        @block.scalar
        def _(act):
            def split_w(*which):
                W.split_high(act, *which)

            def halves(g, i):
                for h in range(2):
                    n = g * 4 + (2 * i + h)
                    act.wait_ge(a_done, n + 1)
                    act.wait_ge(gated, n + 1)
                    act.activation(silu[:, h, :], a_ps[h], ACT.Silu).then_inc(silued, 1)
                    if (i, h) == (1, 1):
                        split_w(g, R1, a_done, g * 4 + 4)
                    act.wait_ge(gated, n + 1 + 2)
                    act.activation(u_hi[:, i, HALF * h:HALF * (h + 1)], u[:, h, :], ACT.Copy)\
                        .then_inc(u_hi_done, 1)

            def body(g, more):
                halves(g, 0)
                split_w(g, C1, a_done, g * 4 + 2)
                split_w(g, R0, c_done, g * 4 + 2 + 2)
                halves(g, 1)
                if more:
                    split_w(g + 1, A0, c_done, g * 4 + 4 + 2)
                    split_w(g + 1, C0, part_done, g * 16 + 16 + 4)
                    split_w(g + 1, A1, part_done, g * 16 + 16 + 4)

            with act.Fori(0, NG - 1) as g:
                body(g, True)
            body(NG - 1, False)
            for t in range(NT):
                act.wait_ge(added, 16 * (NG - 1) + 4 + 2 * (t + 1))
                if t >= 1:
                    act.wait_ge(squared, t)
                act.activation(junk[:], y[:, t, :], ACT.Square, accum_out=ssq[:, t:t + 1]).then_inc(squared, 1)

        @block.vector
        def _(dve):
            dve.sem_inc(gated, 2)
            dve.sem_inc(added, 4)

            def split_w(g, i):
                W.split_low(dve, g, i)

            def halves(g, i):
                for h in range(2):
                    n = g * 4 + (2 * i + h)
                    if (i, h) == (1, 1):
                        split_w(g, R1)
                    dve.wait_ge(silued, n + 1)
                    dve.wait_ge(c_done, n + 1 + 2)
                    dve.tensor_tensor(u[:, h, :], c_ps[h], silu[:, h, :], ALU.mult).then_inc(gated, 1)
                    dve.wait_ge(u_hi_done, n + 1)
                    at = slice(HALF * h, HALF * (h + 1))
                    dve.tensor_tensor(u_lo[:, i, at], u[:, h, :], f32(u_hi[:, i, at]),
                                      ALU.subtract).then_inc(u_lo_done, 1)

            def add_parts(g, first, last):
                for n in range(first, last):
                    dve.wait_ge(part_done, g * 16 + (n + 1 + 4))
                    at = y[:, n // 2, HALF * (n % 2):HALF * (n % 2 + 1)]
                    dve.tensor_tensor(at, out_ps[:, n % 4, :], at, ALU.add).then_inc(added, 1)

            def body(g, more):
                halves(g, 0)
                split_w(g, C1)
                split_w(g, R0)
                halves(g, 1)
                if more:
                    split_w(g + 1, A0)
                dve.wait_ge(added, g * 16 + 4)
                if more:
                    add_parts(g, 0, 16)
                    split_w(g + 1, C0)
                    split_w(g + 1, A1)
                    return
                dve.wait_ge(g_loaded, 16)
                for quarter in range(4):
                    add_parts(g, 4 * quarter, 4 * quarter + 4)
                    if quarter >= 1:
                        scale_rows(2 * quarter - 2)
                        scale_rows(2 * quarter - 1)
                for t in (NT - 2, NT - 1):
                    scale_rows(t)
                    dve.wait_ge(scaled, t + 1)
                    dve.tensor_tensor(y[:, t, :], y[:, t, :], x1[:, t, :], ALU.add).then_inc(last_finished, 1)

            def scale_rows(t):
                dve.wait_ge(rooted, t + 1)
                dve.scalar_tensor_tensor(out=y[:, t, :], in0=y[:, t, :], scalar=rstd[:, t:t + 1],
                                         in1=gain[:], op0=ALU.mult, op1=ALU.mult).then_inc(scaled, 1)

            dve.wait_ge(zeroed, 1)
            with dve.Fori(0, NG - 1) as g:
                body(g, True)
            body(NG - 1, False)

        @block.gpsimd
        def _(pool):
            pool.memset(y[:], 0.0).then_inc(zeroed, 1)
            for quarter in range(4):
                for t in (2 * quarter, 2 * quarter + 1):
                    pool.wait_ge(squared, t + 1)
                    pool.tensor_scalar(mean[:, t:t + 1], ssq[:, t:t + 1], 1.0 / D, EPS, ALU.mult, ALU.add)\
                        .then_inc(meaned, 1)
                    pool.wait_ge(meaned, t + 1)
                    pool.tensor_tensor(rstd[:, t:t + 1], mean[:, t:t + 1], T.minus_half[:], ALU.pow)\
                        .then_inc(rooted, 1)
                for t in (2 * quarter - 2, 2 * quarter - 1) if quarter else ():
                    pool.wait_ge(scaled, t + 1)
                    pool.tensor_tensor(y[:, t, :], y[:, t, :], x1[:, t, :], ALU.add).then_inc(finished, 1)

        @block.tensor
        def _(pe):
            pe.sem_inc(part_done, 4)

            def hidden(g, i, first=0):
                for h in range(first, 2):
                    pe.wait_ge(gated, g * 4 + (2 * i + h + 1))
                    for which, slot in enumerate((A0, C0) if i == 0 else (A1, C1)):
                        if h == 0:
                            pe.wait_ge(W.lo_ready, g * 6 + (slot + 1))
                        W.hidden_half(pe, T, which, h, slot=slot)

            def output(g):
                for quarter in range(4):
                    for i in range(2):
                        slot = R0 + i
                        hi, lo = W.view(W.hi, slot % 3), W.view(W.lo, slot % 3)
                        if quarter == 0:
                            pe.wait_ge(W.lo_ready, g * 6 + (slot + 1))
                            pe.wait_ge(u_lo_done, g * 4 + (2 * i + 2))
                        for n in range(4 * quarter, 4 * quarter + 4):
                            if i == 0:
                                pe.wait_ge(added, g * 16 + (n + 1))
                            cut = slice(P * (n // 2), P * (n // 2 + 1))
                            at = slice(HALF * (n % 2), HALF * (n % 2 + 1))
                            mm = product(pe, out_ps[:, n % 4, :], u_hi[:, i, cut], u_lo[:, i, cut],
                                         hi[:, at], lo[:, at], start=(i == 0), stop=(i == 1))
                            if i == 1:
                                mm.then_inc(part_done, 1)

            hidden(0, 0, first=1)
            hidden(0, 1)
            output(0)
            with pe.Fori(1, NG) as g:
                for i in range(2):
                    hidden(g, i)
                output(g)


class Shared:
    pass


def build_program(nc, drams):
    T = Shared()
    Kit.sems = []
    T.d = drams
    T.scale = {FOX: HD ** -0.5, SWA: HD ** -0.5, MEM: 128 ** -0.5}
    T.cum_dram = nc.dram_tensor("cum_scratch", (8, S), F32, kind="Internal").ap()
    T.out_dram = [nc.dram_tensor(f"branch_scratch{b}", (4 * P, S), F32, kind="Internal").ap() for b in range(3)]
    with ExitStack() as whole:
        kit = Kit(nc, whole)
        T.ident = kit.sb("ident", [P, P])
        T.minus_half = kit.sb("minus_half", [P, 1])
        T.ident_bf = kit.sb("ident_bf", [P, P], BF16)
        T.masks_bf = kit.sb("masks_bf", [P, 3 * P], BF16)
        T.w_raw = kit.sb("w_raw", [P, 3 * D])
        T.w_hi, T.w_lo = kit.sb("w_hi", [P, 3 * D], F32R), kit.sb("w_lo", [P, 3 * D], F32R)
        T.projection, T.stores = {}, []
        with ExitStack() as first:
            kit1 = Kit(nc, first)
            T.h_hi, T.h_lo = (kit1.sb(n, [P, KD, S], F32R) for n in ("h_hi", "h_lo"))
            projected = first.enter_context(ExitStack())
            kit5 = Kit(nc, projected)
            T.raw = kit5.sb("raw", [P, 3, S])
            T.out_sb = kit5.sb("branch_out", [P, 2, S])
            T.proj_ps = kit5.ps("proj_ps", [P, 2, HALF])
            with ExitStack() as early:
                kit2 = Kit(nc, early)
                T.rot = kit2.sb("rot", [P, 2, S])
                T.rope = kit2.sb("rope_sb", [P, 2, S])
                T.sink, T.sink_raw = kit2.sb("sink", [P, 8]), kit2.sb("sink_unscaled", [P, 8])
                T.k1, T.k2 = kit2.sb("swa_k1", [P, 2, S], F32R), kit2.sb("swa_k2", [P, 2, S], F32R)
                T.v = kit2.sb("swa_v", [P, 2, NT, 2, HD], F32R)
                with ExitStack() as memory:
                    kit3 = Kit(nc, memory)
                    T.mk_hi, T.mk_lo = (kit3.sb(n, [P, 4, N_MEM], F32R) for n in ("mk_hi", "mk_lo"))
                    T.mv_hi, T.mv_lo = (kit3.sb(n, [P, 4, 2, P], F32R) for n in ("mv_hi", "mv_lo"))
                    with ExitStack() as raw:
                        kit4 = Kit(nc, raw)
                        T.masks = kit4.sb("masks_sb", [P, 3 * P])
                        T.mem_kv = kit4.sb("mem_kv", [P, 8, N_MEM])
                        normalise_stage(nc, T)
                        shared_stage(nc, T)
                    attention_stage(nc, T, MEM)
                    still = [sem for sem, _ in T.stores]
                    T.spent = [x for x in Kit.sems if x not in still and x not in T.projection[SWA].sems()]
                attention_stage(nc, T, SWA)
            attention_stage(nc, T, FOX)
            T.merged = kit.sb("merged", [P, KD, S], side="right")
            merge_stage(nc, T)
            projected.close()
            T.ac_ps = kit.ps("ac_ps", [P, 2, HALF])
            output_stage(nc, T)
            ffn_stage(nc, T)


_INS = ["x", "mem", "g_mix_pre", "g_mix_post", "w_in", "b_fgate", "b_branch", "sinks", "g_mem", "w_mem_kv",
        "w_o_fox", "w_o_swa", "w_o_mem", "w_out", "g_ffn_pre", "g_ffn_post", "w_ffn_in", "w_ffn_out"]


def _constants():
    query, key = np.arange(P)[:, None], np.arange(P)[None, :]
    causal = np.where(key <= query, 0.0, -BIG)
    band_key = np.arange(2 * P)[None, :] - P
    chunk_q, chunk_k = query // 64, band_key // 64
    band = np.where((chunk_k <= chunk_q) & (chunk_k > chunk_q - 2), 0.0, -BIG)
    half = HD // 2
    inv = (np.float32(10000.0) ** (-np.arange(half, dtype=np.float32) / np.float32(half))).astype(np.float32)
    angle = (np.arange(S, dtype=np.float32)[None, :] * inv[:, None]).astype(np.float32)
    cos, sin = np.cos(angle), np.sin(angle)
    rope = np.stack([np.tile(cos, (4, 1)), np.concatenate([-sin, sin, -sin, sin])], axis=1)
    return {"ident": np.eye(P, dtype=np.float32),
            "masks": np.concatenate([causal, band], axis=1).astype(np.float32),
            "rope": rope.astype(np.float32)}


def kernel(**inputs):
    import concourse.bacc as bacc
    from concourse.bass_utils import run_bass_kernel_spmd

    nc = bacc.Bacc("TRN2", target_bir_lowering=False, num_devices=1, dynamic_dma_scratch_size=1024)
    arrays, drams = {}, {}
    given = {name: np.ascontiguousarray(inputs[name]) for name in _INS}
    for name, a in list(given.items()) + list(_constants().items()):
        arrays[f"in_{name}"] = a
        drams[name] = nc.dram_tensor(f"in_{name}", a.shape, mybir.dt.from_np(a.dtype), kind="ExternalInput").ap()
    drams["out"] = nc.dram_tensor("out", (1, S, D), F32, kind="ExternalOutput").ap()
    build_program(nc, drams)
    result = run_bass_kernel_spmd(nc, [arrays], core_ids=[0])
    return result.results[0]["out"]
```
